# Optimizing a Trainium2 kernel written in Bass

```python
import jax, jax.numpy as jnp
from jax import lax
import numpy as np

D_MODEL = 1024
BATCH = 1
SEQ = 256
DEPTH = 2

GRID_W = 64
CTX_LEN = 256
N_BRANCH = 3
BRANCH_W = 512
ML_HEADS = 8
ML_DH = 64
ML_W = ML_HEADS * ML_DH
ML_QK_W = 2 * ML_W
CONV_K = 5
MLA_HEADS = 8
Q_LORA = 384
KV_LORA = 256
NOPE_D = 64
ROPE_D = 32
QK_D = NOPE_D + ROPE_D
MLA_DV = 64
RET_HEADS = 8
RET_DK = 32
RET_DV = 64
RET_W = RET_HEADS * RET_DV
N_EXPERTS = 16
EXPERT_FF = 1024
CAP_FACTOR = 2
CHUNK = 128
QBLK = 128
ROPE_BASE = 10000.0
EPS = 1e-6
PROJ_WIDTHS = (ML_QK_W, ML_W, ML_W, 4 * ML_HEADS, Q_LORA, KV_LORA, ROPE_D,
               RET_HEADS * RET_DK, RET_HEADS * RET_DK, RET_W, RET_W, N_BRANCH * D_MODEL)
N_IN = sum(PROJ_WIDTHS)

kernel_name = 'hybrid_mlstm_mla_retention_ecmoe_dit'

def _rmsnorm(x, w):
    xf = x.astype(jnp.float32)
    out = xf * lax.rsqrt(jnp.mean(xf * xf, axis=-1, keepdims=True) + EPS)
    return (out * w.astype(jnp.float32)).astype(x.dtype)

def _head_layernorm(y, w):
    yf = y.astype(jnp.float32)
    mu = jnp.mean(yf, axis=-1, keepdims=True)
    var = jnp.mean(jnp.square(yf - mu), axis=-1, keepdims=True)
    out = (yf - mu) * lax.rsqrt(var + EPS)
    b, l = y.shape[:2]
    return (out.reshape(b, l, -1) * w.astype(jnp.float32)).astype(w.dtype)

def _ada(cond, w, b):
    m = jax.nn.silu(cond) @ w + b
    return jnp.split(m[..., None, :], 6, axis=-1)

def _split_proj(p):
    idx = np.cumsum(PROJ_WIDTHS)[:-1].tolist()
    return jnp.split(p, idx, axis=-1)

def _rope_tables(row, col, dim):
    half = dim // 4
    inv = ROPE_BASE ** (-jnp.arange(half, dtype=jnp.float32) / half)
    ar = row[:, None] * inv
    ac = col[:, None] * inv
    return (jnp.cos(ar), jnp.sin(ar), jnp.cos(ac), jnp.sin(ac))

def _rot(x, cos, sin):
    xf = x.astype(jnp.float32)
    x1, x2 = jnp.split(xf, 2, axis=-1)
    c = cos[None, :, None, :]
    s = sin[None, :, None, :]
    return jnp.concatenate([x1 * c - x2 * s, x1 * s + x2 * c], axis=-1).astype(x.dtype)

def _rope2d(x, tabs):
    cr, sr, cc, sc = tabs
    d2 = x.shape[-1] // 2
    return jnp.concatenate([_rot(x[..., :d2], cr, sr), _rot(x[..., d2:], cc, sc)], axis=-1)

def _dwconv(x, w, b):
    k = w.shape[0]
    out = lax.conv_general_dilated(x, w[:, None, :].astype(x.dtype), window_strides=(1,),
                                   padding=[(k // 2, k // 2)],
                                   dimension_numbers=('NWC', 'WIO', 'NWC'),
                                   feature_group_count=x.shape[-1])
    return out + b

def _to_chunks(t):
    b, h, l = t.shape[:3]
    t = t.reshape((b, h, l // CHUNK, CHUNK) + t.shape[3:])
    return jnp.moveaxis(t, 2, 0)

def _from_chunks(t):
    t = jnp.moveaxis(t, 0, 2)
    b, h, nc, ch = t.shape[:4]
    return t.reshape((b, h, nc * ch) + t.shape[4:])

def _mlstm_scan(args, state):
    q, k, v, ig, lf = args
    idx = jnp.arange(CHUNK)
    causal = idx[:, None] >= idx[None, :]

    def step(carry, inp):
        C, n, m = carry
        qc, kc, vc, igc, lfc = inp
        b = jnp.cumsum(lfc, axis=-1)
        a = b + m[..., None]
        dlog = jnp.where(causal, b[..., :, None] - b[..., None, :] + igc[..., None, :], -jnp.inf)
        mt = jnp.maximum(a, jnp.max(dlog, axis=-1))
        w = jnp.exp(dlog - mt[..., None])
        inter = jnp.exp(a - mt)
        s = jnp.einsum('bhtd,bhsd->bhts', qc, kc) * w
        num = jnp.einsum('bhts,bhsv->bhtv', s, vc) + inter[..., None] * jnp.einsum('bhvd,bhtd->bhtv', C, qc)
        den = jnp.sum(s, axis=-1) + inter * jnp.einsum('bhd,bhtd->bht', n, qc)
        h = num / jnp.maximum(jnp.abs(den), jnp.exp(-mt))[..., None]
        bl = b[..., -1]
        g = bl[..., None] - b + igc
        m_new = jnp.maximum(bl + m, jnp.max(g, axis=-1))
        dp = jnp.exp(bl + m - m_new)
        wg = jnp.exp(g - m_new[..., None])
        C = dp[..., None, None] * C + jnp.einsum('bhs,bhsv,bhsd->bhvd', wg, vc, kc)
        n = dp[..., None] * n + jnp.einsum('bhs,bhsd->bhd', wg, kc)
        return (C, n, m_new), h

    state, hs = lax.scan(step, state, tuple(_to_chunks(t) for t in (q, k, v, ig, lf)))
    return _from_chunks(hs), state

def _retention_scan(args, lg, R):
    q, k, v = args
    idx = jnp.arange(CHUNK, dtype=jnp.float32)
    diff = idx[:, None] - idx[None, :]
    dmat = jnp.exp(jnp.where(diff[None] >= 0, diff[None] * lg[:, None, None], -jnp.inf))
    xi = jnp.exp((idx + 1.0)[None] * lg[:, None])
    kd = jnp.exp((CHUNK - 1.0 - idx)[None] * lg[:, None])
    cd = jnp.exp(CHUNK * lg)

    def step(R, inp):
        qc, kc, vc = inp
        s = jnp.einsum('bhtd,bhsd->bhts', qc, kc) * dmat
        o = jnp.einsum('bhts,bhsv->bhtv', s, vc) + xi[..., None] * jnp.einsum('bhtd,bhdv->bhtv', qc, R)
        R = cd[:, None, None] * R + jnp.einsum('bhsd,hs,bhsv->bhdv', kc, kd, vc)
        return R, o

    R, os_ = lax.scan(step, R, tuple(_to_chunks(t) for t in (q, k, v)))
    return _from_chunks(os_), R

def _bidirectional(scan_f, scan_b, ctx_f, lat_f, ctx_b, lat_b, init):
    flip = lambda ts: tuple(jnp.flip(t, axis=2) for t in ts)
    hc_f, st_f = scan_f(ctx_f, init)
    hl_f, _ = scan_f(lat_f, st_f)
    hc_b, st_b = scan_b(flip(ctx_b), init)
    hl_b, _ = scan_b(flip(lat_b), st_b)
    return hl_f + jnp.flip(hl_b, axis=2), hc_f + jnp.flip(hc_b, axis=2)

def _mlstm_inputs(qk_pre, v_pre, gates, conv_w, conv_b):
    b, l, _ = qk_pre.shape
    qk = jax.nn.silu(_dwconv(qk_pre, conv_w, conv_b))
    q, k = jnp.split(qk, 2, axis=-1)
    heads = lambda t: t.reshape(b, l, ML_HEADS, ML_DH).transpose(0, 2, 1, 3).astype(jnp.float32)
    q, k, v = heads(q), heads(k) * (ML_DH ** -0.5), heads(v_pre)
    g = gates.astype(jnp.float32).reshape(b, l, 4, ML_HEADS).transpose(2, 0, 3, 1)
    fwd = (q, k, v, g[0], jax.nn.log_sigmoid(g[1]))
    bwd = (q, k, v, g[2], jax.nn.log_sigmoid(g[3]))
    return fwd, bwd

def _mla_q(q_lat, qa_norm, wq_b, qn_w, tabs):
    b, l, _ = q_lat.shape
    q = (_rmsnorm(q_lat, qa_norm) @ wq_b).reshape(b, l, MLA_HEADS, QK_D)
    q = _rmsnorm(q, qn_w)
    if tabs is not None:
        q = jnp.concatenate([q[..., :NOPE_D], _rope2d(q[..., NOPE_D:], tabs)], axis=-1)
    return q

def _mla_kv(kv_lat, k_rope, kva_norm, wkv_b, kn_w, tabs):
    b, l, _ = kv_lat.shape
    kv = (_rmsnorm(kv_lat, kva_norm) @ wkv_b).reshape(b, l, MLA_HEADS, NOPE_D + MLA_DV)
    k_nope, v = kv[..., :NOPE_D], kv[..., NOPE_D:]
    k_r = jnp.broadcast_to(k_rope[:, :, None, :], (b, l, MLA_HEADS, ROPE_D))
    k = _rmsnorm(jnp.concatenate([k_nope, k_r], axis=-1), kn_w)
    if tabs is not None:
        k = jnp.concatenate([k[..., :NOPE_D], _rope2d(k[..., NOPE_D:], tabs)], axis=-1)
    return k, v

def _attend(q, k, v):
    b, s, h, dq = q.shape
    nb = s // QBLK
    qb = jnp.moveaxis(q.reshape(b, nb, QBLK, h, dq), 1, 0)
    scale = dq ** -0.5

    def one(qi):
        sc = jnp.einsum('bqhd,bkhd->bhqk', qi, k).astype(jnp.float32) * scale
        p = jax.nn.softmax(sc, axis=-1)
        return jnp.einsum('bhqk,bkhd->bqhd', p.astype(v.dtype), v)

    o = lax.map(one, qb)
    return jnp.moveaxis(o, 0, 1).reshape(b, s, h * v.shape[-1])

def _ret_inputs(q, k, v, tabs):
    b, l, _ = q.shape
    q = q.reshape(b, l, RET_HEADS, RET_DK)
    k = k.reshape(b, l, RET_HEADS, RET_DK)
    if tabs is not None:
        q, k = _rope2d(q, tabs), _rope2d(k, tabs)
    t = lambda a: a.transpose(0, 2, 1, 3).astype(jnp.float32)
    return (t(q), t(k) * (RET_DK ** -0.5), t(v.reshape(b, l, RET_HEADS, RET_DV)))

def _ret_log_gammas():
    lg = jnp.log1p(-jnp.exp2(-5.0 - jnp.arange(RET_HEADS, dtype=jnp.float32)))
    return lg, lg[::-1]

def _merge(ys, logits, w_branch, w_out):
    b, l, _ = logits.shape
    y = jnp.stack(ys, axis=2)
    br = jnp.einsum('blnc,ncd->blnd', y, w_branch)
    gate = jax.nn.sigmoid(logits.reshape(b, l, N_BRANCH, D_MODEL))
    return jnp.sum(gate * br, axis=2) @ w_out

def _mixer(hl, hc, tabs_mla, tabs_ret, need_ctx, w_in, b_in, conv_w, conv_b, ml_norm_w,
           qa_norm, wq_b, kva_norm, wkv_b, qn_w, kn_w, ret_norm_w, w_branch, w_out):
    pl = _split_proj(hl @ w_in + b_in)
    pc = _split_proj(hc @ w_in + b_in)
    bsz = hl.shape[0]
    lat_f, lat_b = _mlstm_inputs(pl[0], pl[1], pl[3], conv_w, conv_b)
    ctx_f, ctx_b = _mlstm_inputs(pc[0], pc[1], pc[3], conv_w, conv_b)
    init_m = (jnp.zeros((bsz, ML_HEADS, ML_DH, ML_DH), jnp.float32),
              jnp.zeros((bsz, ML_HEADS, ML_DH), jnp.float32),
              jnp.zeros((bsz, ML_HEADS), jnp.float32))
    al, ac = _bidirectional(_mlstm_scan, _mlstm_scan, ctx_f, lat_f, ctx_b, lat_b, init_m)
    ya_l = jax.nn.sigmoid(pl[2]) * _head_layernorm(al.transpose(0, 2, 1, 3), ml_norm_w)
    kc, vc = _mla_kv(pc[5], pc[6], kva_norm, wkv_b, kn_w, None)
    kl, vl = _mla_kv(pl[5], pl[6], kva_norm, wkv_b, kn_w, tabs_mla)
    ql = _mla_q(pl[4], qa_norm, wq_b, qn_w, tabs_mla)
    yb_l = _attend(ql, jnp.concatenate([kc, kl], axis=1), jnp.concatenate([vc, vl], axis=1))
    lg_f, lg_b = _ret_log_gammas()
    scan_f = lambda args, st: _retention_scan(args, lg_f, st)
    scan_b = lambda args, st: _retention_scan(args, lg_b, st)
    r_lat = _ret_inputs(pl[7], pl[8], pl[9], tabs_ret)
    r_ctx = _ret_inputs(pc[7], pc[8], pc[9], None)
    init_r = jnp.zeros((bsz, RET_HEADS, RET_DK, RET_DV), jnp.float32)
    rl, rc = _bidirectional(scan_f, scan_b, r_ctx, r_lat, r_ctx, r_lat, init_r)
    yc_l = jax.nn.silu(pl[10]) * _head_layernorm(rl.transpose(0, 2, 1, 3), ret_norm_w)
    y_lat = _merge((ya_l, yb_l, yc_l), pl[11], w_branch, w_out)
    if not need_ctx:
        return y_lat, None
    ya_c = jax.nn.sigmoid(pc[2]) * _head_layernorm(ac.transpose(0, 2, 1, 3), ml_norm_w)
    qc = _mla_q(pc[4], qa_norm, wq_b, qn_w, None)
    yb_c = _attend(qc, kc, vc)
    yc_c = jax.nn.silu(pc[10]) * _head_layernorm(rc.transpose(0, 2, 1, 3), ret_norm_w)
    y_ctx = _merge((ya_c, yb_c, yc_c), pc[11], w_branch, w_out)
    return y_lat, y_ctx

def _ec_moe(h, router_w, w1, w3, w2):
    bsz, n, _ = h.shape
    cap = CAP_FACTOR * n // N_EXPERTS
    aff = jax.nn.softmax((h @ router_w).astype(jnp.float32), axis=-1)
    g, idx = lax.top_k(jnp.swapaxes(aff, 1, 2), cap)
    bidx = jnp.arange(bsz)[:, None, None]
    xs = h[bidx, idx]
    hid = jax.nn.silu(jnp.einsum('becd,edf->becf', xs, w1)) * jnp.einsum('becd,edf->becf', xs, w3)
    ys = jnp.einsum('becf,efd->becd', hid, w2) * g[..., None].astype(h.dtype)
    return jnp.zeros_like(h).at[bidx, idx].add(ys.astype(h.dtype))

def setup_inputs(seed: int = 0) -> dict:
    key = jax.random.key(seed)
    ks = jax.random.split(key, 32)
    f32 = jnp.float32
    nrm = lambda k, shape: jax.random.normal(k, shape, f32)
    w = lambda k, shape, fan_in, s=1.0: nrm(k, shape) * (s * fan_in ** -0.5)
    gain = lambda k, shape: 1.0 + 0.02 * nrm(k, shape)
    bias = lambda k, shape: 0.02 * nrm(k, shape)
    D = D_MODEL
    b_in = bias(ks[9], (DEPTH, N_IN))
    goff = ML_QK_W + 2 * ML_W
    fb = jnp.linspace(3.0, 6.0, ML_HEADS, dtype=f32) + bias(ks[10], (DEPTH, 2, ML_HEADS))
    b_in = b_in.at[:, goff + ML_HEADS:goff + 2 * ML_HEADS].set(fb[:, 0])
    b_in = b_in.at[:, goff + 3 * ML_HEADS:goff + 4 * ML_HEADS].set(fb[:, 1])
    return {
        'x': nrm(ks[0], (BATCH, SEQ, D)),
        'c': nrm(ks[1], (BATCH, D)),
        'ctx': nrm(ks[2], (BATCH, CTX_LEN, D)),
        'c_ctx': nrm(ks[3], (D,)),
        'ada_w': w(ks[4], (DEPTH, D, 6 * D), D, 0.5),
        'ada_b': bias(ks[5], (DEPTH, 6 * D)),
        'norm1_w': gain(ks[6], (DEPTH, D)),
        'norm2_w': gain(ks[7], (DEPTH, D)),
        'w_in': w(ks[8], (DEPTH, D, N_IN), D),
        'b_in': b_in,
        'conv_w': w(ks[11], (DEPTH, CONV_K, ML_QK_W), CONV_K),
        'conv_b': bias(ks[12], (DEPTH, ML_QK_W)),
        'ml_norm_w': gain(ks[13], (DEPTH, ML_W)),
        'mla_qa_norm': gain(ks[14], (DEPTH, Q_LORA)),
        'mla_wq_b': w(ks[15], (DEPTH, Q_LORA, MLA_HEADS * QK_D), Q_LORA),
        'mla_kva_norm': gain(ks[16], (DEPTH, KV_LORA)),
        'mla_wkv_b': w(ks[17], (DEPTH, KV_LORA, MLA_HEADS * (NOPE_D + MLA_DV)), KV_LORA),
        'q_norm_w': gain(ks[18], (DEPTH, QK_D)),
        'k_norm_w': gain(ks[19], (DEPTH, QK_D)),
        'ret_norm_w': gain(ks[20], (DEPTH, RET_W)),
        'w_branch': w(ks[21], (DEPTH, N_BRANCH, BRANCH_W, D), BRANCH_W),
        'w_out': w(ks[22], (DEPTH, D, D), D),
        'router_w': w(ks[23], (DEPTH, D, N_EXPERTS), D),
        'exp_w1': w(ks[24], (DEPTH, N_EXPERTS, D, EXPERT_FF), D),
        'exp_w3': w(ks[25], (DEPTH, N_EXPERTS, D, EXPERT_FF), D),
        'exp_w2': w(ks[26], (DEPTH, N_EXPERTS, EXPERT_FF, D), EXPERT_FF),
    }

def reference(x, c, ctx, c_ctx, ada_w, ada_b, norm1_w, norm2_w, w_in, b_in, conv_w, conv_b,
              ml_norm_w, mla_qa_norm, mla_wq_b, mla_kva_norm, mla_wkv_b, q_norm_w, k_norm_w,
              ret_norm_w, w_branch, w_out, router_w, exp_w1, exp_w3, exp_w2):
    n_lat = x.shape[1]
    rows = n_lat // GRID_W
    row = jnp.repeat(jnp.arange(rows), GRID_W).astype(jnp.float32)
    col = jnp.tile(jnp.arange(GRID_W), rows).astype(jnp.float32)
    tabs_mla = _rope_tables(row, col, ROPE_D)
    tabs_ret = _rope_tables(row, col, RET_DK)
    for l in range(DEPTH):
        last = l == DEPTH - 1
        sh1, sc1, g1, sh2, sc2, g2 = _ada(c, ada_w[l], ada_b[l])
        csh1, csc1, cg1, csh2, csc2, cg2 = _ada(c_ctx, ada_w[l], ada_b[l])
        hl = _rmsnorm(x, norm1_w[l]) * (1.0 + sc1) + sh1
        hc = _rmsnorm(ctx, norm1_w[l]) * (1.0 + csc1) + csh1
        y_lat, y_ctx = _mixer(hl, hc, tabs_mla, tabs_ret, not last, w_in[l], b_in[l], conv_w[l], conv_b[l],
                              ml_norm_w[l], mla_qa_norm[l], mla_wq_b[l], mla_kva_norm[l], mla_wkv_b[l],
                              q_norm_w[l], k_norm_w[l], ret_norm_w[l], w_branch[l], w_out[l])
        x = x + g1 * y_lat
        hl = _rmsnorm(x, norm2_w[l]) * (1.0 + sc2) + sh2
        x = x + g2 * _ec_moe(hl, router_w[l], exp_w1[l], exp_w3[l], exp_w2[l])
        if not last:
            ctx = ctx + cg1 * y_ctx
            hc = _rmsnorm(ctx, norm2_w[l]) * (1.0 + csc2) + csh2
            ctx = ctx + cg2 * _ec_moe(hc, router_w[l], exp_w1[l], exp_w3[l], exp_w2[l])
    return x


_drawn_inputs = setup_inputs


def setup_inputs(seed=0):
    import zlib

    import numpy as np

    out = dict(_drawn_inputs(seed))
    spreads = {}
    factors = {'norm1_w': 6.828,
     'norm2_w': 5.903,
     'conv_b': 64.0,
     'ml_norm_w': 33.172,
     'mla_qa_norm': 8.0,
     'mla_kva_norm': 8.0,
     'q_norm_w': 8.0,
     'k_norm_w': 8.0,
     'ret_norm_w': 8.0}
    for name, (base, spread) in spreads.items():
        noise = np.random.default_rng([zlib.crc32(name.encode()), seed]).standard_normal(out[name].shape)
        drawn = base * np.exp(spread * noise) if base else spread * noise
        out[name] = __import__('jax').numpy.asarray(drawn.astype(out[name].dtype))
    for name, factor in factors.items():
        out[name] = (out[name] * factor).astype(out[name].dtype)
    return out
```

```python
import concourse.bass as bass
from concourse import mybir
from contextlib import ExitStack

F32 = mybir.dt.float32
BF16 = mybir.dt.bfloat16
ALU = mybir.AluOpType
ACT = mybir.ActivationFunctionType
AX = mybir.AxisListType

P = 128
D = 1024
KD = D // P
CT, LT = 256, 256
T = CT + LT
NT = T // P
DEPTH = 2
H = 8
W = 512
DH = 64
Q_LORA, KV_LORA, NOPE, ROPE, QK = 384, 256, 64, 32, 96
RK = 32
E, FF, CAP = 16, 1024, 32
EPS = 1e-6
C_QK, C_V, C_O, C_G, C_QL, C_KV = 0, 1024, 1536, 2048, 2080, 2464
C_RQ, C_RV, C_RG, C_LOG = 2752, 3264, 3776, 4288
SLOTS, SLOT = 6, 4096
VA = dict(ada=0, n1=48, n2=56, bqk=64, blog=72, cb=96)
VA_N = 104
VB = dict(cw=0, qa=40, kva=43, mln=45, retn=49)
VB_N = 53


class Signal:

    def __init__(self, sem):
        self.sem, self.base, self.total = sem, 0, 0

    def inc(self, n=1):
        self.total += n
        return self.sem, n

    def reach(self, n):
        return self.sem, self.base + n

    def latest(self):
        return self.sem, self.total


def token_runs(tiles):
    runs = []
    for t in tiles:
        if runs and runs[-1][0] + runs[-1][1] == t:
            runs[-1][1] += 1
        else:
            runs.append([t, 1])
    return runs


def seen_by(direction, s, last):
    if direction == 0:
        tiles = range(s, NT)
    else:
        tiles = {0: (0, 2, 3), 1: (0, 1, 2, 3), 2: (2,), 3: (2, 3)}[s]
    return [t for t in tiles if not last or t >= 2]


def build_program(nc, a, out):
    ctx = ExitStack()
    with ctx:
        def sb(name, shape, dt=F32):
            return ctx.enter_context(nc.sbuf_tensor(name, shape, dt))

        ring = sb("ring", [P, SLOTS, SLOT])
        xT = sb("xT", [P, KD, T])
        hT = sb("hT", [P, KD, T])
        work = sb("work", [P, 12544 + 6144])
        consts = sb("consts", [P, 4 * P])
        cbf = sb("cbf", [P, 3 * P], BF16)
        rope = sb("rope", [P, 2, 2, ROPE])
        slot_no = sb("slot_no", [P, CAP])
        condT = sb("condT", [P, KD, 32])
        vA = sb("vA", [P, VA_N])
        vB = sb("vB", [P, VB_N])
        mod = sb("mod", [P, 48, 2])
        scale12 = sb("scale12", [P, 2, KD, 2])
        eps = sb("eps", [P, 1])
        bank = [ctx.enter_context(nc.psum_tensor(f"bank{i}", [P, 512], F32)) for i in range(8)]

        ident, ones = consts[:, 0:P], consts[:, P:2 * P]
        tri_le, tri_ge = consts[:, 2 * P:3 * P], consts[:, 3 * P:4 * P]
        identb, neg_f, neg_b = cbf[:, 0:P], cbf[:, P:2 * P], cbf[:, 2 * P:3 * P]

        class Signals:
            def __init__(self, names):
                self.all = [Signal(ctx.enter_context(nc.semaphore(name))) for name in names]
                (self.pe, self.act, self.dve, self.pool, self.weights_used, self.small_loaded, self.stored,
                 self.rows_ready, self.w_ready, self.p_ready, self.pv_done, self.scores_ready, self.num_read,
                 self.dve_step, self.act_step, self.even_table, self.odd_table, self.sel_ready, self.gathered,
                 self.selT_done, self.w13_done, self.silu_done, self.hid_ready, self.hidT_done,
                 self.hidT_ready, self.ys_ready, self.scattered, self.x_added, self.xs_ready,
                 self.selT_ready, self.max_ready, self.exp_ready, self.pT_done, self.pT_ready) = self.all

        S = Signals(("pe", "act", "dve", "pool", "weights_used", "small_loaded", "stored", "rows_ready",
            "w_ready", "p_ready", "pv_done", "scores_ready", "num_read", "dve_step", "act_step",
            "even_table", "odd_table", "sel_ready", "gathered", "selT_done", "w13_done", "silu_done",
            "hid_ready", "hidT_done", "hidT_ready", "ys_ready", "scattered", "x_added",
            "xs_ready", "selT_ready", "max_ready", "exp_ready", "pT_done", "pT_ready"))
        slot_loaded = [ctx.enter_context(nc.semaphore(f"slot_loaded{i}")) for i in range(SLOTS)]

        def link(eng, sig, ins):
            ins.then_inc(*sig.inc())
            eng.wait_ge(*sig.latest())

        def stage():
            for s in S.all:
                s.base = s.total
            return nc.Block(no_gpsimd_drain=True)

        def region(at, *shape):
            n = 1
            for x in shape:
                n *= x
            v = work[:, at:at + n]
            if len(shape) == 2:
                return v.rearrange("p (a b) -> p a b", a=shape[0])
            if len(shape) == 3:
                return v.rearrange("p (a b c) -> p a b c", a=shape[0], b=shape[1])
            if len(shape) == 4:
                return v.rearrange("p (a b c d) -> p a b c d", a=shape[0], b=shape[1], c=shape[2])
            return v

        loads = []
        first = {}

        def add(key, srcs):
            first[key] = len(loads)
            loads.extend(srcs)

        def k_major(src):
            return src.rearrange("(k p) n -> p k n", p=P)

        for l in range(DEPTH):
            w_in = k_major(a["w_in"][l])
            ada = k_major(a["ada_w"][l])
            add(("ada", l), [ada[:, :, j * 512:(j + 1) * 512] for j in range(12)])
            add(("a", l), [w_in[:, :, c:c + n] for c, n in
                           ((C_QK, 512), (C_QK + 512, 512), (C_V, 512), (C_O, 512), (C_G, 32))])
            add(("b", l), [w_in[:, :, c:c + n] for c, n in ((C_QL, 384), (C_KV, 288))])
            add(("bh", l), [k_major(a["mla_wq_b"][l]), k_major(a["mla_wkv_b"][l])])
            add(("c", l), [w_in[:, :, c:c + n] for c, n in ((C_RQ, 512), (C_RV, 512), (C_RG, 512))])
            merge = []
            for n in range(3):
                for c in range(2):
                    col = C_LOG + n * D + c * 512
                    merge.append(w_in[:, :, col:col + 512])
                    merge.append(k_major(a["w_branch"][l, n])[:, :, c * 512:(c + 1) * 512])
            add(("merge", l), merge)
            add(("out", l), [k_major(a["w_out"][l])[:, :, c * 512:(c + 1) * 512] for c in range(2)])
            experts = []
            for e in range(E):
                w1, w3, w2 = (k_major(a[x][l, e]) for x in ("exp_w1", "exp_w3", "exp_w2"))
                experts += [w1[:, 0:4], w3[:, 0:4], w1[:, 4:8], w3[:, 4:8], w2[:, 0:4], w2[:, 4:8]]
            add(("moe", l), experts)

        def slot_view(n, k, cols):
            return ring[:, n % SLOTS, 0:k * cols].rearrange("p (k n) -> p k n", k=k)

        def load(sp, n):
            if n >= len(loads):
                return
            if n >= SLOTS:
                sp.wait_ge(S.weights_used.sem, n - SLOTS + 1)
            src = loads[n]
            sp.dma_start(slot_view(n, src.shape[1], src.shape[2]), src).then_inc(slot_loaded[n % SLOTS], 16)

        def run_ahead(sp, key, count):
            for n in range(first[key] + SLOTS, first[key] + SLOTS + count):
                load(sp, n)

        def arrived(pe, n):
            pe.wait_ge(slot_loaded[n % SLOTS], 16 * (n // SLOTS + 1))

        x_rows = region(0, NT, D)
        cond_rows = work[0:2 * KD, 4096:4096 + P]
        mask_in = work[:, 4224:4224 + 3 * P]
        with stage() as block:
            @block.sync
            def _(sp):
                for n in range(SLOTS):
                    load(sp, n)

            @block.gpsimd
            def _(pool):
                for dst, src in (
                        (consts[:, :], a["consts"]), (rope[:, :, :, :], a["rope"]),
                        (slot_no[:, :], a["slot_no"]), (mask_in, a["masks"]),
                        (cond_rows[0:KD, :], a["c_ctx"].rearrange("(k p) -> k p", p=P)),
                        (cond_rows[KD:2 * KD, :], a["c"].rearrange("b (k p) -> (b k) p", p=P)),
                        (x_rows[:, 0:2, :], a["ctx"].rearrange("b (t p) d -> p (b t) d", p=P)),
                        (x_rows[:, 2:4, :], a["x"].rearrange("b (t p) d -> p (b t) d", p=P))):
                    pool.dma_start(dst, src).then_inc(*S.small_loaded.inc(16))
                nc.gpsimd.memset(condT[:, :, :], 0.0).then_inc(*S.pool.inc())
                nc.gpsimd.memset(eps[:, :], EPS).then_inc(*S.pool.inc())

            @block.tensor
            def _(pe):
                pe.wait_ge(*S.small_loaded.reach(16 * 8))
                nc.tensor.transpose(bank[7][:, 0:2 * KD], cond_rows, ident[0:2 * KD, 0:2 * KD]) \
                    .then_inc(*S.pe.inc())
                for k in range(KD):
                    if k >= 4:
                        pe.wait_ge(*S.dve.reach(k - 3))
                    for t in range(NT):
                        ins = nc.tensor.transpose(bank[k % 4][:, t * P:(t + 1) * P],
                                                  x_rows[:, t, k * P:(k + 1) * P], ident)
                    ins.then_inc(*S.pe.inc())

            @block.scalar
            def _(act):
                act.wait_ge(*S.pool.reach(2))
                act.wait_ge(*S.pe.reach(1))
                nc.scalar.activation(condT[:, :, 0:2], bank[7][:, 0:2 * KD].rearrange("p (s k) -> p k s", s=2),
                                     ACT.Silu).then_inc(*S.act.inc())

            @block.vector
            def _(dve):
                dve.wait_ge(*S.small_loaded.reach(16 * 8))
                nc.vector.tensor_copy(cbf[:, :], mask_in)
                for k in range(KD):
                    dve.wait_ge(*S.pe.reach(k + 2))
                    nc.vector.tensor_copy(xT[:, k, :], bank[k % 4][:, :]).then_inc(*S.dve.inc())

        def vectors_and_modulation(l):
            rows_a, rows_b = work[0:VA_N, 0:P], work[0:VB_N, P:2 * P]
            mod_rows = region(512, 3, 512)
            n0 = first["ada", l]
            with stage() as block:
                @block.sync
                def _(sp):
                    run_ahead(sp, ("ada", l), 12)

                @block.gpsimd
                def _(pool):
                    def rows(dst, at, src):
                        n = src.shape[0]
                        pool.dma_start(dst[at:at + n, :], src).then_inc(*S.small_loaded.inc(16))

                    def cut(v):
                        return v.rearrange("(r p) -> r p", p=P)

                    rows(rows_a, VA["ada"], cut(a["ada_b"][l]))
                    rows(rows_a, VA["n1"], cut(a["norm1_w"][l]))
                    rows(rows_a, VA["n2"], cut(a["norm2_w"][l]))
                    rows(rows_a, VA["bqk"], cut(a["b_in"][l, C_QK:C_QK + 1024]))
                    rows(rows_a, VA["blog"], cut(a["b_in"][l, C_LOG:C_LOG + 3 * D]))
                    rows(rows_a, VA["cb"], cut(a["conv_b"][l]))
                    rows(rows_b, VB["cw"], a["conv_w"][l].rearrange("j (r p) -> (j r) p", p=P))
                    rows(rows_b, VB["qa"], cut(a["mla_qa_norm"][l]))
                    rows(rows_b, VB["kva"], cut(a["mla_kva_norm"][l]))
                    rows(rows_b, VB["mln"], cut(a["ml_norm_w"][l]))
                    rows(rows_b, VB["retn"], cut(a["ret_norm_w"][l]))

                @block.tensor
                def _(pe):
                    pe.wait_ge(*S.small_loaded.reach(16 * 11))
                    nc.tensor.transpose(bank[7][:, 0:VA_N], rows_a, ident[0:VA_N, 0:VA_N])
                    nc.tensor.transpose(bank[6][:, 0:VB_N], rows_b, ident[0:VB_N, 0:VB_N]) \
                        .then_inc(*S.pe.inc())
                    for r in range(3):
                        for j in range(4):
                            arrived(pe, n0 + 4 * r + j)
                        for k in range(KD):
                            for j in range(4):
                                ins = nc.tensor.matmul(bank[r][32 * j:32 * j + 32, :], condT[:, k, :],
                                                       slot_view(n0 + 4 * r + j, KD, 512)[:, k, :],
                                                       start=(k == 0), stop=(k == KD - 1))
                        ins.then_inc(*S.weights_used.inc(4))
                    for r in range(3):
                        pe.wait_ge(*S.act.reach(r + 1))
                        for i in range(4):
                            ins = nc.tensor.transpose(bank[3 + r][:, i * P:(i + 1) * P],
                                                      mod_rows[:, r, i * P:(i + 1) * P], ident)
                        ins.then_inc(*S.pe.inc())

                @block.scalar
                def _(act):
                    for r in range(3):
                        act.wait_ge(S.weights_used.sem, n0 + 4 * (r + 1))
                        nc.scalar.copy(mod_rows[:, r, :], bank[r][:, :]).then_inc(*S.act.inc())

                @block.vector
                def _(dve):
                    dve.wait_ge(*S.pe.reach(1))
                    nc.vector.tensor_copy(vA[:, :], bank[7][:, 0:VA_N])
                    link(dve, S.dve_step, nc.vector.tensor_copy(vB[:, :], bank[6][:, 0:VB_N]))
                    for r in range(3):
                        dve.wait_ge(*S.pe.reach(2 + r))
                        for j in range(4):
                            at = 16 * r + 4 * j
                            ins = nc.vector.tensor_tensor(
                                mod[:, at:at + 4, :],
                                bank[3 + r][:, :].rearrange("p (i w) -> p i w", i=4)[:, :, 32 * j:32 * j + 2],
                                vA[:, at:at + 4].unsqueeze(2).broadcast_to([P, 4, 2]), ALU.add)
                    link(dve, S.dve_step, ins)
                    for i, key in enumerate(("n1", "n2")):
                        sc = mod[:, (1 + 3 * i) * KD:(2 + 3 * i) * KD, :]
                        w = vA[:, VA[key]:VA[key] + KD].unsqueeze(2).broadcast_to([P, KD, 2])
                        link(dve, S.dve_step, nc.vector.scalar_tensor_tensor(
                            scale12[:, i, :, :], sc, 1.0, w, ALU.add, ALU.mult))

        def normalise(l, which, q0):
            square = region(0, KD, T)
            root, inv = region(4096, T), region(4096 + T, T)
            with stage() as block:
                @block.scalar
                def _(act):
                    for k in range(KD):
                        nc.scalar.activation(square[:, k, q0:], xT[:, k, q0:], ACT.Square).then_inc(*S.act.inc())
                    act.wait_ge(*S.pe.reach(1))
                    nc.scalar.activation(root[:, q0:], bank[0][:, q0:], ACT.Sqrt, scale=1.0 / D,
                                         bias=eps[:, 0:1]).then_inc(*S.act.inc())
                    for k in range(KD):
                        act.wait_ge(*S.dve.reach(k + 1))
                        for s in range(q0 // CT, 2):
                            ins = nc.scalar.activation(hT[:, k, s * CT:(s + 1) * CT], hT[:, k, s * CT:(s + 1) * CT],
                                                       ACT.Identity, bias=mod[:, 3 * which * KD + k, s:s + 1])
                    ins.then_inc(*S.act.inc())

                @block.tensor
                def _(pe):
                    for k in range(KD):
                        pe.wait_ge(*S.act.reach(k + 1))
                        ins = nc.tensor.matmul(bank[0][:, q0:], ones, square[:, k, q0:], start=(k == 0),
                                               stop=(k == KD - 1))
                    ins.then_inc(*S.pe.inc())

                @block.vector
                def _(dve):
                    dve.wait_ge(*S.act.reach(KD + 1))
                    link(dve, S.dve_step, nc.vector.reciprocal(inv[:, q0:], root[:, q0:]))
                    for k in range(KD):
                        for s in range(q0 // CT, 2):
                            sl = slice(s * CT, (s + 1) * CT)
                            ins = nc.vector.scalar_tensor_tensor(hT[:, k, sl], xT[:, k, sl],
                                                                 scale12[:, which, k, s:s + 1], inv[:, sl],
                                                                 ALU.mult, ALU.mult)
                        ins.then_inc(*S.dve.inc())

        def token_major(pe, jobs, banks):
            g = 0
            for job in jobs:
                n, cols, tiles = job[:3]
                arrived(pe, n)
                for i, t in enumerate(tiles):
                    if g >= banks:
                        pe.wait_ge(*S.dve.reach(g - banks + 1))
                    for k in range(KD):
                        ins = nc.tensor.matmul(bank[g % banks][:, 0:cols], hT[:, k, t * P:(t + 1) * P],
                                               slot_view(n, KD, cols)[:, k, :], start=(k == 0), stop=(k == KD - 1))
                    if i < len(tiles) - 1:
                        ins.then_inc(*S.pe.inc())
                    else:
                        ins.then_inc(*S.weights_used.inc())
                    g += 1

        YA, YB, YC = 12544, 12544 + 2048, 12544 + 4096
        yT = region(YA, 12, T)

        def add_bias(dve, banks, jobs, bias):
            g = 0
            for j, (n, cols, tiles, b0, dst) in enumerate(jobs):
                for i, t in enumerate(tiles):
                    if i < len(tiles) - 1:
                        dve.wait_ge(*S.pe.reach(g - j + 1))
                    else:
                        dve.wait_ge(S.weights_used.sem, n + 1)
                    src, b = bank[g % banks][:, 0:cols], bias[:, b0:b0 + cols]
                    o = dst(t)
                    if o.ndim == 3:
                        src = src.rearrange("p (h d) -> p h d", h=H)
                        b = b.rearrange("p (h d) -> p h d", h=H)
                    nc.vector.tensor_tensor(o, src, b, ALU.add).then_inc(*S.dve.inc())
                    g += 1

        def load_bias(pool, l, dst, col, n):
            pool.dma_start(dst, a["b_in"][l, col:col + n].partition_broadcast(P)) \
                .then_inc(*S.small_loaded.inc(16))

        qkT = region(0, 8, T)
        v_aug = region(4096, NT, H, DH + 1)
        o_gate = region(6176, NT, W)
        bias_a = region(8224, 1056)
        g_pre = region(9280, NT, 32)
        nlf, igate = region(9408, NT, 2, 32), region(9664, NT, 2, 32)
        c_tok, e_tok = region(9920, NT, 64), region(10176, NT, 64)
        c_rows, m_rows, d_rows = (work[0:64, x:x + T] for x in (10432, 10944, 11456))
        h_sum = region(YC, NT, H, DH)
        pad = region(YB, 2, 2, CT + 4)
        conv = region(YA, 2, T)

        def project_a(l, last):
            q_tiles = [2, 3] if last else [0, 1, 2, 3]
            n0 = first["a", l]
            jobs = [(n0 + 2, 512, range(NT), 0, lambda t: v_aug[:, t, :, 0:DH]),
                    (n0 + 3, 512, q_tiles, 512, lambda t: o_gate[:, t, :]),
                    (n0 + 4, 32, range(NT), 1024, lambda t: g_pre[:, t, :])]
            with stage() as block:
                @block.sync
                def _(sp):
                    run_ahead(sp, ("a", l), 5)

                @block.gpsimd
                def _(pool):
                    load_bias(pool, l, bias_a, C_V, 1056)
                    nc.gpsimd.memset(pad[:, :, :, :], 0.0).then_inc(*S.pool.inc())
                    nc.gpsimd.memset(v_aug[:, :, :, DH:DH + 1], 1.0).then_inc(*S.pool.inc())
                    nc.gpsimd.memset(region(9408, 512), 0.0).then_inc(*S.pool.inc())

                @block.tensor
                def _(pe):
                    for f in range(8):
                        if f % 4 == 0:
                            arrived(pe, n0 + f // 4)
                        if f >= 2:
                            pe.wait_ge(*S.act.reach(max(1, 2 * f - 4)))
                        t0 = CT if last and f < 4 else 0
                        for k in range(KD):
                            ins = nc.tensor.matmul(bank[6 + f % 2][:, t0:], slot_view(n0 + f // 4, KD, 512)[:, k, (f % 4) * P:(f % 4 + 1) * P],
                                                   hT[:, k, t0:], start=(k == 0), stop=(k == KD - 1))
                        if f % 4 < 3:
                            ins.then_inc(*S.pv_done.inc())
                        else:
                            ins.then_inc(*S.weights_used.inc())
                    token_major(pe, jobs, 4)

                @block.scalar
                def _(act):
                    act.wait_ge(*S.pool.reach(1))
                    for f in range(9):
                        if f < 8:
                            if f % 4 < 3:
                                act.wait_ge(*S.pv_done.reach(f - f // 4 + 1))
                            else:
                                act.wait_ge(S.weights_used.sem, n0 + f // 4 + 1)
                            if f >= 2:
                                act.wait_ge(*S.p_ready.reach(f - 1))
                            for s in range(1 if last and f < 4 else 0, 2):
                                ins = nc.scalar.activation(pad[:, f % 2, s, 2:2 + CT],
                                                           bank[6 + f % 2][:, s * CT:(s + 1) * CT], ACT.Identity,
                                                           bias=vA[:, VA["bqk"] + f:VA["bqk"] + f + 1])
                            ins.then_inc(*S.act.inc())
                        if f >= 1:
                            g = f - 1
                            t0 = CT if last and g < 4 else 0
                            act.wait_ge(*S.p_ready.reach(g + 1))
                            nc.scalar.activation(qkT[:, g, t0:], conv[:, g % 2, t0:], ACT.Silu,
                                                 bias=vA[:, VA["cb"] + g:VA["cb"] + g + 1]).then_inc(*S.act.inc())
                    act.wait_ge(*S.dve.reach(NT + len(q_tiles)))
                    for t in q_tiles:
                        nc.scalar.activation(o_gate[:, t, :], o_gate[:, t, :], ACT.Sigmoid)

                @block.vector
                def _(dve):
                    for f in range(8):
                        dve.wait_ge(*S.act.reach(1 if f == 0 else 2 * f))
                        if f >= 2:
                            dve.wait_ge(*S.act.reach(2 * f - 1))
                        s0 = 1 if last and f < 4 else 0
                        o = conv[:, f % 2, s0 * CT:].rearrange("p (s t) -> p s t", t=CT)
                        for j in range(5):
                            x = pad[:, f % 2, s0:, j:j + CT]
                            w = vB[:, VB["cw"] + j * 8 + f:VB["cw"] + j * 8 + f + 1]
                            if j == 0:
                                ins = nc.vector.tensor_scalar(o, x, w, None, ALU.mult)
                            else:
                                ins = nc.vector.scalar_tensor_tensor(o, x, w, o, ALU.mult, ALU.add)
                            if j < 4:
                                link(dve, S.dve_step, ins)
                        ins.then_inc(*S.p_ready.inc())
                    dve.wait_ge(*S.small_loaded.reach(16))
                    dve.wait_ge(*S.pool.reach(3))
                    add_bias(dve, 4, jobs, bias_a)

        def gates(l):
            m, mag = region(YB, NT, 2, H), region(YB + 64, NT, 2, H)
            g4 = g_pre.rearrange("p t (g h) -> p t g h", g=4)
            cum = work[0:64, YB + 512:YB + 1024]
            with stage() as block:
                @block.vector
                def _(dve):
                    for d in range(2):
                        f = g4[:, :, 2 * d + 1, :]
                        nc.vector.tensor_copy(igate[:, :, d, 0:H], g4[:, :, 2 * d, :])
                        link(dve, S.dve_step, nc.vector.tensor_scalar(m[:, :, d, :], f, 0.0, None, ALU.min))
                        ins = nc.vector.scalar_tensor_tensor(mag[:, :, d, :], m[:, :, d, :], -2.0, f,
                                                             ALU.mult, ALU.add)
                    ins.then_inc(*S.dve.inc())
                    dve.wait_ge(*S.act.reach(1))
                    for d in range(2):
                        ins = nc.vector.tensor_tensor(nlf[:, :, d, 0:H], mag[:, :, d, :], m[:, :, d, :],
                                                      ALU.subtract)
                    ins.then_inc(*S.dve.inc())
                    dve.wait_ge(*S.act.reach(2))
                    link(dve, S.dve_step, nc.vector.tensor_tensor(c_rows, bank[1][0:64, :], cum, ALU.add))
                    nc.vector.tensor_tensor_scan(m_rows[0:32, :], c_rows[0:32, :], c_rows[0:32, :], 0.0,
                                                 ALU.max, ALU.max)
                    b, mb = c_rows[32:64, :], m_rows[32:64, :]
                    link(dve, S.dve_step, nc.vector.tensor_tensor_scan(
                        mb[:, CT - 1::-1], b[:, CT - 1::-1], b[:, CT - 1::-1], 0.0, ALU.max, ALU.max))
                    link(dve, S.dve_step, nc.vector.tensor_tensor_scan(
                        mb[:, T - 1:CT - 1:-1], b[:, T - 1:CT - 1:-1], b[:, T - 1:CT - 1:-1], mb[:, 0:1],
                        ALU.max, ALU.max))
                    link(dve, S.dve_step, nc.vector.tensor_scalar(m_rows, m_rows, -1.0, None, ALU.mult))
                    nc.vector.tensor_tensor(d_rows, cum, m_rows, ALU.add).then_inc(*S.dve.inc())
                    dve.wait_ge(*S.pe.reach(2))
                    nc.vector.tensor_copy(c_tok, bank[2][:, 0:256].rearrange("p (t r) -> p t r", t=NT))

                @block.scalar
                def _(act):
                    act.wait_ge(*S.dve.reach(1))
                    link(act, S.act_step, nc.scalar.activation(mag, mag, ACT.Exp, scale=-1.0))
                    nc.scalar.activation(mag, mag, ACT.Ln, bias=1.0).then_inc(*S.act.inc())
                    act.wait_ge(*S.pe.reach(1))
                    nc.scalar.copy(cum, bank[0][0:64, :]).then_inc(*S.act.inc())
                    act.wait_ge(*S.pe.reach(2))
                    nc.scalar.activation(e_tok, bank[3][:, 0:256].rearrange("p (t r) -> p t r", t=NT), ACT.Exp)

                @block.tensor
                def _(pe):
                    pe.wait_ge(*S.dve.reach(2))
                    for d in range(2):
                        rows = slice(32 * d, 32 * d + 32)
                        for t in range(NT):
                            cols = slice(t * P, (t + 1) * P)
                            if d == 0:
                                passed = [s for s in range(t)]
                            else:
                                passed = [1] if t == 0 else [] if t == 1 else [0, 1, 3] if t == 2 else [0, 1]
                            for i, s in enumerate(passed):
                                nc.tensor.matmul(bank[0][rows, cols], nlf[:, s, d, :], ones, start=(i == 0),
                                                 stop=False)
                            nc.tensor.matmul(bank[0][rows, cols], nlf[:, t, d, :], tri_ge if d else tri_le,
                                             start=not passed, stop=True)
                            ins = nc.tensor.matmul(bank[1][rows, cols], igate[:, t, d, :], ident, start=True,
                                                   stop=True)
                    ins.then_inc(*S.pe.inc())
                    pe.wait_ge(*S.dve.reach(3))
                    for i, rows in enumerate((c_rows, d_rows)):
                        for t in range(NT):
                            ins = nc.tensor.transpose(bank[2 + i][:, t * 64:(t + 1) * 64],
                                                      rows[:, t * P:(t + 1) * P], ident[0:64, 0:64])
                    ins.then_inc(*S.pe.inc())

        def mlstm(l, last):
            w_ring, p_ring = region(YA, 4, T), region(YB, 4, T)
            small = region(YA - 512, 512)
            t0 = 2 if last else 0
            nq = NT - t0
            items = [[(s, seen_by(d, s, last)) for s in range(NT)] for d in range(2)]
            ends = [0]
            for u in range(2 * H):
                ends.append(ends[-1] + len(items[u % 2]))
            num = bank[7][:, 0:NT * (DH + 1)].rearrange("p (t c) -> p t c", t=NT)

            def score(s):
                return bank[s][:, :] if s < 2 else bank[2][:, (s - 2) * 256:(s - 1) * 256]

            def score_at(s, t, n):
                off = t if s < 2 else t - 2
                return score(s)[:, off * P:(off + n) * P]

            with stage() as block:
                @block.tensor
                def _(pe):
                    def rows(u):
                        h, d = divmod(u, 2)
                        r = 32 * d + h
                        if u >= 2:
                            pe.wait_ge(*S.w_ready.reach(ends[u - 1]))
                        pick = ident[0:64, r:r + 1].broadcast_to([64, P])
                        nc.tensor.matmul(bank[3 + u % 2][:, :], pick, m_rows, start=True, stop=True)
                        nc.tensor.matmul(bank[5 + u % 2][:, :], pick, m_rows, start=True, stop=False)
                        nc.tensor.matmul(bank[5 + u % 2][:, :], identb,
                                         (neg_b if d else neg_f).unsqueeze(1).broadcast_to([P, NT, P]),
                                         start=False, stop=True).then_inc(*S.rows_ready.inc())

                    def scores(h):
                        at = DH * (h % 2)
                        q, k = qkT[at:at + DH, h // 2, :], qkT[at:at + DH, 4 + h // 2, :]
                        for s in range(NT):
                            lo = CT if s >= 2 or last else 0
                            ins = nc.tensor.matmul(score(s)[:, (CT if last and s < 2 else 0):], k[:, s * P:(s + 1) * P], q[:, lo:],
                                                   start=True, stop=True)
                        ins.then_inc(*S.scores_ready.inc())

                    rows(0)
                    scores(0)
                    n = 0
                    for u in range(2 * H):
                        h, d = divmod(u, 2)
                        if u + 1 < 2 * H:
                            rows(u + 1)
                        if u:
                            pe.wait_ge(*S.num_read.reach(u))
                        for i, (s, tiles) in enumerate(items[d]):
                            pe.wait_ge(*S.p_ready.reach(n + 1))
                            for j, t in enumerate(tiles):
                                ins = nc.tensor.matmul(num[:, t, :], p_ring[:, n % 4, t * P:(t + 1) * P],
                                                       v_aug[:, s, h, :], start=(i == 0 and j == 0),
                                                       stop=(i == NT - 1 and j == len(tiles) - 1),
                                                       skip_group_check=True)
                            ins.then_inc(*S.pv_done.inc())
                            n += 1
                        if d == 1 and h + 1 < H:
                            scores(h + 1)

                @block.scalar
                def _(act):
                    n = 0
                    for u in range(2 * H):
                        h, d = divmod(u, 2)
                        act.wait_ge(*S.rows_ready.reach(u + 1))
                        for s, tiles in items[d]:
                            if n >= 4:
                                act.wait_ge(*S.p_ready.reach(n - 3))
                            bias = c_tok[:, s, 32 * d + h:32 * d + h + 1]
                            ins = None
                            for t, k in token_runs([x for x in tiles if x != s]):
                                ins = nc.scalar.activation(w_ring[:, n % 4, t * P:(t + k) * P],
                                                           bank[3 + u % 2][:, t * P:(t + k) * P], ACT.Exp, bias=bias)
                            if s in tiles:
                                ins = nc.scalar.activation(w_ring[:, n % 4, s * P:(s + 1) * P],
                                                           bank[5 + u % 2][:, s * P:(s + 1) * P], ACT.Exp, bias=bias)
                            ins.then_inc(*S.w_ready.inc())
                            n += 1

                @block.vector
                def _(dve):
                    def finish(u):
                        h, d = divmod(u, 2)
                        dve.wait_ge(*S.pv_done.reach(ends[u + 1]))
                        den = num[:, t0:, DH:DH + 1]
                        e = e_tok[:, t0:, 32 * d + h:32 * d + h + 1]
                        big = small[:, 0:nq].unsqueeze(2)
                        link(dve, S.dve_step, nc.vector.scalar_tensor_tensor(big, den, -1.0, e, ALU.mult, ALU.max))
                        link(dve, S.dve_step, nc.vector.tensor_tensor(big, big, den, ALU.max))
                        link(dve, S.dve_step, nc.vector.reciprocal(big, big))
                        o = h_sum[:, t0:, h, :]
                        tmp = small[:, 128:128 + nq * DH].rearrange("p (t c) -> p t c", t=nq)
                        ins = nc.vector.tensor_tensor(tmp if d else o, num[:, t0:, 0:DH],
                                                      big.broadcast_to([P, nq, DH]), ALU.mult)
                        ins.then_inc(*S.num_read.inc())
                        if d:
                            dve.wait_ge(*S.num_read.latest())
                            link(dve, S.dve_step, nc.vector.tensor_tensor(o, o, tmp, ALU.add))

                    n = 0
                    for u in range(2 * H):
                        h, d = divmod(u, 2)
                        if d == 0:
                            dve.wait_ge(*S.scores_ready.reach(h + 1))
                        for i, (s, tiles) in enumerate(items[d]):
                            dve.wait_ge(*S.w_ready.reach(n + 1))
                            if n >= 4:
                                dve.wait_ge(*S.pv_done.reach(n - 3))
                            for t, k in token_runs(tiles):
                                ins = nc.vector.scalar_tensor_tensor(
                                    p_ring[:, n % 4, t * P:(t + k) * P], score_at(s, t, k), DH ** -0.5,
                                    w_ring[:, n % 4, t * P:(t + k) * P], ALU.mult, ALU.mult)
                            ins.then_inc(*S.p_ready.inc())
                            n += 1
                            if i == 1 and u:
                                finish(u - 1)
                    finish(2 * H - 1)

        def head_norm(l, last, h_in, gate, sq, y_out, vec):
            t0 = 2 if last else 0
            nq = NT - t0
            n = nq * H
            stats = region(YA - 512, 4, 32)
            x = h_in[:, t0:].rearrange("p t h d -> p (t h) d")
            s = sq[:, t0:].rearrange("p t (h d) -> p (t h) d", h=H)
            g = gate[:, t0:].rearrange("p t (h d) -> p (t h) d", h=H)
            mean, var = stats[:, 0, 0:n], stats[:, 1, 0:n]

            def wide(v):
                return v.unsqueeze(2).broadcast_to([P, n, DH])

            with stage() as block:
                @block.vector
                def _(dve):
                    link(dve, S.dve_step, nc.vector.reduce_sum(mean, x, axis=AX.X))
                    link(dve, S.dve_step, nc.vector.tensor_scalar(mean, mean, 1.0 / DH, None, ALU.mult))
                    nc.vector.tensor_tensor(x, x, wide(mean), ALU.subtract).then_inc(*S.dve.inc())
                    dve.wait_ge(*S.act.reach(1))
                    nc.vector.reduce_sum(var, s, axis=AX.X).then_inc(*S.dve.inc())
                    dve.wait_ge(*S.act.reach(2))
                    link(dve, S.dve_step, nc.vector.reciprocal(var, stats[:, 2, 0:n]))
                    link(dve, S.dve_step, nc.vector.tensor_tensor(x, x, wide(var), ALU.mult))
                    nc.vector.tensor_tensor(x, x, g, ALU.mult).then_inc(*S.dve.inc())
                    for i in range(nq):
                        dve.wait_ge(*S.pe.reach(i + 1))
                        t = t0 + i
                        nc.vector.tensor_tensor(yT[:, y_out:y_out + 4, t * P:(t + 1) * P],
                                                bank[i][:, :].rearrange("p (f t) -> p f t", f=4),
                                                vB[:, VB[vec]:VB[vec] + 4].unsqueeze(2).broadcast_to([P, 4, P]),
                                                ALU.mult)

                @block.scalar
                def _(act):
                    act.wait_ge(*S.dve.reach(1))
                    nc.scalar.activation(s, x, ACT.Square).then_inc(*S.act.inc())
                    act.wait_ge(*S.dve.reach(2))
                    nc.scalar.activation(stats[:, 2, 0:n], var, ACT.Sqrt, scale=1.0 / DH, bias=eps[:, 0:1]) \
                        .then_inc(*S.act.inc())

                @block.tensor
                def _(pe):
                    pe.wait_ge(*S.dve.reach(3))
                    flat = h_in.rearrange("p t h d -> p t (h d)")
                    for i in range(nq):
                        for f in range(4):
                            ins = nc.tensor.transpose(bank[i][:, f * P:(f + 1) * P],
                                                      flat[:, t0 + i, f * P:(f + 1) * P], ident)
                        ins.then_inc(*S.pe.inc())

        qT, kT = region(0, H, T), region(4096, H, T)
        bias_b = region(0, 672)
        q_lat, kv_lat = region(YB, NT, Q_LORA), region(4096, NT, KV_LORA + ROPE)
        k_rope = region(12288, NT, ROPE)
        qlT, kvT = region(8192, 3, T), region(9728, 2, T)
        v_mla = region(YC, NT, H, DH)

        def project_b(l, last):
            q_tiles = [2, 3] if last else [0, 1, 2, 3]
            n0 = first["b", l]
            jobs = [(n0, Q_LORA, q_tiles, 0, lambda t: q_lat[:, t, :]),
                    (n0 + 1, KV_LORA + ROPE, range(NT), Q_LORA, lambda t: kv_lat[:, t, :])]
            sums, roots = region(12416, 8), region(12424, 8)
            squares = region(10752, 2, 512)
            lows = [(q_lat, Q_LORA, t, i) for i, t in enumerate(q_tiles)] + \
                   [(kv_lat, KV_LORA, t, 4 + t) for t in range(NT)]
            with stage() as block:
                @block.sync
                def _(sp):
                    run_ahead(sp, ("b", l), 2)

                @block.gpsimd
                def _(pool):
                    load_bias(pool, l, bias_b, C_QL, 672)
                    nc.gpsimd.memset(sums, 1.0).then_inc(*S.pool.inc())

                @block.tensor
                def _(pe):
                    token_major(pe, jobs, 4)
                    for i, (src, width, t, _) in enumerate(lows):
                        pe.wait_ge(*S.p_ready.reach(i + 1))
                        if i >= 4:
                            pe.wait_ge(*S.act.reach(i - 3))
                        for f in range(width // P):
                            ins = nc.tensor.transpose(bank[4 + i % 4][:, f * P:(f + 1) * P],
                                                      src[:, t, f * P:(f + 1) * P], ident)
                        ins.then_inc(*S.pv_done.inc())

                @block.vector
                def _(dve):
                    dve.wait_ge(*S.small_loaded.reach(16))
                    add_bias(dve, 4, jobs, bias_b)
                    dve.wait_ge(*S.dve.latest())
                    nc.vector.tensor_copy(k_rope, kv_lat[:, :, KV_LORA:])
                    dve.wait_ge(*S.exp_ready.reach(1))
                    link(dve, S.dve_step, nc.vector.reciprocal(roots, roots))
                    for src, width, t, j in lows:
                        nc.vector.tensor_scalar(src[:, t, 0:width], src[:, t, 0:width], roots[:, j:j + 1], None,
                                                ALU.mult).then_inc(*S.p_ready.inc())

                @block.scalar
                def _(act):
                    act.wait_ge(*S.pool.reach(1))
                    for i, (src, width, t, j) in enumerate(lows):
                        act.wait_ge(*S.dve.reach(i + 1))
                        if i:
                            act.wait_ge(*S.w_ready.reach(i))
                        nc.scalar.activation(squares[:, 0, 0:width], src[:, t, 0:width], ACT.Square,
                                             scale=width ** -0.5, accum_out=sums[:, j:j + 1]) \
                            .then_inc(*S.w_ready.inc())
                    act.wait_ge(*S.w_ready.latest())
                    nc.scalar.activation(roots, sums, ACT.Sqrt, bias=eps[:, 0:1]).then_inc(*S.exp_ready.inc())
                    for i, (src, width, t, j) in enumerate(lows):
                        act.wait_ge(*S.pv_done.reach(i + 1))
                        dst, vec = (qlT, "qa") if width == Q_LORA else (kvT, "kva")
                        for f in range(width // P):
                            ins = nc.scalar.activation(dst[:, f, t * P:(t + 1) * P], bank[4 + i % 4][:, f * P:(f + 1) * P],
                                                       ACT.Copy, scale=vB[:, VB[vec] + f:VB[vec] + f + 1])
                        ins.then_inc(*S.act.inc())

        def rope_halves(src, dst, tmp, tab, heads):
            cos, sin = (tab[:, i, :].unsqueeze(1).broadcast_to([P, heads, ROPE]) for i in range(2))
            s5 = src.rearrange("p h (a b c) -> p h a b c", a=2, b=2)
            t5 = tmp.rearrange("p h (a b c) -> p h a b c", a=2, b=2)
            n5 = tab[:, 1, :].rearrange("p (a b c) -> p a b c", a=2, b=2)
            for part in range(2):
                for half in range(2):
                    nc.vector.tensor_tensor(t5[:, :, part, half, :], s5[:, :, part, 1 - half, :],
                                            n5[:, part, half, :].unsqueeze(1).broadcast_to([P, heads, 8]), ALU.mult)
            return nc.vector.tensor_tensor(dst, src, cos, ALU.mult)

        def mla_heads(l, last):
            q_tiles = [2, 3] if last else [0, 1, 2, 3]
            n0 = first["bh", l]
            wq = slot_view(n0, 3, H * QK)
            wkv = slot_view(n0 + 1, 2, H * (NOPE + DH))
            head = region(10752, 2, H, QK)
            sq, tmp = region(YB, H, QK), region(YB + 768, H, ROPE)
            norm_w = region(YB + 1024, 2, QK)
            st = region(YB + 1216, 4, H)
            jobs = [("q", t) for t in q_tiles] + [("k", t) for t in range(NT)]
            with stage() as block:
                @block.sync
                def _(sp):
                    run_ahead(sp, ("bh", l), 2)

                @block.gpsimd
                def _(pool):
                    for i, x in enumerate(("q_norm_w", "k_norm_w")):
                        pool.dma_start(norm_w[:, i, :], a[x][l].partition_broadcast(P)) \
                            .then_inc(*S.small_loaded.inc(16))

                @block.tensor
                def _(pe):
                    def product(i):
                        kind, t = jobs[i]
                        if i == 0:
                            arrived(pe, n0)
                        if i == len(q_tiles):
                            arrived(pe, n0 + 1)
                        if i >= 2:
                            pe.wait_ge(*S.num_read.reach(i - 1))
                        src, w, ks, cols = (qlT, wq, 3, 384) if kind == "q" else (kvT, wkv, 2, 512)
                        for c in range(2):
                            for k in range(ks):
                                ins = nc.tensor.matmul(bank[2 * (i % 2) + c][:, 0:cols], src[:, k, t * P:(t + 1) * P],
                                                       w[:, k, c * cols:(c + 1) * cols], start=(k == 0),
                                                       stop=(k == ks - 1))
                        if i + 1 in (len(q_tiles), len(jobs)):
                            ins.then_inc(*S.weights_used.inc())
                        else:
                            ins.then_inc(*S.pe.inc())

                    product(0)
                    for i, (kind, t) in enumerate(jobs):
                        if i + 1 < len(jobs):
                            product(i + 1)
                        pe.wait_ge(*S.dve.reach(i + 1))
                        for h in range(H):
                            if h % 4 == 0 and i:
                                pe.wait_ge(*S.act.reach(2 * i - 1 + h // 4))
                            ins = nc.tensor.transpose(bank[4 + h // 4][0:QK, (h % 4) * P:(h % 4 + 1) * P],
                                                      head[:, i % 2, h, :], ident)
                            if h % 4 == 3:
                                ins.then_inc(*S.pv_done.inc())

                @block.scalar
                def _(act):
                    for i, (kind, t) in enumerate(jobs):
                        act.wait_ge(*S.p_ready.reach(i + 1))
                        nc.scalar.activation(st[:, 1, :], st[:, 0, :], ACT.Sqrt, scale=1.0 / QK, bias=eps[:, 0:1]) \
                            .then_inc(*S.exp_ready.inc())
                        dst = qT if kind == "q" else kT
                        for c in range(2):
                            act.wait_ge(*S.pv_done.reach(2 * i + c + 1))
                            nc.scalar.copy(dst[0:QK, 4 * c:4 * c + 4, t * P:(t + 1) * P],
                                           bank[4 + c][0:QK, :].rearrange("p (h t) -> p h t", h=4)) \
                                .then_inc(*S.act.inc())

                @block.vector
                def _(dve):
                    dve.wait_ge(*S.small_loaded.reach(32))
                    for i, (kind, t) in enumerate(jobs):
                        if i + 1 in (len(q_tiles), len(jobs)):
                            dve.wait_ge(S.weights_used.sem, n0 + (1 if i < len(q_tiles) else 2))
                        else:
                            dve.wait_ge(*S.pe.reach(i + 1 - (i >= len(q_tiles))))
                        if i >= 2:
                            dve.wait_ge(*S.pv_done.reach(2 * i - 2))
                        x = head[:, i % 2, :, :]
                        for c in range(2):
                            b = bank[2 * (i % 2) + c]
                            hs = slice(4 * c, 4 * c + 4)
                            if kind == "q":
                                ins = nc.vector.tensor_copy(x[:, hs, :], b[:, 0:384].rearrange("p (h d) -> p h d", h=4))
                            else:
                                b4 = b[:, :].rearrange("p (h d) -> p h d", h=4)
                                nc.vector.tensor_copy(x[:, hs, 0:NOPE], b4[:, :, 0:NOPE])
                                nc.vector.tensor_copy(v_mla[:, t, hs, :], b4[:, :, NOPE:])
                                ins = nc.vector.tensor_copy(x[:, hs, NOPE:],
                                                            k_rope[:, t, :].unsqueeze(1).broadcast_to([P, 4, ROPE]))
                        ins.then_inc(*S.num_read.inc())
                        dve.wait_ge(*S.num_read.latest())
                        link(dve, S.dve_step, nc.vector.tensor_tensor(sq, x, x, ALU.mult))
                        nc.vector.reduce_sum(st[:, 0, :], sq, axis=AX.X).then_inc(*S.p_ready.inc())
                        dve.wait_ge(*S.exp_ready.reach(i + 1))
                        link(dve, S.dve_step, nc.vector.reciprocal(st[:, 2, :], st[:, 1, :]))
                        link(dve, S.dve_step, nc.vector.tensor_tensor(
                            sq, x, st[:, 2, :].unsqueeze(2).broadcast_to([P, H, QK]), ALU.mult))
                        w = norm_w[:, 0 if kind == "q" else 1, :].unsqueeze(1).broadcast_to([P, H, QK])
                        if t < 2:
                            nc.vector.tensor_tensor(x, sq, w, ALU.mult).then_inc(*S.dve.inc())
                        else:
                            link(dve, S.dve_step, nc.vector.tensor_tensor(sq, sq, w, ALU.mult))
                            nc.vector.tensor_copy(x[:, :, 0:NOPE], sq[:, :, 0:NOPE])
                            link(dve, S.dve_step, rope_halves(sq[:, :, NOPE:], x[:, :, NOPE:], tmp, rope[:, t - 2], H))
                            nc.vector.tensor_tensor(x[:, :, NOPE:], x[:, :, NOPE:], tmp, ALU.add) \
                                .then_inc(*S.dve.inc())

        def mla_attention(l, last):
            q_tiles = [2, 3] if last else [0, 1, 2, 3]
            probs, pT = region(8192, 2, T), region(9216, 2, T)
            y = region(10240, NT, W)
            st = region(12416, 2, 4)
            jobs = [(t, h) for t in q_tiles for h in range(H)]
            scale = QK ** -0.5

            def keys(t):
                return CT if t < 2 else T

            with stage() as block:
                @block.tensor
                def _(pe):
                    def score(i):
                        t, h = jobs[i]
                        if i >= 2:
                            pe.wait_ge(*S.exp_ready.reach(i - 1))
                        nc.tensor.matmul(bank[i % 2][:, 0:keys(t)], qT[0:QK, h, t * P:(t + 1) * P],
                                         kT[0:QK, h, 0:keys(t)], start=True, stop=True).then_inc(*S.scores_ready.inc())

                    def values(i):
                        t, h = jobs[i]
                        pe.wait_ge(*S.pT_ready.reach(i + 1))
                        if i >= 2:
                            pe.wait_ge(*S.num_read.reach(i - 1))
                        nk = keys(t) // P
                        for s in range(nk):
                            ins = nc.tensor.matmul(bank[4 + i % 2][:, 0:DH], pT[:, i % 2, s * P:(s + 1) * P],
                                                   v_mla[:, s, h, :], start=(s == 0), stop=(s == nk - 1))
                        ins.then_inc(*S.pv_done.inc())

                    score(0)
                    for i, (t, h) in enumerate(jobs):
                        if i + 1 < len(jobs):
                            score(i + 1)
                        pe.wait_ge(*S.exp_ready.reach(i + 1))
                        if i >= 2:
                            pe.wait_ge(*S.pT_ready.reach(i - 1))
                        for s in range(keys(t) // P):
                            ins = nc.tensor.transpose(bank[2 + i % 2][:, s * P:(s + 1) * P],
                                                      probs[:, i % 2, s * P:(s + 1) * P], ident)
                        ins.then_inc(*S.pT_done.inc())
                        if i:
                            values(i - 1)
                    values(len(jobs) - 1)
                    pe.wait_ge(*S.num_read.reach(len(jobs)))
                    for j, t in enumerate(q_tiles):
                        for f in range(4):
                            ins = nc.tensor.transpose(bank[j][:, f * P:(f + 1) * P], y[:, t, f * P:(f + 1) * P], ident)
                        ins.then_inc(*S.pe.inc())

                @block.vector
                def _(dve):
                    def sums_out(i):
                        t, h = jobs[i]
                        dve.wait_ge(*S.pv_done.reach(i + 1))
                        link(dve, S.dve_step, nc.vector.reciprocal(st[:, i % 2, 3:4], st[:, i % 2, 2:3]))
                        nc.vector.tensor_scalar(y[:, t, h * DH:(h + 1) * DH], bank[4 + i % 2][:, 0:DH],
                                                st[:, i % 2, 3:4], None, ALU.mult).then_inc(*S.num_read.inc())

                    for i, (t, h) in enumerate(jobs):
                        dve.wait_ge(*S.scores_ready.reach(i + 1))
                        if i >= 2:
                            sums_out(i - 2)
                        link(dve, S.dve_step, nc.vector.reduce_max(st[:, i % 2, 0:1], bank[i % 2][:, 0:keys(t)],
                                                                   axis=AX.X))
                        nc.vector.tensor_scalar(st[:, i % 2, 1:2], st[:, i % 2, 0:1], -scale, None, ALU.mult) \
                            .then_inc(*S.max_ready.inc())
                        if i:
                            dve.wait_ge(*S.pT_done.reach(i))
                            tp = keys(jobs[i - 1][0])
                            nc.vector.tensor_copy(pT[:, (i - 1) % 2, 0:tp], bank[2 + (i - 1) % 2][:, 0:tp]) \
                                .then_inc(*S.pT_ready.inc())
                    i = len(jobs)
                    sums_out(i - 2)
                    dve.wait_ge(*S.pT_done.reach(i))
                    nc.vector.tensor_copy(pT[:, (i - 1) % 2, :], bank[2 + (i - 1) % 2][:, :]).then_inc(*S.pT_ready.inc())
                    sums_out(i - 1)
                    for j, t in enumerate(q_tiles):
                        dve.wait_ge(*S.pe.reach(j + 1))
                        nc.vector.tensor_copy(yT[:, 4:8, t * P:(t + 1) * P],
                                              bank[j][:, :].rearrange("p (f t) -> p f t", f=4))

                @block.scalar
                def _(act):
                    for i, (t, h) in enumerate(jobs):
                        act.wait_ge(*S.max_ready.reach(i + 1))
                        if i >= 2:
                            act.wait_ge(*S.pT_done.reach(i - 1))
                        nc.scalar.activation(probs[:, i % 2, 0:keys(t)], bank[i % 2][:, 0:keys(t)], ACT.Exp,
                                             bias=st[:, i % 2, 1:2], scale=scale, accum_out=st[:, i % 2, 2:3]) \
                            .then_inc(*S.exp_ready.inc())

        rqk, rT = region(0, NT, W), region(2048, 4, T)
        h_ret = region(0, NT, H, DH)
        v_ret, s_gate = region(4096, NT, H, DH), region(6144, NT, W)
        bias_c, decay = region(8192, 1536), region(8192, 2, 2, 3 * P)
        ret_ring = region(9728, 4, T)

        def project_c(l, last):
            q_tiles = [2, 3] if last else [0, 1, 2, 3]
            n0 = first["c", l]
            jobs = [(n0, 512, range(NT), 0, lambda t: rqk[:, t, :]),
                    (n0 + 1, 512, range(NT), 512, lambda t: v_ret[:, t]),
                    (n0 + 2, 512, q_tiles, 1024, lambda t: s_gate[:, t, :])]
            with stage() as block:
                @block.sync
                def _(sp):
                    run_ahead(sp, ("c", l), 3)

                @block.gpsimd
                def _(pool):
                    load_bias(pool, l, bias_c, C_RQ, 1536)

                @block.tensor
                def _(pe):
                    token_major(pe, jobs, 4)
                    for t in range(NT):
                        if t < 2:
                            pe.wait_ge(*S.dve.reach(t + 1))
                        else:
                            pe.wait_ge(*S.p_ready.reach(t - 1))
                        for f in range(4):
                            ins = nc.tensor.transpose(bank[4 + t][:, f * P:(f + 1) * P],
                                                      rqk[:, t, f * P:(f + 1) * P], ident)
                        ins.then_inc(*S.pv_done.inc())

                @block.vector
                def _(dve):
                    dve.wait_ge(*S.small_loaded.reach(16))
                    add_bias(dve, 4, jobs, bias_c)
                    for t in (2, 3):
                        x = rqk[:, t, :].rearrange("p (h d) -> p h d", d=RK)
                        swapped, turned = (ret_ring[:, r, :].rearrange("p (h d) -> p h d", d=RK) for r in (t, t - 2))
                        link(dve, S.dve_step, rope_halves(x, turned, swapped, rope[:, t - 2], 2 * H))
                        nc.vector.tensor_tensor(x, turned, swapped, ALU.add).then_inc(*S.p_ready.inc())

                @block.scalar
                def _(act):
                    for i, t in enumerate(q_tiles):
                        act.wait_ge(*S.dve.reach(2 * NT + i + 1))
                        nc.scalar.activation(s_gate[:, t, :], s_gate[:, t, :], ACT.Silu)
                    for t in range(NT):
                        act.wait_ge(*S.pv_done.reach(t + 1))
                        nc.scalar.copy(rT[:, :, t * P:(t + 1) * P],
                                       bank[4 + t][:, :].rearrange("p (f t) -> p f t", f=4))

        def retention(l, last):
            t0 = 2 if last else 0
            lo = t0 * P
            table_loaded = (S.even_table, S.odd_table)
            with stage() as block:
                @block.gpsimd
                def _(pool):
                    for h in range(H):
                        if h >= 2:
                            pool.wait_ge(*S.p_ready.reach(NT * (h - 1)))
                        pool.dma_start(decay[:, h % 2], a["decay"][h]).then_inc(*table_loaded[h % 2].inc(16))

                @block.tensor
                def _(pe):
                    def scores(h):
                        at = RK * (h % 4)
                        if h >= 2:
                            pe.wait_ge(*S.p_ready.reach(NT * (h - 1)))
                        b = 3 * (h % 2)
                        q, k = rT[at:at + RK, h // 4, :], rT[at:at + RK, 2 + h // 4, :]
                        for s in range(NT):
                            o = bank[b + s][:, lo:] if s < 2 else bank[b + 2][:, (s - 2) * CT:(s - 1) * CT]
                            ins = nc.tensor.matmul(o, k[:, s * P:(s + 1) * P], q[:, (lo if s < 2 else CT):],
                                                   start=True, stop=True)
                        ins.then_inc(*S.scores_ready.inc())

                    scores(0)
                    for h in range(H):
                        if h + 1 < H:
                            scores(h + 1)
                        if h >= 2:
                            pe.wait_ge(*S.num_read.reach(h - 1))
                        for s in range(NT):
                            pe.wait_ge(*S.p_ready.reach(NT * h + s + 1))
                            tiles = range(t0 if s < 2 else 2, NT)
                            for t in tiles:
                                ins = nc.tensor.matmul(bank[6 + h % 2][:, t * DH:(t + 1) * DH],
                                                       ret_ring[:, s, t * P:(t + 1) * P], v_ret[:, s, h, :],
                                                       start=(s == 0 and t == t0), stop=(s == NT - 1 and t == NT - 1),
                                                       skip_group_check=True)
                            ins.then_inc(*S.pv_done.inc())

                @block.vector
                def _(dve):
                    for h in range(H):
                        dve.wait_ge(*S.scores_ready.reach(h + 1))
                        dve.wait_ge(*table_loaded[h % 2].reach(16 * (h // 2 + 1)))
                        b = 3 * (h % 2)
                        for s in range(NT):
                            if h:
                                dve.wait_ge(*S.pv_done.reach(NT * (h - 1) + s + 1))
                            off = P if s % 2 == 0 else 0
                            if s < 2:
                                part = slice(1 if last else 0, 2)
                                o = ret_ring[:, s, lo:].rearrange("p (a t) -> p a t", t=CT)
                                x = bank[b + s][:, lo:].rearrange("p (a t) -> p a t", t=CT)
                                tab = decay[:, h % 2, part, off:off + CT]
                            else:
                                o, x = ret_ring[:, s, CT:], bank[b + 2][:, (s - 2) * CT:(s - 1) * CT]
                                tab = decay[:, h % 2, 0, off:off + CT]
                            nc.vector.tensor_tensor(o, x, tab, ALU.mult).then_inc(*S.p_ready.inc())

                @block.scalar
                def _(act):
                    for h in range(H):
                        act.wait_ge(*S.pv_done.reach(NT * (h + 1)))
                        nc.scalar.copy(h_ret[:, t0:, h, :],
                                       bank[6 + h % 2][:, t0 * DH:NT * DH].rearrange("p (t d) -> p t d", d=DH)) \
                            .then_inc(*S.num_read.inc())

        def merge_branches(l, last):
            lo = CT if last else 0
            merged, sig, tmp = region(0, KD, T), region(4096, 2, T), region(5120, 2, T)
            n0 = first["merge", l]
            jobs = [(n, c, d) for n in range(3) for c in range(2) for d in range(4)]
            m0 = first["out", l]
            with stage() as block:
                @block.sync
                def _(sp):
                    run_ahead(sp, ("merge", l), 14)

                @block.tensor
                def _(pe):
                    for i, (n, c, d) in enumerate(jobs):
                        at = n0 + 2 * (2 * n + c)
                        cols = slice(d * P, (d + 1) * P)
                        if d == 0:
                            arrived(pe, at)
                            arrived(pe, at + 1)
                        if i >= 2:
                            pe.wait_ge(*S.act.reach(i - 1))
                        for k in range(KD):
                            ins = nc.tensor.matmul(bank[i % 2][:, lo:], slot_view(at, KD, 512)[:, k, cols], hT[:, k, lo:],
                                                   start=(k == 0), stop=(k == KD - 1))
                        ins.then_inc(*S.pe.inc())
                        if i >= 2:
                            pe.wait_ge(*S.dve.reach(i - 1))
                        for k in range(4):
                            ins = nc.tensor.matmul(bank[2 + i % 2][:, lo:], slot_view(at + 1, 4, 512)[:, k, cols],
                                                   yT[:, 4 * n + k, lo:], start=(k == 0), stop=(k == 3))
                        if d < 3:
                            ins.then_inc(*S.pv_done.inc())
                        else:
                            ins.then_inc(*S.weights_used.inc(2))
                    pe.wait_ge(*S.dve.reach(len(jobs)))
                    for d in range(KD):
                        if d % 4 == 0:
                            arrived(pe, m0 + d // 4)
                        if d >= 4:
                            pe.wait_ge(*S.x_added.reach(d - 3))
                        for k in range(KD):
                            ins = nc.tensor.matmul(bank[4 + d % 4][:, lo:],
                                                   slot_view(m0 + d // 4, KD, 512)[:, k, (d % 4) * P:(d % 4 + 1) * P],
                                                   merged[:, k, lo:], start=(k == 0), stop=(k == KD - 1))
                        if d % 4 < 3:
                            ins.then_inc(*S.pT_done.inc())
                        else:
                            ins.then_inc(*S.weights_used.inc())

                @block.scalar
                def _(act):
                    for i, (n, c, d) in enumerate(jobs):
                        f = VA["blog"] + n * KD + c * 4 + d
                        act.wait_ge(*S.pe.reach(i + 1))
                        if i >= 2:
                            act.wait_ge(*S.dve.reach(i - 1))
                        nc.scalar.activation(sig[:, i % 2, lo:], bank[i % 2][:, lo:], ACT.Sigmoid,
                                             bias=vA[:, f:f + 1]).then_inc(*S.act.inc())

                @block.vector
                def _(dve):
                    for i, (n, c, d) in enumerate(jobs):
                        m = merged[:, 4 * c + d, lo:]
                        dve.wait_ge(*S.act.reach(i + 1))
                        if d < 3:
                            dve.wait_ge(*S.pv_done.reach(i - i // 4 + 1))
                        else:
                            dve.wait_ge(S.weights_used.sem, n0 + 2 * (i // 4 + 1))
                        if n == 0:
                            nc.vector.tensor_tensor(m, sig[:, i % 2, lo:], bank[2 + i % 2][:, lo:], ALU.mult) \
                                .then_inc(*S.dve.inc())
                        else:
                            link(dve, S.dve_step, nc.vector.tensor_tensor(tmp[:, i % 2, lo:], sig[:, i % 2, lo:],
                                                                          bank[2 + i % 2][:, lo:], ALU.mult))
                            nc.vector.tensor_tensor(m, m, tmp[:, i % 2, lo:], ALU.add).then_inc(*S.dve.inc())
                    for d in range(KD):
                        if d % 4 < 3:
                            dve.wait_ge(*S.pT_done.reach(d - d // 4 + 1))
                        else:
                            dve.wait_ge(S.weights_used.sem, m0 + d // 4 + 1)
                        for s in range(lo // CT, 2):
                            sl = slice(s * CT, (s + 1) * CT)
                            ins = nc.vector.scalar_tensor_tensor(xT[:, d, sl], bank[4 + d % 4][:, sl],
                                                                 mod[:, 2 * KD + d, s:s + 1], xT[:, d, sl],
                                                                 ALU.mult, ALU.add)
                        ins.then_inc(*S.x_added.inc())

        SCATTER = (0, 4, 1, 5, 2, 6, 3, 7)
        OUT_BANKS = (0, 6, 7)
        h_tok = region(0, NT, D)
        select = region(4096, NT, E + 1, CAP)
        weight = region(6272, NT, E + 1)
        xs_all = region(10240, KD, E, 64)
        placed = region(0, 2, NT, P)
        selT = region(1024, 2, T)
        gate_s, hid = work[0:64, 2048:3072], work[0:64, 3072:4096]
        hidT = region(6400, 2, KD, 64)
        ys = region(7424, 2, 512)
        xs = region(8448, 2, KD, 64)

        def route(l, last):
            tiles = [2, 3] if last else [0, 1, 2, 3]
            t0, s0 = tiles[0], tiles[0] // 2
            nt = len(tiles)
            rows = [work[0:E, x:x + T] for x in (6400, 6912, 7424, 7936)]
            aff, rest, mask, pos = rows
            one_row = work[0:E, 8448:8448 + CT]
            posT = region(8960, NT, E)
            best = work[0:E, 9024:9032]
            router = region(9104, KD, E)
            top, tot, ex = region(9300, NT), region(9304, NT), region(9308, NT, E)
            gathers = [(d, s) for d in range(KD) for s in range(s0, 2)]

            def gathered_out(i):
                d, s = gathers[i]
                return (bank[2 + i % 4][:, :].rearrange("p (e c) -> p e c", c=CAP),
                        xs_all[:, d, :, CAP * (s - s0):CAP * (s - s0) + CAP])
            with stage() as block:
                @block.gpsimd
                def _(pool):
                    pool.dma_start(router, a["router_w"][l].rearrange("(k p) e -> p k e", p=P)) \
                        .then_inc(*S.small_loaded.inc(16))
                    nc.gpsimd.memset(one_row, 1.0).then_inc(*S.pool.inc())
                    nc.gpsimd.memset(select[:, :, :, :], 0.0).then_inc(*S.pool.inc())
                    nc.gpsimd.memset(weight[:, :, :], 0.0).then_inc(*S.pool.inc())

                @block.tensor
                def _(pe):
                    pe.wait_ge(*S.small_loaded.reach(16))
                    for i, t in enumerate(tiles):
                        for k in range(KD):
                            ins = nc.tensor.matmul(bank[0][:, t * E:(t + 1) * E], hT[:, k, t * P:(t + 1) * P],
                                                   router[:, k, :], start=(k == 0), stop=(k == KD - 1))
                    ins.then_inc(*S.pe.inc())
                    for i, t in enumerate(tiles):
                        for c in range(2):
                            b = 2 + (2 * i + c) % 4
                            if 2 * i + c >= 4:
                                pe.wait_ge(*S.act.reach(2 * i + c - 3))
                            for j in range(4):
                                ins = nc.tensor.transpose(bank[b][:, j * P:(j + 1) * P],
                                                          hT[:, 4 * c + j, t * P:(t + 1) * P], ident)
                            ins.then_inc(*S.pv_done.inc())
                    pe.wait_ge(*S.dve.reach(2))
                    for t in tiles:
                        ins = nc.tensor.transpose(bank[6][0:E, t * P:(t + 1) * P], weight[:, t, 0:E], ident)
                    ins.then_inc(*S.pe.inc())
                    pe.wait_ge(*S.dve.reach(3))
                    for t in tiles:
                        ins = nc.tensor.transpose(bank[7][:, t * E:(t + 1) * E], pos[:, t * P:(t + 1) * P],
                                                  ident[0:E, 0:E])
                    ins.then_inc(*S.pe.inc())
                    for i, (d, s) in enumerate(gathers):
                        if i < 2:
                            pe.wait_ge(*S.dve.reach(4))
                            pe.wait_ge(*S.act.reach(2 * nt))
                        if i >= 4:
                            pe.wait_ge(*(S.xs_ready if i % 2 else S.x_added).reach(i // 2 - 1))
                        for t in (0, 1):
                            ins = nc.tensor.matmul(bank[2 + i % 4][:, :], h_tok[:, 2 * s + t, d * P:(d + 1) * P],
                                                   select[:, 2 * s + t, 0:E, :].rearrange("p e c -> p (e c)"),
                                                   start=(t == 0), stop=(t == 1))
                        ins.then_inc(*S.gathered.inc())

                @block.scalar
                def _(act):
                    for i in range(2 * nt):
                        if i == 2 * nt - 1:
                            act.wait_ge(*S.dve.reach(1))
                            nc.scalar.activation(ex[:, t0:, :], ex[:, t0:, :], ACT.Exp).then_inc(*S.exp_ready.inc())
                        t, c = tiles[i // 2], i % 2
                        act.wait_ge(*S.pv_done.reach(i + 1))
                        nc.scalar.copy(h_tok[:, t, c * 512:(c + 1) * 512], bank[2 + i % 4][:, :]).then_inc(*S.act.inc())
                    for i in range(1, len(gathers), 2):
                        src, dst = gathered_out(i)
                        act.wait_ge(*S.gathered.reach(i + 1))
                        nc.scalar.copy(dst, src).then_inc(*S.xs_ready.inc())

                @block.vector
                def _(dve):
                    dve.wait_ge(*S.pe.reach(1))
                    lg = bank[0][:, t0 * E:NT * E].rearrange("p (t e) -> p t e", e=E)
                    link(dve, S.dve_step, nc.vector.reduce_max(top[:, t0:], lg, axis=AX.X))
                    nc.vector.tensor_tensor(ex[:, t0:, :], lg, top[:, t0:].unsqueeze(2).broadcast_to([P, nt, E]),
                                            ALU.subtract).then_inc(*S.dve.inc())
                    dve.wait_ge(*S.exp_ready.reach(1))
                    link(dve, S.dve_step, nc.vector.reduce_sum(tot[:, t0:], ex[:, t0:, :], axis=AX.X))
                    link(dve, S.dve_step, nc.vector.reciprocal(tot[:, t0:], tot[:, t0:]))
                    dve.wait_ge(*S.pool.reach(3))
                    nc.vector.tensor_tensor(weight[:, t0:, 0:E], ex[:, t0:, :],
                                            tot[:, t0:].unsqueeze(2).broadcast_to([P, nt, E]),
                                            ALU.mult).then_inc(*S.dve.inc())
                    dve.wait_ge(*S.pe.reach(2))
                    lo = t0 * P
                    nc.vector.tensor_copy(aff[:, lo:], bank[6][0:E, lo:])
                    link(dve, S.dve_step, nc.vector.tensor_copy(rest[:, lo:], bank[6][0:E, lo:]))
                    for s in range(s0, 2):
                        r = rest[:, s * CT:(s + 1) * CT]
                        for _ in range(CAP // 8):
                            link(dve, S.dve_step, nc.vector.max(best, r))
                            link(dve, S.dve_step, nc.vector.match_replace(r, best, r, -1.0))
                    link(dve, S.dve_step, nc.vector.tensor_scalar(mask[:, lo:], rest[:, lo:], 0.0, None, ALU.is_lt))
                    for s in range(s0, 2):
                        sl = slice(s * CT, (s + 1) * CT)
                        ins = nc.vector.tensor_tensor_scan(pos[:, sl], one_row, mask[:, sl], 0.0, ALU.mult, ALU.add)
                    link(dve, S.dve_step, ins)
                    nc.vector.tensor_tensor(pos[:, lo:], pos[:, lo:], mask[:, lo:], ALU.mult).then_inc(*S.dve.inc())
                    dve.wait_ge(*S.pe.reach(3))
                    link(dve, S.dve_step, nc.vector.tensor_copy(
                        posT[:, t0:, :], bank[7][:, t0 * E:NT * E].rearrange("p (t e) -> p t e", e=E)))
                    for t in tiles:
                        ins = nc.vector.tensor_tensor(select[:, t, 0:E, :],
                                                      posT[:, t, :].unsqueeze(2).broadcast_to([P, E, CAP]),
                                                      slot_no[:, :].unsqueeze(1).broadcast_to([P, E, CAP]),
                                                      ALU.is_equal)
                    ins.then_inc(*S.dve.inc())
                    for i in range(0, len(gathers), 2):
                        src, dst = gathered_out(i)
                        dve.wait_ge(*S.gathered.reach(i + 1))
                        nc.vector.tensor_copy(dst, src).then_inc(*S.x_added.inc())

        def experts(l, last):
            tiles = [2, 3] if last else [0, 1, 2, 3]
            t0, s0 = tiles[0], tiles[0] // 2
            ns, nt, lo = 2 - s0, len(tiles), t0 * P
            M = CAP * ns
            n0 = first["moe", l]

            def weights_at(j, k4, cols):
                return slot_view(n0 + j, k4, cols)

            with stage() as block:
                @block.sync
                def _(sp):
                    with sp.Fori(0, E - 1) as e:
                        for j in range(6):
                            sp.wait_ge(S.weights_used.sem, n0 + 6 * e + j + 1)
                            src = a[("exp_w1", "exp_w3", "exp_w1", "exp_w3", "exp_w2", "exp_w2")[j]][l]
                            k4 = (0, 0, 1, 1, 0, 1)[j]
                            sp.dma_start(weights_at(j, 4, 1024),
                                         src[bass.ds(e + 1, 1), k4 * 512:(k4 + 1) * 512, :]
                                         .rearrange("e (k p) n -> p (e k) n", p=P)) \
                                .then_inc(slot_loaded[(n0 + j) % SLOTS], 16)
                    for n in range(n0 + 6 * E, n0 + 6 * E + SLOTS):
                        load(sp, n)

                @block.gpsimd
                def _(pool):
                    def stage_in(e, b):
                        for half in range(2):
                            for s in range(s0, 2):
                                at = 64 * half + CAP * (s - s0)
                                ins = nc.gpsimd.tensor_tensor(
                                    placed[:, b, 2 * s:2 * s + 2, at:at + CAP],
                                    select[:, 2 * s:2 * s + 2, bass.ds(e, 1), :].rearrange("p t e c -> p t (e c)"),
                                    weight[:, 2 * s:2 * s + 2, bass.ds(e, 1)].broadcast_to([P, 2, CAP]), ALU.mult)
                        return ins

                    def tokens_in(e, b):
                        nc.gpsimd.tensor_copy(xs[:, b, :, 0:M],
                                              xs_all[:, :, bass.ds(e, 1), 0:M].rearrange("p k e c -> p k (e c)"))

                    nc.gpsimd.memset(placed[:, :, :, :], 0.0).then_inc(*S.pool.inc())
                    pool.wait_ge(*S.pool.latest())
                    for e in range(2):
                        tokens_in(e, e)
                        stage_in(e, e).then_inc(S.sel_ready.sem, 1)
                    with pool.Fori(0, E // 2 - 1) as i:
                        for j in range(2):
                            pool.wait_ge(S.selT_done.sem, S.selT_done.base + 2 * i + j + 2)
                            tokens_in(2 * i + 2 + j, j)
                            stage_in(2 * i + 2 + j, j).then_inc(S.sel_ready.sem, 1)
                    pool.wait_ge(*S.selT_done.reach(E))
                    stage_in(E, 0).then_inc(S.sel_ready.sem, 1)

                @block.tensor
                def _(pe):
                    def turn_selection(b):
                        for t in tiles:
                            ins = nc.tensor.transpose(bank[1][:, t * P:(t + 1) * P], placed[:, b, t, :], ident)
                        ins.then_inc(S.selT_done.sem, 1)

                    def scatter(e, b):
                        pe.wait_ge(S.ys_ready.sem, S.ys_ready.base + e + 2)
                        for i, d in enumerate(SCATTER):
                            half = 64 * (d // 4)
                            pe.wait_ge(S.x_added.sem, S.x_added.base + 8 * e + 9 + max(i - 2, 0))
                            nc.tensor.matmul(bank[OUT_BANKS[i % 3]][:, lo:], ys[half:half + M, b, (d % 4) * P:(d % 4 + 1) * P],
                                             selT[half:half + M, b, lo:], start=True, stop=True) \
                                .then_inc(S.scattered.sem, 1)

                    pe.wait_ge(*S.sel_ready.reach(1))
                    turn_selection(0)
                    with pe.Fori(0, E // 2) as i:
                        for b in range(2):
                            e = 2 * i + b
                            pe.wait_ge(S.sel_ready.sem, S.sel_ready.base + e + 1)
                            pe.wait_ge(S.hid_ready.sem, S.hid_ready.base + 2 * e + 2)
                            for kh in range(2):
                                for j in (2 * kh, 2 * kh + 1):
                                    pe.wait_ge(slot_loaded[(n0 + j) % SLOTS], 16 * ((n0 + j) // SLOTS + 1) + 16 * e)
                                w1, w3 = weights_at(2 * kh, 4, 1024), weights_at(2 * kh + 1, 4, 1024)
                                for c in range(2):
                                    for k in range(4):
                                        st, en = kh == 0 and k == 0, kh == 1 and k == 3
                                        x = xs[:, b, 4 * kh + k, 0:M]
                                        nc.tensor.matmul(bank[2 + c][0:M, :], x, w1[:, k, c * 512:(c + 1) * 512],
                                                         start=st, stop=en)
                                        ins = nc.tensor.matmul(bank[2 + c][64:64 + M, :], x,
                                                               w3[:, k, c * 512:(c + 1) * 512], start=st, stop=en)
                                    if kh == 1 and c == 0:
                                        ins.then_inc(S.w13_done.sem, 1)
                                ins.then_inc(S.weights_used.sem, 2)
                            scatter(e - 1, 1 - b)
                            pe.wait_ge(S.sel_ready.sem, S.sel_ready.base + e + 2)
                            pe.wait_ge(S.hid_ready.sem, S.hid_ready.base + 2 * e + 4)
                            pe.wait_ge(S.hidT_ready.sem, S.hidT_ready.base + e + 1)
                            turn_selection(1 - b)
                            for k in range(KD):
                                ins = nc.tensor.transpose(bank[4][:, k * 64:k * 64 + M], hid[0:M, k * P:(k + 1) * P],
                                                          ident[0:M, 0:M])
                            ins.then_inc(S.hidT_done.sem, 1)
                            pe.wait_ge(S.hidT_ready.sem, S.hidT_ready.base + e + 2)
                            for kh in range(2):
                                j = 4 + kh
                                pe.wait_ge(slot_loaded[(n0 + j) % SLOTS], 16 * ((n0 + j) // SLOTS + 1) + 16 * e)
                                w2 = weights_at(j, 4, 1024)
                                for k in range(4):
                                    for c in range(2):
                                        ins = nc.tensor.matmul(bank[5][64 * c:64 * c + M, :], hidT[:, b, 4 * kh + k, 0:M],
                                                               w2[:, k, c * 512:(c + 1) * 512],
                                                               start=(kh == 0 and k == 0), stop=(kh == 1 and k == 3))
                                ins.then_inc(S.weights_used.sem, 1)
                    scatter(E - 1, 1)

                @block.scalar
                def _(act):
                    with act.Fori(0, E // 2) as i:
                        for b in range(2):
                            e = 2 * i + b
                            for c in range(2):
                                if c == 0:
                                    act.wait_ge(S.w13_done.sem, S.w13_done.base + e + 1)
                                else:
                                    act.wait_ge(S.weights_used.sem, n0 + 6 * e + 4)
                                nc.scalar.activation(gate_s[0:M, c * 512:(c + 1) * 512], bank[2 + c][0:M, :], ACT.Silu) \
                                    .then_inc(S.silu_done.sem, 1)
                            act.wait_ge(S.hidT_done.sem, S.hidT_done.base + e + 2)
                            nc.scalar.copy(hidT[:, b, :, 0:M], bank[4][:, :].rearrange("p (k c) -> p k c", c=64)[:, :, 0:M]) \
                                .then_inc(S.hidT_ready.sem, 1)
                            act.wait_ge(S.weights_used.sem, n0 + 6 * e + 6)
                            for half in (0, 64):
                                ins = nc.scalar.copy(ys[half:half + M, b, :], bank[5][half:half + M, :])
                            ins.then_inc(S.ys_ready.sem, 1)

                @block.vector
                def _(dve):
                    def add_to_x(e):
                        for i, d in enumerate(SCATTER):
                            dve.wait_ge(S.scattered.sem, S.scattered.base + 8 * e + 9 + i)
                            for s in range(s0, 2):
                                sl = slice(s * CT, (s + 1) * CT)
                                ins = nc.vector.scalar_tensor_tensor(xT[:, d, sl], bank[OUT_BANKS[i % 3]][:, sl],
                                                                     mod[:, 5 * KD + d, s:s + 1], xT[:, d, sl],
                                                                     ALU.mult, ALU.add)
                            ins.then_inc(S.x_added.sem, 1)

                    def selT_copy(e, b):
                        dve.wait_ge(S.selT_done.sem, S.selT_done.base + e + 1)
                        nc.vector.tensor_copy(selT[:, b, lo:], bank[1][:, lo:])

                    nc.vector.memset(ys[:, 1, :], 0.0)
                    nc.vector.memset(selT[:, 1, :], 0.0).then_inc(S.ys_ready.sem, 1)
                    nc.vector.engine_nop().then_inc(S.x_added.sem, 1)
                    nc.vector.engine_nop().then_inc(S.hid_ready.sem, 2)
                    nc.vector.engine_nop().then_inc(S.hidT_ready.sem, 1)
                    nc.vector.engine_nop().then_inc(S.hidT_done.sem, 1)
                    selT_copy(0, 0)
                    with dve.Fori(0, E // 2) as i:
                        for b in range(2):
                            e = 2 * i + b
                            dve.wait_ge(S.hidT_done.sem, S.hidT_done.base + e + 1)
                            for c in range(2):
                                cols = slice(c * 512, (c + 1) * 512)
                                dve.wait_ge(S.silu_done.sem, S.silu_done.base + 2 * e + c + 1)
                                nc.vector.tensor_tensor(hid[0:M, cols], bank[2 + c][64:64 + M, :], gate_s[0:M, cols],
                                                        ALU.mult).then_inc(S.hid_ready.sem, 1)
                            add_to_x(e - 1)
                            selT_copy(e + 1, 1 - b)
                    add_to_x(E - 1)
            S.sel_ready.total += E + 1
            S.selT_done.total += E + 1
            S.hid_ready.total += 2 * E + 2
            S.w13_done.total += E
            S.silu_done.total += 2 * E
            S.weights_used.total += 6 * E
            S.hidT_done.total += E + 1
            S.hidT_ready.total += E + 1
            S.ys_ready.total += E + 1
            S.scattered.total += 8 * (E + 1)
            S.x_added.total += 8 * (E + 1) + 1

        def store_latents():
            rows = region(0, 2, D)
            with stage() as block:
                @block.tensor
                def _(pe):
                    for i in range(4):
                        for j in range(4):
                            ins = nc.tensor.transpose(bank[i][:, j * P:(j + 1) * P],
                                                      xT[:, 4 * (i % 2) + j, CT + (i // 2) * P:CT + (i // 2 + 1) * P], ident)
                        ins.then_inc(*S.pe.inc())

                @block.vector
                def _(dve):
                    for i in range(4):
                        dve.wait_ge(*S.pe.reach(i + 1))
                        nc.vector.tensor_copy(rows[:, i // 2, (i % 2) * 512:(i % 2 + 1) * 512], bank[i][:, :]) \
                            .then_inc(*S.dve.inc())

                @block.sync
                def _(sp):
                    dst = out.rearrange("b (t p) d -> p (b t) d", p=P)
                    for t in range(2):
                        sp.wait_ge(*S.dve.reach(2 * t + 2))
                        sp.dma_start(dst[:, t, :], rows[:, t, :]).then_inc(*S.stored.inc(16))
                    sp.wait_ge(*S.stored.reach(32))

        for l in range(DEPTH):
            last = l == DEPTH - 1
            q0 = CT if last else 0
            vectors_and_modulation(l)
            normalise(l, 0, 0)
            project_a(l, last)
            gates(l)
            mlstm(l, last)
            head_norm(l, last, h_sum, o_gate, region(0, NT, W), 0, "mln")
            project_b(l, last)
            mla_heads(l, last)
            mla_attention(l, last)
            project_c(l, last)
            retention(l, last)
            head_norm(l, last, h_ret, s_gate, ret_ring, 8, "retn")
            merge_branches(l, last)
            normalise(l, 1, q0)
            route(l, last)
            experts(l, last)
        store_latents()


_INS = ["x", "c", "ctx", "c_ctx", "ada_w", "ada_b", "norm1_w", "norm2_w", "w_in", "b_in", "conv_w", "conv_b",
        "ml_norm_w", "mla_qa_norm", "mla_wq_b", "mla_kva_norm", "mla_wkv_b", "q_norm_w", "k_norm_w", "ret_norm_w",
        "w_branch", "w_out", "router_w", "exp_w1", "exp_w3", "exp_w2"]


def shape_constants(np):
    i = np.arange(P)
    f32 = np.float32
    before = (i[:, None] <= i[None, :]).astype(f32)
    after = (i[:, None] >= i[None, :]).astype(f32)
    eye = np.eye(P, dtype=f32)
    big = f32(-1e30)
    half = ROPE // 4
    inv = (f32(10000.0) ** (-np.arange(half, dtype=f32) / f32(half))).astype(f32)
    tok = np.arange(LT)
    angle = [(v.astype(f32)[:, None] * inv).astype(f32) for v in (tok // 64, tok % 64)]
    cos, sin = [np.cos(v).astype(f32) for v in angle], [np.sin(v).astype(f32) for v in angle]
    rope = np.stack([np.concatenate([cos[0], cos[0], cos[1], cos[1]], 1),
                     np.concatenate([-sin[0], sin[0], -sin[1], sin[1]], 1)], 1)
    rope = rope.reshape(2, P, 2, ROPE).transpose(1, 0, 2, 3)
    g = np.log1p(-np.exp2(-5.0 - np.arange(H)))
    dt = (np.arange(3 * P)[None, :] - P - i[:, None]).astype(np.float64)
    decay = np.zeros((H, P, 2, 3 * P))
    for h in range(H):
        gf, gb = g[h], g[H - 1 - h]
        decay[h, :, 0] = np.where(dt >= 0, np.exp(np.maximum(dt, 0) * gf), 0) + \
            np.where(dt <= 0, np.exp(np.maximum(-dt, 0) * gb), 0)
        decay[h, :, 1] = np.exp((CT + dt) * gf) + np.exp((CT - dt) * gb)
    return {
        "consts": np.concatenate([eye, np.ones((P, P), f32), before, after], 1),
        "masks": np.concatenate([eye, big * (1 - before), big * (1 - after)], 1),
        "rope": rope.astype(f32),
        "slot_no": np.tile(np.arange(1, CAP + 1, dtype=f32), (P, 1)),
        "decay": (decay * RK ** -0.5).astype(f32),
    }


def kernel(**inputs):
    import numpy as np
    import concourse.bacc as bacc
    from concourse.bass_utils import run_bass_kernel_spmd

    nc = bacc.Bacc("TRN2", target_bir_lowering=False, num_devices=1)
    arrays = {name: np.ascontiguousarray(inputs[name]) for name in _INS}
    arrays.update({k: np.ascontiguousarray(v) for k, v in shape_constants(np).items()})
    aps = {name: nc.dram_tensor(f"in_{name}", v.shape, mybir.dt.from_np(v.dtype), kind="ExternalInput").ap()
           for name, v in arrays.items()}
    out = nc.dram_tensor("out_latents", (1, LT, D), F32, kind="ExternalOutput").ap()
    build_program(nc, aps, out)
    r = run_bass_kernel_spmd(nc, [{f"in_{name}": v for name, v in arrays.items()}], core_ids=[0])
    return r.results[0]["out_latents"]
```

```python
import concourse.bass as bass
from concourse import mybir
from contextlib import ExitStack

F32 = mybir.dt.float32
BF16 = mybir.dt.bfloat16
ALU = mybir.AluOpType
ACT = mybir.ActivationFunctionType
AX = mybir.AxisListType

P = 128
D = 1024
KD = D // P
CT, LT = 256, 256
T = CT + LT
NT = T // P
DEPTH = 2
H = 8
W = 512
DH = 64
Q_LORA, KV_LORA, NOPE, ROPE, QK = 384, 256, 64, 32, 96
RK = 32
E, FF, CAP = 16, 1024, 32
EPS = 1e-6
C_QK, C_V, C_O, C_G, C_QL, C_KV = 0, 1024, 1536, 2048, 2080, 2464
C_RQ, C_RV, C_RG, C_LOG = 2752, 3264, 3776, 4288
SLOTS, SLOT = 6, 4096
VA = dict(ada=0, n1=48, n2=56, bqk=64, blog=72, cb=96)
VA_N = 104
VB = dict(cw=0, qa=40, kva=43, mln=45, retn=49)
VB_N = 53


class Signal:

    def __init__(self, sem):
        self.sem, self.base, self.total = sem, 0, 0

    def inc(self, n=1):
        self.total += n
        return self.sem, n

    def reach(self, n):
        return self.sem, self.base + n

    def latest(self):
        return self.sem, self.total


def token_runs(tiles):
    runs = []
    for t in tiles:
        if runs and runs[-1][0] + runs[-1][1] == t:
            runs[-1][1] += 1
        else:
            runs.append([t, 1])
    return runs


def seen_by(direction, s, last):
    if direction == 0:
        tiles = range(s, NT)
    else:
        tiles = {0: (0, 2, 3), 1: (0, 1, 2, 3), 2: (2,), 3: (2, 3)}[s]
    return [t for t in tiles if not last or t >= 2]


def build_program(nc, a, out):
    ctx = ExitStack()
    with ctx:
        def sb(name, shape, dt=F32):
            return ctx.enter_context(nc.sbuf_tensor(name, shape, dt))

        ring = sb("ring", [P, SLOTS, SLOT])
        xT = sb("xT", [P, KD, T])
        hT = sb("hT", [P, KD, T])
        work = sb("work", [P, 12544 + 6144])
        consts = sb("consts", [P, 4 * P])
        cbf = sb("cbf", [P, 3 * P], BF16)
        pick3 = sb("pick3", [P, H], BF16)
        rope = sb("rope", [P, 2, 2, ROPE])
        slot_no = sb("slot_no", [P, CAP])
        condT = sb("condT", [P, KD, 32])
        vA = sb("vA", [P, DEPTH, VA_N])
        vB = sb("vB", [P, DEPTH, VB_N])
        mod = sb("mod", [P, DEPTH, 48, 2])
        scale12 = sb("scale12", [P, DEPTH, 2, KD, 2])
        eps = sb("eps", [P, 1])
        bank = [ctx.enter_context(nc.psum_tensor(f"bank{i}", [P, 512], F32)) for i in range(8)]

        ident, ones = consts[:, 0:P], consts[:, P:2 * P]
        tri_le, tri_ge = consts[:, 2 * P:3 * P], consts[:, 3 * P:4 * P]
        identb, neg_f, neg_b = cbf[:, 0:P], cbf[:, P:2 * P], cbf[:, 2 * P:3 * P]

        class Signals:
            def __init__(self, names):
                self.all = [Signal(ctx.enter_context(nc.semaphore(name))) for name in names]
                (self.pe, self.act, self.dve, self.pool, self.weights_used, self.small_loaded, self.stored,
                 self.rows_ready, self.w_ready, self.p_ready, self.pv_done, self.scores_ready, self.num_read,
                 self.dve_step, self.act_step, self.even_table, self.odd_table, self.sel_ready, self.gathered,
                 self.selT_done, self.w13_done, self.silu_done, self.hid_ready, self.hidT_done,
                 self.hidT_ready, self.ys_ready, self.scattered, self.x_added, self.xs_ready,
                 self.selT_ready, self.max_ready, self.exp_ready, self.pT_done, self.pT_ready, self.gate_pe,
                 self.gate_act, self.gate_dve, self.masked_ready, self.norm_pe, self.norm_act,
                 self.norm_dve, self.x_loaded, self.mod_rows_ready, self.mod_turned, self.mod_added,
                 self.vectors_turned) = self.all

        S = Signals(("pe", "act", "dve", "pool", "weights_used", "small_loaded", "stored", "rows_ready",
            "w_ready", "p_ready", "pv_done", "scores_ready", "num_read", "dve_step", "act_step",
            "even_table", "odd_table", "sel_ready", "gathered", "selT_done", "w13_done", "silu_done",
            "hid_ready", "hidT_done", "hidT_ready", "ys_ready", "scattered", "x_added",
            "xs_ready", "selT_ready", "max_ready", "exp_ready", "pT_done", "pT_ready", "gate_pe", "gate_act",
            "gate_dve", "masked_ready", "norm_pe", "norm_act", "norm_dve",
            "x_loaded", "mod_rows_ready", "mod_turned", "mod_added", "vectors_turned"))
        slot_loaded = [ctx.enter_context(nc.semaphore(f"slot_loaded{i}")) for i in range(SLOTS)]

        def link(eng, sig, ins):
            ins.then_inc(*sig.inc())
            eng.wait_ge(*sig.latest())

        def stage():
            for s in S.all:
                s.base = s.total
            return nc.Block(no_gpsimd_drain=True)

        def region(at, *shape):
            n = 1
            for x in shape:
                n *= x
            v = work[:, at:at + n]
            if len(shape) == 2:
                return v.rearrange("p (a b) -> p a b", a=shape[0])
            if len(shape) == 3:
                return v.rearrange("p (a b c) -> p a b c", a=shape[0], b=shape[1])
            if len(shape) == 4:
                return v.rearrange("p (a b c d) -> p a b c d", a=shape[0], b=shape[1], c=shape[2])
            return v

        loads = []
        first = {}

        def add(key, srcs):
            first[key] = len(loads)
            loads.extend(srcs)

        def k_major(src):
            return src.rearrange("(k p) n -> p k n", p=P)

        def add_modulation(l, r):
            ada = k_major(a["ada_w"][l])
            add(("ada", l, r), [ada[:, :, j * 512:(j + 1) * 512] for j in range(4 * r, 4 * r + 4)])

        add_modulation(0, 0)
        for l in range(DEPTH):
            w_in = k_major(a["w_in"][l])

            def add_w_in(key, c, n):
                add((key, l), [w_in[:, :, c:c + n]])

            add_w_in("g", C_G, 32)
            add_w_in("qk", C_QK, 512)
            add_w_in("qk2", C_QK + 512, 512)
            if l == 0:
                add_modulation(0, 1)
            add_w_in("o", C_O, 512)
            if l == 0:
                add_modulation(0, 2)
            add_w_in("v", C_V, 512)
            add(("b", l), [w_in[:, :, c:c + n] for c, n in ((C_QL, 384), (C_KV, 288))])
            add(("bh", l), [k_major(a["mla_wq_b"][l]), k_major(a["mla_wkv_b"][l])])
            for i, (key, c) in enumerate((("rqk", C_RQ), ("rv", C_RV), ("rg", C_RG))):
                add_w_in(key, c, 512)
                if l == 0:
                    add_modulation(1, i)
            merge = []
            for n in range(3):
                for c in range(2):
                    col = C_LOG + n * D + c * 512
                    merge.append(w_in[:, :, col:col + 512])
                    merge.append(k_major(a["w_branch"][l, n])[:, :, c * 512:(c + 1) * 512])
            add(("merge", l), merge)
            add(("out", l), [k_major(a["w_out"][l])[:, :, c * 512:(c + 1) * 512] for c in range(2)])
            experts = []
            for e in range(E):
                w1, w3, w2 = (k_major(a[x][l, e]) for x in ("exp_w1", "exp_w3", "exp_w2"))
                experts += [w1[:, 0:4], w3[:, 0:4], w1[:, 4:8], w3[:, 4:8], w2[:, 0:4], w2[:, 4:8]]
            add(("moe", l), experts)

        def slot_view(n, k, cols):
            return ring[:, n % SLOTS, 0:k * cols].rearrange("p (k n) -> p k n", k=k)

        def load(sp, n):
            if n >= len(loads):
                return
            if n >= SLOTS:
                sp.wait_ge(S.weights_used.sem, n - SLOTS + 1)
            src = loads[n]
            sp.dma_start(slot_view(n, src.shape[1], src.shape[2]), src).then_inc(slot_loaded[n % SLOTS], 16)

        def run_ahead(sp, key, next_key):
            for n in range(first[key] + SLOTS, first[next_key] + SLOTS):
                load(sp, n)

        def arrived(pe, n):
            pe.wait_ge(slot_loaded[n % SLOTS], 16 * (n // SLOTS + 1))

        class Vectors:

            def __init__(self, l, at):
                self.l = l
                self.rows_a, self.rows_b = work[0:VA_N, at:at + P], work[0:VB_N, at + P:at + 2 * P]

            def load(self, pool):
                l = self.l

                def rows(dst, at, src):
                    pool.dma_start(dst[at:at + src.shape[0], :], src).then_inc(*S.small_loaded.inc(16))

                def cut(v):
                    return v.rearrange("(r p) -> r p", p=P)

                rows(self.rows_a, VA["ada"], cut(a["ada_b"][l]))
                rows(self.rows_a, VA["n1"], cut(a["norm1_w"][l]))
                rows(self.rows_a, VA["n2"], cut(a["norm2_w"][l]))
                rows(self.rows_a, VA["bqk"], cut(a["b_in"][l, C_QK:C_QK + 1024]))
                rows(self.rows_a, VA["blog"], cut(a["b_in"][l, C_LOG:C_LOG + 3 * D]))
                rows(self.rows_a, VA["cb"], cut(a["conv_b"][l]))
                rows(self.rows_b, VB["cw"], a["conv_w"][l].rearrange("j (r p) -> (j r) p", p=P))
                rows(self.rows_b, VB["qa"], cut(a["mla_qa_norm"][l]))
                rows(self.rows_b, VB["kva"], cut(a["mla_kva_norm"][l]))
                rows(self.rows_b, VB["mln"], cut(a["ml_norm_w"][l]))
                rows(self.rows_b, VB["retn"], cut(a["ret_norm_w"][l]))

            def turn(self, pe, b):
                nc.tensor.transpose(b[:, 0:VA_N], self.rows_a, ident[0:VA_N, 0:VA_N])
                nc.tensor.transpose(b[:, P:P + VB_N], self.rows_b, ident[0:VB_N, 0:VB_N]) \
                    .then_inc(*S.vectors_turned.inc())

            def store(self, dve, b):
                dve.wait_ge(*S.vectors_turned.reach(1))
                nc.vector.tensor_copy(vA[:, self.l, :], b[:, 0:VA_N])
                link(dve, S.dve_step, nc.vector.tensor_copy(vB[:, self.l, :], b[:, P:P + VB_N]))

        class Modulation:

            def __init__(self, l, r, i, at, product_bank, turn_bank):
                self.l, self.r, self.i = l, r, i
                self.rows = region(at, 512)
                self.a, self.b = product_bank, turn_bank
                self.n0 = first["ada", l, r]

            def product(self, pe):
                if self.i:
                    pe.wait_ge(*S.mod_rows_ready.reach(self.i))
                for j in range(4):
                    arrived(pe, self.n0 + j)
                for k in range(KD):
                    for j in range(4):
                        ins = nc.tensor.matmul(self.a[32 * j:32 * j + 32, :], condT[:, k, :],
                                               slot_view(self.n0 + j, KD, 512)[:, k, :],
                                               start=(k == 0), stop=(k == KD - 1))
                ins.then_inc(*S.weights_used.inc(4))

            def copy_rows(self, act):
                if self.i:
                    act.wait_ge(*S.mod_turned.reach(self.i))
                act.wait_ge(S.weights_used.sem, self.n0 + 4)
                nc.scalar.copy(self.rows, self.a[:, :]).then_inc(*S.mod_rows_ready.inc())

            def turn(self, pe):
                pe.wait_ge(*S.mod_rows_ready.reach(self.i + 1))
                if self.i:
                    pe.wait_ge(*S.mod_added.reach(self.i))
                for i in range(4):
                    ins = nc.tensor.transpose(self.b[:, i * P:(i + 1) * P], self.rows[:, i * P:(i + 1) * P], ident)
                ins.then_inc(*S.mod_turned.inc())

            def add(self, dve):
                dve.wait_ge(*S.mod_turned.reach(self.i + 1))
                for j in range(4):
                    at = 16 * self.r + 4 * j
                    ins = nc.vector.tensor_tensor(
                        mod[:, self.l, at:at + 4, :],
                        self.b[:, :].rearrange("p (i w) -> p i w", i=4)[:, :, 32 * j:32 * j + 2],
                        vA[:, self.l, at:at + 4].unsqueeze(2).broadcast_to([P, 4, 2]), ALU.add)
                ins.then_inc(*S.mod_added.inc())
                dve.wait_ge(*S.mod_added.latest())
                if self.r != 1:
                    i, item = (0, 1) if self.r == 0 else (1, 4)
                    w = vA[:, self.l, VA["n1" if i == 0 else "n2"]:][:, 0:KD].unsqueeze(2).broadcast_to([P, KD, 2])
                    link(dve, S.dve_step, nc.vector.scalar_tensor_tensor(
                        scale12[:, self.l, i, :, :], mod[:, self.l, item * KD:(item + 1) * KD, :], 1.0, w,
                        ALU.add, ALU.mult))

        x_rows = region(0, NT, D)
        cond_rows = work[0:2 * KD, 4096:4096 + P]
        mask_in = work[:, 4224:4224 + 3 * P]
        with stage() as block:
            vectors = Vectors(0, 4608)
            shifts = Modulation(0, 0, 0, 5120, bank[4], bank[5])

            @block.sync
            def _(sp):
                for dst, src in (
                        (consts[:, :], a["consts"]),
                        (cond_rows[0:KD, :], a["c_ctx"].rearrange("(k p) -> k p", p=P)),
                        (cond_rows[KD:2 * KD, :], a["c"].rearrange("b (k p) -> (b k) p", p=P)),
                        (x_rows[:, 0:2, :], a["ctx"].rearrange("b (t p) d -> p (b t) d", p=P)),
                        (x_rows[:, 2:4, :], a["x"].rearrange("b (t p) d -> p (b t) d", p=P))):
                    sp.dma_start(dst, src).then_inc(*S.x_loaded.inc(16))
                for n in range(SLOTS):
                    load(sp, n)
                run_ahead(sp, ("ada", 0, 0), ("g", 0))

            @block.gpsimd
            def _(pool):
                nc.gpsimd.memset(condT[:, :, :], 0.0).then_inc(*S.pool.inc())
                nc.gpsimd.memset(eps[:, :], EPS).then_inc(*S.pool.inc())
                vectors.load(pool)
                for dst, src in ((mask_in, a["masks"]), (rope[:, :, :, :], a["rope"]), (slot_no[:, :], a["slot_no"])):
                    pool.dma_start(dst, src).then_inc(*S.small_loaded.inc(16))

            @block.tensor
            def _(pe):
                pe.wait_ge(*S.x_loaded.reach(16 * 5))
                nc.tensor.transpose(bank[7][:, 0:2 * KD], cond_rows, ident[0:2 * KD, 0:2 * KD]) \
                    .then_inc(*S.pe.inc())
                for k in range(KD):
                    if k >= 4:
                        pe.wait_ge(*S.dve.reach(k - 3))
                    for t in range(NT):
                        ins = nc.tensor.transpose(bank[k % 4][:, t * P:(t + 1) * P],
                                                  x_rows[:, t, k * P:(k + 1) * P], ident)
                    ins.then_inc(*S.pe.inc())
                pe.wait_ge(*S.act.reach(1))
                pe.wait_ge(*S.small_loaded.reach(16 * 14))
                vectors.turn(pe, bank[6])
                shifts.product(pe)
                shifts.turn(pe)

            @block.scalar
            def _(act):
                act.wait_ge(*S.pool.reach(2))
                act.wait_ge(*S.pe.reach(1))
                nc.scalar.activation(condT[:, :, 0:2], bank[7][:, 0:2 * KD].rearrange("p (s k) -> p k s", s=2),
                                     ACT.Silu).then_inc(*S.act.inc())
                shifts.copy_rows(act)

            @block.vector
            def _(dve):
                for k in range(KD):
                    dve.wait_ge(*S.pe.reach(k + 2))
                    nc.vector.tensor_copy(xT[:, k, :], bank[k % 4][:, :]).then_inc(*S.dve.inc())
                dve.wait_ge(*S.small_loaded.reach(16 * 14))
                link(dve, S.dve_step, nc.vector.tensor_copy(cbf[:, :], mask_in))
                link(dve, S.dve_step, nc.vector.tensor_tensor(pick3[:, :], identb[:, 0:H], identb[:, 32:32 + H],
                                                              ALU.add))
                nc.vector.tensor_tensor(pick3[:, :], pick3[:, :], identb[:, 64:64 + H], ALU.add)
                vectors.store(dve, bank[6])
                shifts.add(dve)

        def normalise(l, which, q0):
            square = region(0, KD, T)
            root, inv = region(4096, T), region(4096 + T, T)
            with stage() as block:
                @block.scalar
                def _(act):
                    for k in range(KD):
                        nc.scalar.activation(square[:, k, q0:], xT[:, k, q0:], ACT.Square).then_inc(*S.act.inc())
                    act.wait_ge(*S.pe.reach(1))
                    nc.scalar.activation(root[:, q0:], bank[0][:, q0:], ACT.Sqrt, scale=1.0 / D,
                                         bias=eps[:, 0:1]).then_inc(*S.act.inc())
                    for k in range(KD):
                        act.wait_ge(*S.dve.reach(k + 1))
                        for s in range(q0 // CT, 2):
                            ins = nc.scalar.activation(hT[:, k, s * CT:(s + 1) * CT], hT[:, k, s * CT:(s + 1) * CT],
                                                       ACT.Identity, bias=mod[:, l, 3 * which * KD + k, s:s + 1])
                    ins.then_inc(*S.act.inc())

                @block.tensor
                def _(pe):
                    for k in range(KD):
                        pe.wait_ge(*S.act.reach(k + 1))
                        ins = nc.tensor.matmul(bank[0][:, q0:], ones, square[:, k, q0:], start=(k == 0),
                                               stop=(k == KD - 1))
                    ins.then_inc(*S.pe.inc())

                @block.vector
                def _(dve):
                    dve.wait_ge(*S.act.reach(KD + 1))
                    link(dve, S.dve_step, nc.vector.reciprocal(inv[:, q0:], root[:, q0:]))
                    for k in range(KD):
                        for s in range(q0 // CT, 2):
                            sl = slice(s * CT, (s + 1) * CT)
                            ins = nc.vector.scalar_tensor_tensor(hT[:, k, sl], xT[:, k, sl],
                                                                 scale12[:, l, which, k, s:s + 1], inv[:, sl],
                                                                 ALU.mult, ALU.mult)
                        ins.then_inc(*S.dve.inc())

        def token_major(pe, jobs, banks, g=0):
            for job in jobs:
                n, cols, tiles = job[:3]
                arrived(pe, n)
                for i, t in enumerate(tiles):
                    if g >= banks:
                        pe.wait_ge(*S.dve.reach(g - banks + 1))
                    for k in range(KD):
                        ins = nc.tensor.matmul(bank[g % banks][:, 0:cols], hT[:, k, t * P:(t + 1) * P],
                                               slot_view(n, KD, cols)[:, k, :], start=(k == 0), stop=(k == KD - 1))
                    if i < len(tiles) - 1:
                        ins.then_inc(*S.pe.inc())
                    else:
                        ins.then_inc(*S.weights_used.inc())
                    g += 1

        YA, YB, YC = 12544, 12544 + 2048, 12544 + 4096
        yT = region(YA, 12, T)

        def add_bias(dve, banks, jobs, bias, g=0, jobs_before=0, after={}):
            for j, (n, cols, tiles, b0, dst) in enumerate(jobs):
                for i, t in enumerate(tiles):
                    if i < len(tiles) - 1:
                        dve.wait_ge(*S.pe.reach(g - jobs_before - j + 1))
                    else:
                        dve.wait_ge(S.weights_used.sem, n + 1)
                    src, b = bank[g % banks][:, 0:cols], bias[:, b0:b0 + cols]
                    o = dst(t)
                    if o.ndim == 3:
                        src = src.rearrange("p (h d) -> p h d", h=H)
                        b = b.rearrange("p (h d) -> p h d", h=H)
                    nc.vector.tensor_tensor(o, src, b, ALU.add).then_inc(*S.dve.inc())
                    if g in after:
                        after[g](dve)
                    g += 1

        def load_bias(pool, l, dst, col, n):
            pool.dma_start(dst, a["b_in"][l, col:col + n].partition_broadcast(P)) \
                .then_inc(*S.small_loaded.inc(16))

        qkT = region(0, 8, T)
        v_aug = region(4096, NT, H, DH + 1)
        o_gate = region(6176, NT, W)
        bias_a = region(8224, 1056)
        g_pre = region(9280, NT, 32)
        nlf, igate = region(9408, NT, 2, 32), region(9664, NT, 2, 32)
        c_tok, e_tok = region(9920, NT, 64), region(10176, NT, 64)
        c_rows, d_rows = (work[0:64, x:x + T] for x in (10432, 11456))
        stack = work[:, 10944:11456].bitcast(BF16).rearrange("p (d t) -> p d t", d=2)
        h_sum = region(YC, NT, H, DH)
        pad = region(YB, 2, 2, CT + 4)
        conv = region(YA, 2, T)

        def project_a(l, last):
            q_tiles = [2, 3] if last else [0, 1, 2, 3]
            n_g, n_qk, n_o, n_v = (first[key, l] for key in ("g", "qk", "o", "v"))
            jobs = [(n_g, 32, range(NT), 1024, lambda t: g_pre[:, t, :]),
                    (n_o, 512, q_tiles, 512, lambda t: o_gate[:, t, :]),
                    (n_v, 512, range(NT), 0, lambda t: v_aug[:, t, :, 0:DH])]
            rounds = [] if l else [Modulation(0, 1, 0, YC, bank[2], bank[3]), Modulation(0, 2, 1, YC, bank[2], bank[3])]
            m_rows = work[0:64, YC:YC + T]
            hi, mid = (work[0:64, x:x + T // 2].bitcast(BF16) for x in (YC + 512, YC + 768))
            m, mag = region(YC + 1024, NT, 2, H), region(YC + 1088, NT, 2, H)
            cum = work[0:64, YC + 1280:YC + 1792]
            g4 = g_pre.rearrange("p t (g h) -> p t g h", g=4)
            with stage() as block:
                @block.sync
                def _(sp):
                    run_ahead(sp, ("g", l), ("b", l))

                @block.gpsimd
                def _(pool):
                    load_bias(pool, l, bias_a, C_V, 1056)
                    nc.gpsimd.memset(region(9408, 512), 0.0).then_inc(*S.pool.inc())
                    nc.gpsimd.memset(pad[:, :, :, :], 0.0).then_inc(*S.pool.inc())
                    nc.gpsimd.memset(v_aug[:, :, :, DH:DH + 1], 1.0).then_inc(*S.pool.inc())
                    nc.gpsimd.memset(stack[:, :, :], 0.0).then_inc(*S.pool.inc())

                @block.tensor
                def _(pe):
                    def running_sums():
                        pe.wait_ge(*S.gate_dve.reach(2))
                        for d in range(2):
                            rows = slice(32 * d, 32 * d + 32)
                            for t in range(NT):
                                cols = slice(t * P, (t + 1) * P)
                                if d == 0:
                                    passed = [s for s in range(t)]
                                else:
                                    passed = [1] if t == 0 else [] if t == 1 else [0, 1, 3] if t == 2 else [0, 1]
                                for i, s in enumerate(passed):
                                    nc.tensor.matmul(bank[2][rows, cols], nlf[:, s, d, :], ones, start=(i == 0),
                                                     stop=False)
                                nc.tensor.matmul(bank[2][rows, cols], nlf[:, t, d, :], tri_ge if d else tri_le,
                                                 start=not passed, stop=True)
                                ins = nc.tensor.matmul(bank[3][rows, cols], igate[:, t, d, :], ident, start=True,
                                                       stop=True)
                        ins.then_inc(*S.gate_pe.inc())

                    def rows_to_columns():
                        pe.wait_ge(*S.gate_dve.reach(3))
                        for i, rows in enumerate((c_rows, d_rows)):
                            for t in range(NT):
                                ins = nc.tensor.transpose(bank[4 + i][:, t * 64:(t + 1) * 64],
                                                          rows[:, t * P:(t + 1) * P], ident[0:64, 0:64])
                        ins.then_inc(*S.gate_pe.inc())

                    token_major(pe, jobs[:1], 2)
                    for f in range(8):
                        if f % 4 == 0:
                            arrived(pe, n_qk + f // 4)
                        if f >= 2:
                            pe.wait_ge(*S.act.reach(max(1, 2 * f - 4)))
                        t0 = CT if last and f < 4 else 0
                        for k in range(KD):
                            ins = nc.tensor.matmul(bank[6 + f % 2][:, t0:], slot_view(n_qk + f // 4, KD, 512)[:, k, (f % 4) * P:(f % 4 + 1) * P],
                                                   hT[:, k, t0:], start=(k == 0), stop=(k == KD - 1))
                        if f % 4 < 3:
                            ins.then_inc(*S.pv_done.inc())
                        else:
                            ins.then_inc(*S.weights_used.inc())
                        if f == 1:
                            running_sums()
                        if f == 4:
                            rows_to_columns()
                    for i, job in enumerate(jobs[1:]):
                        if rounds:
                            rounds[i].product(pe)
                        token_major(pe, [job], 2, NT + i * len(q_tiles))
                        if rounds:
                            rounds[i].turn(pe)

                @block.scalar
                def _(act):
                    act.wait_ge(*S.gate_dve.reach(1))
                    link(act, S.act_step, nc.scalar.activation(mag, mag, ACT.Exp, scale=-1.0))
                    nc.scalar.activation(mag, mag, ACT.Ln, bias=1.0).then_inc(*S.gate_act.inc())
                    act.wait_ge(*S.pool.reach(2))
                    for f in range(9):
                        if f == 2:
                            act.wait_ge(*S.gate_pe.reach(1))
                            nc.scalar.copy(cum, bank[2][0:64, :]).then_inc(*S.gate_act.inc())
                        if f == 4:
                            act.wait_ge(*S.gate_dve.reach(3))
                            act.wait_ge(*S.pool.reach(4))
                            for i, part in enumerate((hi, mid, m_rows)):
                                for d in range(2):
                                    nc.scalar.copy(stack[32 * i:32 * i + 32, d, :], part[32 * d:32 * d + 32, :])
                        if f == 6:
                            act.wait_ge(*S.gate_pe.reach(2))
                            nc.scalar.activation(e_tok, bank[5][:, 0:256].rearrange("p (t r) -> p t r", t=NT), ACT.Exp)
                        if f < 8:
                            if f % 4 < 3:
                                act.wait_ge(*S.pv_done.reach(f - f // 4 + 1))
                            else:
                                act.wait_ge(S.weights_used.sem, n_qk + f // 4 + 1)
                            if f >= 2:
                                act.wait_ge(*S.p_ready.reach(f - 1))
                            for s in range(1 if last and f < 4 else 0, 2):
                                ins = nc.scalar.activation(pad[:, f % 2, s, 2:2 + CT],
                                                           bank[6 + f % 2][:, s * CT:(s + 1) * CT], ACT.Identity,
                                                           bias=vA[:, l, VA["bqk"] + f:VA["bqk"] + f + 1])
                            ins.then_inc(*S.act.inc())
                        if f >= 1:
                            g = f - 1
                            t0 = CT if last and g < 4 else 0
                            act.wait_ge(*S.p_ready.reach(g + 1))
                            nc.scalar.activation(qkT[:, g, t0:], conv[:, g % 2, t0:], ACT.Silu,
                                                 bias=vA[:, l, VA["cb"] + g:VA["cb"] + g + 1]).then_inc(*S.act.inc())
                    if rounds:
                        rounds[0].copy_rows(act)
                    act.wait_ge(*S.dve.reach(NT + len(q_tiles)))
                    for t in q_tiles:
                        nc.scalar.activation(o_gate[:, t, :], o_gate[:, t, :], ACT.Sigmoid)
                    if rounds:
                        rounds[1].copy_rows(act)

                @block.vector
                def _(dve):
                    def min_and_magnitude():
                        for d in range(2):
                            f = g4[:, :, 2 * d + 1, :]
                            nc.vector.tensor_copy(igate[:, :, d, 0:H], g4[:, :, 2 * d, :])
                            link(dve, S.dve_step, nc.vector.tensor_scalar(m[:, :, d, :], f, 0.0, None, ALU.min))
                            ins = nc.vector.scalar_tensor_tensor(mag[:, :, d, :], m[:, :, d, :], -2.0, f,
                                                                 ALU.mult, ALU.add)
                        ins.then_inc(*S.gate_dve.inc())

                    def minus_log_f():
                        dve.wait_ge(*S.gate_act.reach(1))
                        for d in range(2):
                            ins = nc.vector.tensor_tensor(nlf[:, :, d, 0:H], mag[:, :, d, :], m[:, :, d, :],
                                                          ALU.subtract)
                        ins.then_inc(*S.gate_dve.inc())

                    def running_maxima():
                        dve.wait_ge(*S.gate_act.reach(2))
                        link(dve, S.dve_step, nc.vector.tensor_tensor(c_rows, bank[3][0:64, :], cum, ALU.add))
                        nc.vector.tensor_tensor_scan(m_rows[0:32, :], c_rows[0:32, :], c_rows[0:32, :], 0.0,
                                                     ALU.max, ALU.max)
                        b, mb = c_rows[32:64, :], m_rows[32:64, :]
                        link(dve, S.dve_step, nc.vector.tensor_tensor_scan(
                            mb[:, CT - 1::-1], b[:, CT - 1::-1], b[:, CT - 1::-1], 0.0, ALU.max, ALU.max))
                        link(dve, S.dve_step, nc.vector.tensor_tensor_scan(
                            mb[:, T - 1:CT - 1:-1], b[:, T - 1:CT - 1:-1], b[:, T - 1:CT - 1:-1], mb[:, 0:1],
                            ALU.max, ALU.max))
                        link(dve, S.dve_step, nc.vector.tensor_scalar(m_rows, m_rows, -1.0, None, ALU.mult))
                        nc.vector.tensor_tensor(d_rows, cum, m_rows, ALU.add)
                        link(dve, S.dve_step, nc.vector.tensor_copy(hi, m_rows))
                        link(dve, S.dve_step, nc.vector.tensor_tensor(m_rows, m_rows, hi, ALU.subtract))
                        link(dve, S.dve_step, nc.vector.tensor_copy(mid, m_rows))
                        nc.vector.tensor_tensor(m_rows, m_rows, mid, ALU.subtract).then_inc(*S.gate_dve.inc())

                    dve.wait_ge(*S.small_loaded.reach(16))
                    add_bias(dve, 2, jobs[:1], bias_a)
                    dve.wait_ge(*S.dve.latest())
                    dve.wait_ge(*S.pool.reach(1))
                    min_and_magnitude()
                    for f in range(8):
                        dve.wait_ge(*S.act.reach(1 if f == 0 else 2 * f))
                        if f >= 2:
                            dve.wait_ge(*S.act.reach(2 * f - 1))
                        s0 = 1 if last and f < 4 else 0
                        o = conv[:, f % 2, s0 * CT:].rearrange("p (s t) -> p s t", t=CT)
                        for j in range(5):
                            x = pad[:, f % 2, s0:, j:j + CT]
                            w = vB[:, l, VB["cw"] + j * 8 + f:VB["cw"] + j * 8 + f + 1]
                            if j == 0:
                                ins = nc.vector.tensor_scalar(o, x, w, None, ALU.mult)
                            else:
                                ins = nc.vector.scalar_tensor_tensor(o, x, w, o, ALU.mult, ALU.add)
                            if j < 4:
                                link(dve, S.dve_step, ins)
                        ins.then_inc(*S.p_ready.inc())
                        if f == 0:
                            minus_log_f()
                        if f == 1:
                            running_maxima()
                        if f == 5:
                            dve.wait_ge(*S.gate_pe.reach(2))
                            nc.vector.tensor_copy(c_tok, bank[4][:, 0:256].rearrange("p (t r) -> p t r", t=NT))
                    dve.wait_ge(*S.pool.reach(3))
                    last_o, last_v = NT + len(q_tiles) - 1, 2 * NT + len(q_tiles) - 1
                    add_bias(dve, 2, jobs[1:], bias_a, NT, 1,
                             after={last_o: rounds[0].add, last_v: rounds[1].add} if rounds else {})

        def mlstm(l, last):
            w_ring, p_ring = region(YA, 4, T), region(YB, 4, T)
            small = region(YA - 512, 512)
            t0 = 2 if last else 0
            nq = NT - t0
            items = [[(s, seen_by(d, s, last)) for s in range(NT)] for d in range(2)]
            ends = [0]
            for u in range(2 * H):
                ends.append(ends[-1] + len(items[u % 2]))
            lo = t0 * P

            def num(u):
                return bank[6 + u % 2][:, 0:NT * (DH + 1)].rearrange("p (t c) -> p t c", t=NT)

            def score(s):
                return bank[s][:, :] if s < 2 else bank[2][:, (s - 2) * 256:(s - 1) * 256]

            def score_at(s, t, n):
                off = t if s < 2 else t - 2
                return score(s)[:, off * P:(off + n) * P]

            with stage() as block:
                @block.tensor
                def _(pe):
                    def minus_m(b, u, stop):
                        h, d = divmod(u, 2)
                        return nc.tensor.matmul(b[:, lo:], pick3[:, h:h + 1].broadcast_to([P, P]),
                                                stack[:, d, lo:], start=True, stop=stop)

                    def rows(u):
                        if u >= 2:
                            pe.wait_ge(*S.w_ready.reach(ends[u - 1]))
                        minus_m(bank[3 + u % 2], u, True).then_inc(*S.rows_ready.inc())

                    def masked_rows(u):
                        if u:
                            pe.wait_ge(*S.w_ready.reach(ends[u]))
                        minus_m(bank[5], u, False)
                        nc.tensor.matmul(bank[5][:, lo:], identb,
                                         (neg_b if u % 2 else neg_f).unsqueeze(1).broadcast_to([P, nq, P]),
                                         start=False, stop=True).then_inc(*S.masked_ready.inc())

                    def scores(h, s):
                        at = DH * (h % 2)
                        q, k = qkT[at:at + DH, h // 2, :], qkT[at:at + DH, 4 + h // 2, :]
                        nc.tensor.matmul(score(s)[:, (lo if s < 2 else 0):], k[:, s * P:(s + 1) * P],
                                         q[:, max(lo, CT if s >= 2 else 0):], start=True, stop=True) \
                            .then_inc(*S.scores_ready.inc())

                    rows(0)
                    masked_rows(0)
                    for s in range(NT):
                        scores(0, s)
                    n = 0
                    for u in range(2 * H):
                        h, d = divmod(u, 2)
                        if u + 1 < 2 * H:
                            rows(u + 1)
                            masked_rows(u + 1)
                        if u >= 2:
                            pe.wait_ge(*S.num_read.reach(u - 1))
                        for i, (s, tiles) in enumerate(items[d]):
                            pe.wait_ge(*S.p_ready.reach(n + 1))
                            for j, t in enumerate(tiles):
                                ins = nc.tensor.matmul(num(u)[:, t, :], p_ring[:, n % 4, t * P:(t + 1) * P],
                                                       v_aug[:, s, h, :], start=(i == 0 and j == 0),
                                                       stop=(i == NT - 1 and j == len(tiles) - 1),
                                                       skip_group_check=True)
                            ins.then_inc(*S.pv_done.inc())
                            n += 1
                            if d == 1 and h + 1 < H:
                                for s2 in {0: (0,), 1: (1,), 2: (), 3: (2, 3)}[i]:
                                    scores(h + 1, s2)

                @block.scalar
                def _(act):
                    n = 0
                    for u in range(2 * H):
                        h, d = divmod(u, 2)
                        act.wait_ge(*S.rows_ready.reach(u + 1))
                        act.wait_ge(*S.masked_ready.reach(u + 1))
                        for s, tiles in items[d]:
                            if n >= 4:
                                act.wait_ge(*S.p_ready.reach(n - 3))
                            bias = c_tok[:, s, 32 * d + h:32 * d + h + 1]
                            ins = None
                            for t, k in token_runs([x for x in tiles if x != s]):
                                ins = nc.scalar.activation(w_ring[:, n % 4, t * P:(t + k) * P],
                                                           bank[3 + u % 2][:, t * P:(t + k) * P], ACT.Exp, bias=bias)
                            if s in tiles:
                                ins = nc.scalar.activation(w_ring[:, n % 4, s * P:(s + 1) * P],
                                                           bank[5][:, s * P:(s + 1) * P], ACT.Exp, bias=bias)
                            ins.then_inc(*S.w_ready.inc())
                            n += 1

                @block.vector
                def _(dve):
                    def finish(u):
                        h, d = divmod(u, 2)
                        dve.wait_ge(*S.pv_done.reach(ends[u + 1]))
                        den = num(u)[:, t0:, DH:DH + 1]
                        e = e_tok[:, t0:, 32 * d + h:32 * d + h + 1]
                        big = small[:, 0:nq].unsqueeze(2)
                        link(dve, S.dve_step, nc.vector.scalar_tensor_tensor(big, den, -1.0, e, ALU.mult, ALU.max))
                        link(dve, S.dve_step, nc.vector.tensor_tensor(big, big, den, ALU.max))
                        link(dve, S.dve_step, nc.vector.reciprocal(big, big))
                        o = h_sum[:, t0:, h, :]
                        tmp = small[:, 128:128 + nq * DH].rearrange("p (t c) -> p t c", t=nq)
                        ins = nc.vector.tensor_tensor(tmp if d else o, num(u)[:, t0:, 0:DH],
                                                      big.broadcast_to([P, nq, DH]), ALU.mult)
                        ins.then_inc(*S.num_read.inc())
                        if d:
                            dve.wait_ge(*S.num_read.latest())
                            link(dve, S.dve_step, nc.vector.tensor_tensor(o, o, tmp, ALU.add))

                    n = 0
                    for u in range(2 * H):
                        h, d = divmod(u, 2)
                        for i, (s, tiles) in enumerate(items[d]):
                            if d == 0:
                                dve.wait_ge(*S.scores_ready.reach(NT * h + (s + 1 if s < 2 else NT)))
                            dve.wait_ge(*S.w_ready.reach(n + 1))
                            if n >= 4:
                                dve.wait_ge(*S.pv_done.reach(n - 3))
                            for t, k in token_runs(tiles):
                                ins = nc.vector.scalar_tensor_tensor(
                                    p_ring[:, n % 4, t * P:(t + k) * P], score_at(s, t, k), DH ** -0.5,
                                    w_ring[:, n % 4, t * P:(t + k) * P], ALU.mult, ALU.mult)
                            ins.then_inc(*S.p_ready.inc())
                            n += 1
                            if i == 1 and u:
                                finish(u - 1)
                    finish(2 * H - 1)

        class HeadNorm:

            def __init__(self, l, last, h, gate, sq, y_out, vec):
                self.l = l
                self.t0 = 2 if last else 0
                self.nq = NT - self.t0
                self.n = self.nq * H
                self.flat = h.rearrange("p t h d -> p t (h d)")
                self.x = h[:, self.t0:].rearrange("p t h d -> p (t h) d")
                self.sq = sq[:, self.t0:].rearrange("p t (h d) -> p (t h) d", h=H)
                self.gate = gate[:, self.t0:].rearrange("p t (h d) -> p (t h) d", h=H)
                self.mean, self.var, self.dev = (region(YA - 512, 4, 32)[:, i, 0:self.n] for i in range(3))
                self.y_out, self.vec = y_out, vec

            def wide(self, v):
                return v.unsqueeze(2).broadcast_to([P, self.n, DH])

            def centre(self, dve):
                link(dve, S.dve_step, nc.vector.reduce_sum(self.mean, self.x, axis=AX.X))
                link(dve, S.dve_step, nc.vector.tensor_scalar(self.mean, self.mean, 1.0 / DH, None, ALU.mult))
                nc.vector.tensor_tensor(self.x, self.x, self.wide(self.mean), ALU.subtract) \
                    .then_inc(*S.norm_dve.inc())

            def square(self, act):
                act.wait_ge(*S.norm_dve.reach(1))
                nc.scalar.activation(self.sq, self.x, ACT.Square).then_inc(*S.norm_act.inc())

            def variance(self, dve):
                dve.wait_ge(*S.norm_act.reach(1))
                nc.vector.reduce_sum(self.var, self.sq, axis=AX.X).then_inc(*S.norm_dve.inc())

            def root(self, act):
                act.wait_ge(*S.norm_dve.reach(2))
                nc.scalar.activation(self.dev, self.var, ACT.Sqrt, scale=1.0 / DH, bias=eps[:, 0:1]) \
                    .then_inc(*S.norm_act.inc())

            def scale_and_gate(self, dve):
                dve.wait_ge(*S.norm_act.reach(2))
                link(dve, S.dve_step, nc.vector.reciprocal(self.var, self.dev))
                link(dve, S.dve_step, nc.vector.tensor_tensor(self.x, self.x, self.wide(self.var), ALU.mult))
                nc.vector.tensor_tensor(self.x, self.x, self.gate, ALU.mult).then_inc(*S.norm_dve.inc())

            def turn(self, pe):
                pe.wait_ge(*S.norm_dve.reach(3))
                for i in range(self.nq):
                    for f in range(4):
                        ins = nc.tensor.transpose(bank[4 + i][:, f * P:(f + 1) * P],
                                                  self.flat[:, self.t0 + i, f * P:(f + 1) * P], ident)
                    ins.then_inc(*S.norm_pe.inc())

            def store(self, dve):
                for i in range(self.nq):
                    dve.wait_ge(*S.norm_pe.reach(i + 1))
                    t = self.t0 + i
                    nc.vector.tensor_tensor(yT[:, self.y_out:self.y_out + 4, t * P:(t + 1) * P],
                                            bank[4 + i][:, :].rearrange("p (f t) -> p f t", f=4),
                                            vB[:, self.l, VB[self.vec]:VB[self.vec] + 4].unsqueeze(2).broadcast_to([P, 4, P]),
                                            ALU.mult).then_inc(*S.norm_dve.inc())

        qT, kT = region(0, H, T), region(4096, H, T)
        bias_b = region(5248, 672)
        q_lat, kv_lat = region(YB, NT, Q_LORA), region(4096, NT, KV_LORA + ROPE)
        k_rope = region(12288, NT, ROPE)
        qlT, kvT = region(8192, 3, T), region(9728, 2, T)
        v_mla = region(YC, NT, H, DH)

        def project_b(l, last):
            q_tiles = [2, 3] if last else [0, 1, 2, 3]
            n0 = first["b", l]
            jobs = [(n0, Q_LORA, q_tiles, 0, lambda t: q_lat[:, t, :]),
                    (n0 + 1, KV_LORA + ROPE, range(NT), Q_LORA, lambda t: kv_lat[:, t, :])]
            sums, roots = region(12416, 8), region(12424, 8)
            squares = region(10752, 2, 512)
            lows = [(q_lat, Q_LORA, t, i) for i, t in enumerate(q_tiles)] + \
                   [(kv_lat, KV_LORA, t, 4 + t) for t in range(NT)]
            norm = HeadNorm(l, last, h_sum, o_gate, region(0, NT, W), 0, "mln")
            with stage() as block:
                @block.sync
                def _(sp):
                    run_ahead(sp, ("b", l), ("bh", l))

                @block.gpsimd
                def _(pool):
                    load_bias(pool, l, bias_b, C_QL, 672)
                    nc.gpsimd.memset(sums, 1.0).then_inc(*S.pool.inc())

                @block.tensor
                def _(pe):
                    token_major(pe, jobs[:1], 4)
                    norm.turn(pe)
                    token_major(pe, jobs[1:], 4, len(q_tiles))
                    pe.wait_ge(*S.norm_dve.reach(3 + len(q_tiles)))
                    for i, (src, width, t, _) in enumerate(lows):
                        pe.wait_ge(*S.p_ready.reach(i + 1))
                        if i >= 4:
                            pe.wait_ge(*S.act.reach(i - 3))
                        for f in range(width // P):
                            ins = nc.tensor.transpose(bank[4 + i % 4][:, f * P:(f + 1) * P],
                                                      src[:, t, f * P:(f + 1) * P], ident)
                        ins.then_inc(*S.pv_done.inc())

                @block.vector
                def _(dve):
                    norm.centre(dve)
                    dve.wait_ge(*S.small_loaded.reach(16))
                    add_bias(dve, 4, jobs, bias_b, after={0: norm.variance, 1: norm.scale_and_gate,
                                                          2 if last else 3: norm.store})
                    dve.wait_ge(*S.dve.latest())
                    nc.vector.tensor_copy(k_rope, kv_lat[:, :, KV_LORA:])
                    dve.wait_ge(*S.exp_ready.reach(1))
                    link(dve, S.dve_step, nc.vector.reciprocal(roots, roots))
                    for src, width, t, j in lows:
                        nc.vector.tensor_scalar(src[:, t, 0:width], src[:, t, 0:width], roots[:, j:j + 1], None,
                                                ALU.mult).then_inc(*S.p_ready.inc())

                @block.scalar
                def _(act):
                    norm.square(act)
                    act.wait_ge(*S.pool.reach(1))
                    for i, (src, width, t, j) in enumerate(lows):
                        if i == 1:
                            norm.root(act)
                        act.wait_ge(*S.dve.reach(i + 1))
                        if i:
                            act.wait_ge(*S.w_ready.reach(i))
                        nc.scalar.activation(squares[:, 0, 0:width], src[:, t, 0:width], ACT.Square,
                                             scale=width ** -0.5, accum_out=sums[:, j:j + 1]) \
                            .then_inc(*S.w_ready.inc())
                    act.wait_ge(*S.w_ready.latest())
                    nc.scalar.activation(roots, sums, ACT.Sqrt, bias=eps[:, 0:1]).then_inc(*S.exp_ready.inc())
                    for i, (src, width, t, j) in enumerate(lows):
                        act.wait_ge(*S.pv_done.reach(i + 1))
                        dst, vec = (qlT, "qa") if width == Q_LORA else (kvT, "kva")
                        for f in range(width // P):
                            ins = nc.scalar.activation(dst[:, f, t * P:(t + 1) * P], bank[4 + i % 4][:, f * P:(f + 1) * P],
                                                       ACT.Copy, scale=vB[:, l, VB[vec] + f:VB[vec] + f + 1])
                        ins.then_inc(*S.act.inc())

        def rope_halves(src, dst, tmp, tab, heads):
            cos, sin = (tab[:, i, :].unsqueeze(1).broadcast_to([P, heads, ROPE]) for i in range(2))
            s5 = src.rearrange("p h (a b c) -> p h a b c", a=2, b=2)
            t5 = tmp.rearrange("p h (a b c) -> p h a b c", a=2, b=2)
            n5 = tab[:, 1, :].rearrange("p (a b c) -> p a b c", a=2, b=2)
            for part in range(2):
                for half in range(2):
                    nc.vector.tensor_tensor(t5[:, :, part, half, :], s5[:, :, part, 1 - half, :],
                                            n5[:, part, half, :].unsqueeze(1).broadcast_to([P, heads, 8]), ALU.mult)
            return nc.vector.tensor_tensor(dst, src, cos, ALU.mult)

        def mla_heads(l, last):
            q_tiles = [2, 3] if last else [0, 1, 2, 3]
            n0 = first["bh", l]
            wq = slot_view(n0, 3, H * QK)
            wkv = slot_view(n0 + 1, 2, H * (NOPE + DH))
            head = region(10752, 2, H, QK)
            sq, tmp = region(YB, H, QK), region(YB + 768, H, ROPE)
            norm_w = region(YB + 1024, 2, QK)
            st = region(YB + 1216, 4, H)
            jobs = [("q", t) for t in q_tiles] + [("k", t) for t in range(NT)]
            with stage() as block:
                @block.sync
                def _(sp):
                    run_ahead(sp, ("bh", l), ("rqk", l))

                @block.gpsimd
                def _(pool):
                    for i, x in enumerate(("q_norm_w", "k_norm_w")):
                        pool.dma_start(norm_w[:, i, :], a[x][l].partition_broadcast(P)) \
                            .then_inc(*S.small_loaded.inc(16))

                @block.tensor
                def _(pe):
                    def product(i):
                        kind, t = jobs[i]
                        if i == 0:
                            arrived(pe, n0)
                        if i == len(q_tiles):
                            arrived(pe, n0 + 1)
                        if i >= 2:
                            pe.wait_ge(*S.num_read.reach(i - 1))
                        src, w, ks, cols = (qlT, wq, 3, 384) if kind == "q" else (kvT, wkv, 2, 512)
                        for c in range(2):
                            for k in range(ks):
                                ins = nc.tensor.matmul(bank[2 * (i % 2) + c][:, 0:cols], src[:, k, t * P:(t + 1) * P],
                                                       w[:, k, c * cols:(c + 1) * cols], start=(k == 0),
                                                       stop=(k == ks - 1))
                        if i + 1 in (len(q_tiles), len(jobs)):
                            ins.then_inc(*S.weights_used.inc())
                        else:
                            ins.then_inc(*S.pe.inc())

                    product(0)
                    for i, (kind, t) in enumerate(jobs):
                        if i + 1 < len(jobs):
                            product(i + 1)
                        pe.wait_ge(*S.dve.reach(i + 1))
                        for h in range(H):
                            if h % 4 == 0 and i:
                                pe.wait_ge(*S.act.reach(2 * i - 1 + h // 4))
                            ins = nc.tensor.transpose(bank[4 + h // 4][0:QK, (h % 4) * P:(h % 4 + 1) * P],
                                                      head[:, i % 2, h, :], ident)
                            if h % 4 == 3:
                                ins.then_inc(*S.pv_done.inc())

                @block.scalar
                def _(act):
                    for i, (kind, t) in enumerate(jobs):
                        act.wait_ge(*S.p_ready.reach(i + 1))
                        nc.scalar.activation(st[:, 1, :], st[:, 0, :], ACT.Sqrt, scale=1.0 / QK, bias=eps[:, 0:1]) \
                            .then_inc(*S.exp_ready.inc())
                        dst = qT if kind == "q" else kT
                        for c in range(2):
                            act.wait_ge(*S.pv_done.reach(2 * i + c + 1))
                            nc.scalar.copy(dst[0:QK, 4 * c:4 * c + 4, t * P:(t + 1) * P],
                                           bank[4 + c][0:QK, :].rearrange("p (h t) -> p h t", h=4)) \
                                .then_inc(*S.act.inc())

                @block.vector
                def _(dve):
                    dve.wait_ge(*S.small_loaded.reach(32))
                    for i, (kind, t) in enumerate(jobs):
                        if i + 1 in (len(q_tiles), len(jobs)):
                            dve.wait_ge(S.weights_used.sem, n0 + (1 if i < len(q_tiles) else 2))
                        else:
                            dve.wait_ge(*S.pe.reach(i + 1 - (i >= len(q_tiles))))
                        if i >= 2:
                            dve.wait_ge(*S.pv_done.reach(2 * i - 2))
                        x = head[:, i % 2, :, :]
                        for c in range(2):
                            b = bank[2 * (i % 2) + c]
                            hs = slice(4 * c, 4 * c + 4)
                            if kind == "q":
                                ins = nc.vector.tensor_copy(x[:, hs, :], b[:, 0:384].rearrange("p (h d) -> p h d", h=4))
                            else:
                                b4 = b[:, :].rearrange("p (h d) -> p h d", h=4)
                                nc.vector.tensor_copy(x[:, hs, 0:NOPE], b4[:, :, 0:NOPE])
                                nc.vector.tensor_copy(v_mla[:, t, hs, :], b4[:, :, NOPE:])
                                ins = nc.vector.tensor_copy(x[:, hs, NOPE:],
                                                            k_rope[:, t, :].unsqueeze(1).broadcast_to([P, 4, ROPE]))
                        ins.then_inc(*S.num_read.inc())
                        dve.wait_ge(*S.num_read.latest())
                        link(dve, S.dve_step, nc.vector.tensor_tensor(sq, x, x, ALU.mult))
                        nc.vector.reduce_sum(st[:, 0, :], sq, axis=AX.X).then_inc(*S.p_ready.inc())
                        dve.wait_ge(*S.exp_ready.reach(i + 1))
                        link(dve, S.dve_step, nc.vector.reciprocal(st[:, 2, :], st[:, 1, :]))
                        link(dve, S.dve_step, nc.vector.tensor_tensor(
                            sq, x, st[:, 2, :].unsqueeze(2).broadcast_to([P, H, QK]), ALU.mult))
                        w = norm_w[:, 0 if kind == "q" else 1, :].unsqueeze(1).broadcast_to([P, H, QK])
                        if t < 2:
                            nc.vector.tensor_tensor(x, sq, w, ALU.mult).then_inc(*S.dve.inc())
                        else:
                            link(dve, S.dve_step, nc.vector.tensor_tensor(sq, sq, w, ALU.mult))
                            nc.vector.tensor_copy(x[:, :, 0:NOPE], sq[:, :, 0:NOPE])
                            link(dve, S.dve_step, rope_halves(sq[:, :, NOPE:], x[:, :, NOPE:], tmp, rope[:, t - 2], H))
                            nc.vector.tensor_tensor(x[:, :, NOPE:], x[:, :, NOPE:], tmp, ALU.add) \
                                .then_inc(*S.dve.inc())

        def mla_attention(l, last):
            q_tiles = [2, 3] if last else [0, 1, 2, 3]
            probs, pT = region(8192, 2, T), region(9216, 2, T)
            y = region(10240, NT, W)
            st = region(12416, 2, 4)
            jobs = [(t, h) for t in q_tiles for h in range(H)]
            scale = QK ** -0.5

            def keys(t):
                return CT if t < 2 else T

            with stage() as block:
                @block.tensor
                def _(pe):
                    def score(i):
                        t, h = jobs[i]
                        if i >= 2:
                            pe.wait_ge(*S.exp_ready.reach(i - 1))
                        nc.tensor.matmul(bank[i % 2][:, 0:keys(t)], qT[0:QK, h, t * P:(t + 1) * P],
                                         kT[0:QK, h, 0:keys(t)], start=True, stop=True).then_inc(*S.scores_ready.inc())

                    def values(i):
                        t, h = jobs[i]
                        pe.wait_ge(*S.pT_ready.reach(i + 1))
                        if i >= 2:
                            pe.wait_ge(*S.num_read.reach(i - 1))
                        nk = keys(t) // P
                        for s in range(nk):
                            ins = nc.tensor.matmul(bank[4 + i % 2][:, 0:DH], pT[:, i % 2, s * P:(s + 1) * P],
                                                   v_mla[:, s, h, :], start=(s == 0), stop=(s == nk - 1))
                        ins.then_inc(*S.pv_done.inc())

                    score(0)
                    for i, (t, h) in enumerate(jobs):
                        if i + 1 < len(jobs):
                            score(i + 1)
                        pe.wait_ge(*S.exp_ready.reach(i + 1))
                        if i >= 2:
                            pe.wait_ge(*S.pT_ready.reach(i - 1))
                        for s in range(keys(t) // P):
                            ins = nc.tensor.transpose(bank[2 + i % 2][:, s * P:(s + 1) * P],
                                                      probs[:, i % 2, s * P:(s + 1) * P], ident)
                        ins.then_inc(*S.pT_done.inc())
                        if i:
                            values(i - 1)
                    values(len(jobs) - 1)
                    pe.wait_ge(*S.num_read.reach(len(jobs)))
                    for j, t in enumerate(q_tiles):
                        for f in range(4):
                            ins = nc.tensor.transpose(bank[j][:, f * P:(f + 1) * P], y[:, t, f * P:(f + 1) * P], ident)
                        ins.then_inc(*S.pe.inc())

                @block.vector
                def _(dve):
                    def sums_out(i):
                        t, h = jobs[i]
                        dve.wait_ge(*S.pv_done.reach(i + 1))
                        link(dve, S.dve_step, nc.vector.reciprocal(st[:, i % 2, 3:4], st[:, i % 2, 2:3]))
                        nc.vector.tensor_scalar(y[:, t, h * DH:(h + 1) * DH], bank[4 + i % 2][:, 0:DH],
                                                st[:, i % 2, 3:4], None, ALU.mult).then_inc(*S.num_read.inc())

                    for i, (t, h) in enumerate(jobs):
                        dve.wait_ge(*S.scores_ready.reach(i + 1))
                        if i >= 2:
                            sums_out(i - 2)
                        link(dve, S.dve_step, nc.vector.reduce_max(st[:, i % 2, 0:1], bank[i % 2][:, 0:keys(t)],
                                                                   axis=AX.X))
                        nc.vector.tensor_scalar(st[:, i % 2, 1:2], st[:, i % 2, 0:1], -scale, None, ALU.mult) \
                            .then_inc(*S.max_ready.inc())
                        if i:
                            dve.wait_ge(*S.pT_done.reach(i))
                            tp = keys(jobs[i - 1][0])
                            nc.vector.tensor_copy(pT[:, (i - 1) % 2, 0:tp], bank[2 + (i - 1) % 2][:, 0:tp]) \
                                .then_inc(*S.pT_ready.inc())
                    i = len(jobs)
                    sums_out(i - 2)
                    dve.wait_ge(*S.pT_done.reach(i))
                    nc.vector.tensor_copy(pT[:, (i - 1) % 2, :], bank[2 + (i - 1) % 2][:, :]).then_inc(*S.pT_ready.inc())
                    sums_out(i - 1)
                    for j, t in enumerate(q_tiles):
                        dve.wait_ge(*S.pe.reach(j + 1))
                        nc.vector.tensor_copy(yT[:, 4:8, t * P:(t + 1) * P],
                                              bank[j][:, :].rearrange("p (f t) -> p f t", f=4))

                @block.scalar
                def _(act):
                    for i, (t, h) in enumerate(jobs):
                        act.wait_ge(*S.max_ready.reach(i + 1))
                        if i >= 2:
                            act.wait_ge(*S.pT_done.reach(i - 1))
                        nc.scalar.activation(probs[:, i % 2, 0:keys(t)], bank[i % 2][:, 0:keys(t)], ACT.Exp,
                                             bias=st[:, i % 2, 1:2], scale=scale, accum_out=st[:, i % 2, 2:3]) \
                            .then_inc(*S.exp_ready.inc())

        rqk, rT = region(0, NT, W), region(2048, 4, T)
        h_ret = region(0, NT, H, DH)
        v_ret, s_gate = region(4096, NT, H, DH), region(6144, NT, W)
        bias_c, decay = region(8192, 1536), region(8192, 2, 2, 3 * P)
        ret_ring = region(9728, 4, T)

        def project_c(l, last):
            q_tiles = [2, 3] if last else [0, 1, 2, 3]
            n_qk, n_v, n_g = (first[key, l] for key in ("rqk", "rv", "rg"))
            jobs = [(n_qk, 512, range(NT), 0, lambda t: rqk[:, t, :]),
                    (n_v, 512, range(NT), 512, lambda t: v_ret[:, t]),
                    (n_g, 512, q_tiles, 1024, lambda t: s_gate[:, t, :])]
            rounds = [Modulation(1, r, r, 11776, bank[2], bank[3]) for r in range(3)] if l == 0 else []
            vectors = Vectors(1, 12288)
            with stage() as block:
                @block.sync
                def _(sp):
                    run_ahead(sp, ("rqk", l), ("merge", l))

                @block.gpsimd
                def _(pool):
                    load_bias(pool, l, bias_c, C_RQ, 1536)
                    if rounds:
                        vectors.load(pool)

                @block.tensor
                def _(pe):
                    for i, job in enumerate(jobs):
                        token_major(pe, [job], 2, i * NT)
                        if rounds:
                            if i == 0:
                                pe.wait_ge(*S.small_loaded.reach(16 * 12))
                                vectors.turn(pe, bank[4])
                            else:
                                rounds[i - 1].turn(pe)
                            rounds[i].product(pe)
                    if rounds:
                        pe.wait_ge(*S.mod_added.reach(1))
                    for t in range(NT):
                        if t < 2:
                            pe.wait_ge(*S.dve.reach(t + 1))
                        else:
                            pe.wait_ge(*S.p_ready.reach(t - 1))
                        for f in range(4):
                            ins = nc.tensor.transpose(bank[4 + t][:, f * P:(f + 1) * P],
                                                      rqk[:, t, f * P:(f + 1) * P], ident)
                        ins.then_inc(*S.pv_done.inc())
                    if rounds:
                        rounds[2].turn(pe)

                @block.vector
                def _(dve):
                    def take_vectors(dve):
                        vectors.store(dve, bank[4])

                    dve.wait_ge(*S.small_loaded.reach(16 * (12 if rounds else 1)))
                    add_bias(dve, 2, jobs, bias_c, after={NT: take_vectors, 2 * NT - 1: rounds[0].add,
                                                          3 * NT - 1: rounds[1].add} if rounds else {})
                    for t in (2, 3):
                        x = rqk[:, t, :].rearrange("p (h d) -> p h d", d=RK)
                        swapped, turned = (ret_ring[:, r, :].rearrange("p (h d) -> p h d", d=RK) for r in (t, t - 2))
                        link(dve, S.dve_step, rope_halves(x, turned, swapped, rope[:, t - 2], 2 * H))
                        nc.vector.tensor_tensor(x, turned, swapped, ALU.add).then_inc(*S.p_ready.inc())
                    if rounds:
                        rounds[2].add(dve)

                @block.scalar
                def _(act):
                    for r in rounds[:2]:
                        r.copy_rows(act)
                    for i, t in enumerate(q_tiles):
                        act.wait_ge(*S.dve.reach(2 * NT + i + 1))
                        nc.scalar.activation(s_gate[:, t, :], s_gate[:, t, :], ACT.Silu)
                    for r in rounds[2:]:
                        r.copy_rows(act)
                    for t in range(NT):
                        act.wait_ge(*S.pv_done.reach(t + 1))
                        nc.scalar.copy(rT[:, :, t * P:(t + 1) * P],
                                       bank[4 + t][:, :].rearrange("p (f t) -> p f t", f=4))

        def retention(l, last):
            t0 = 2 if last else 0
            lo = t0 * P
            table_loaded = (S.even_table, S.odd_table)
            with stage() as block:
                @block.gpsimd
                def _(pool):
                    for h in range(H):
                        if h >= 2:
                            pool.wait_ge(*S.p_ready.reach(NT * (h - 1)))
                        pool.dma_start(decay[:, h % 2], a["decay"][h]).then_inc(*table_loaded[h % 2].inc(16))

                @block.tensor
                def _(pe):
                    def scores(h):
                        at = RK * (h % 4)
                        if h >= 2:
                            pe.wait_ge(*S.p_ready.reach(NT * (h - 1)))
                        b = 3 * (h % 2)
                        q, k = rT[at:at + RK, h // 4, :], rT[at:at + RK, 2 + h // 4, :]
                        for s in range(NT):
                            o = bank[b + s][:, lo:] if s < 2 else bank[b + 2][:, (s - 2) * CT:(s - 1) * CT]
                            ins = nc.tensor.matmul(o, k[:, s * P:(s + 1) * P], q[:, (lo if s < 2 else CT):],
                                                   start=True, stop=True)
                        ins.then_inc(*S.scores_ready.inc())

                    scores(0)
                    for h in range(H):
                        if h + 1 < H:
                            scores(h + 1)
                        if h >= 2:
                            pe.wait_ge(*S.num_read.reach(h - 1))
                        for s in range(NT):
                            pe.wait_ge(*S.p_ready.reach(NT * h + s + 1))
                            tiles = range(t0 if s < 2 else 2, NT)
                            for t in tiles:
                                ins = nc.tensor.matmul(bank[6 + h % 2][:, t * DH:(t + 1) * DH],
                                                       ret_ring[:, s, t * P:(t + 1) * P], v_ret[:, s, h, :],
                                                       start=(s == 0 and t == t0), stop=(s == NT - 1 and t == NT - 1),
                                                       skip_group_check=True)
                            ins.then_inc(*S.pv_done.inc())

                @block.vector
                def _(dve):
                    for h in range(H):
                        dve.wait_ge(*S.scores_ready.reach(h + 1))
                        dve.wait_ge(*table_loaded[h % 2].reach(16 * (h // 2 + 1)))
                        b = 3 * (h % 2)
                        for s in range(NT):
                            if h:
                                dve.wait_ge(*S.pv_done.reach(NT * (h - 1) + s + 1))
                            off = P if s % 2 == 0 else 0
                            if s < 2:
                                part = slice(1 if last else 0, 2)
                                o = ret_ring[:, s, lo:].rearrange("p (a t) -> p a t", t=CT)
                                x = bank[b + s][:, lo:].rearrange("p (a t) -> p a t", t=CT)
                                tab = decay[:, h % 2, part, off:off + CT]
                            else:
                                o, x = ret_ring[:, s, CT:], bank[b + 2][:, (s - 2) * CT:(s - 1) * CT]
                                tab = decay[:, h % 2, 0, off:off + CT]
                            nc.vector.tensor_tensor(o, x, tab, ALU.mult).then_inc(*S.p_ready.inc())

                @block.scalar
                def _(act):
                    for h in range(H):
                        act.wait_ge(*S.pv_done.reach(NT * (h + 1)))
                        nc.scalar.copy(h_ret[:, t0:, h, :],
                                       bank[6 + h % 2][:, t0 * DH:NT * DH].rearrange("p (t d) -> p t d", d=DH)) \
                            .then_inc(*S.num_read.inc())

        def merge_branches(l, last):
            lo = CT if last else 0
            merged, sig, tmp = region(2048, KD, T), region(8192, 2, T), region(9728, 2, T)
            norm = HeadNorm(l, last, h_ret, s_gate, ret_ring, 8, "retn")
            n0 = first["merge", l]
            jobs = [(n, c, d) for n in range(3) for c in range(2) for d in range(4)]
            m0 = first["out", l]
            with stage() as block:
                @block.sync
                def _(sp):
                    run_ahead(sp, ("merge", l), ("moe", l))

                @block.tensor
                def _(pe):
                    for i, (n, c, d) in enumerate(jobs):
                        at = n0 + 2 * (2 * n + c)
                        cols = slice(d * P, (d + 1) * P)
                        if d == 0:
                            arrived(pe, at)
                            arrived(pe, at + 1)
                        if i >= 2:
                            pe.wait_ge(*S.act.reach(i - 1))
                        for k in range(KD):
                            ins = nc.tensor.matmul(bank[i % 2][:, lo:], slot_view(at, KD, 512)[:, k, cols], hT[:, k, lo:],
                                                   start=(k == 0), stop=(k == KD - 1))
                        ins.then_inc(*S.pe.inc())
                        if i >= 2:
                            pe.wait_ge(*S.dve.reach(i - 1))
                        for k in range(4):
                            ins = nc.tensor.matmul(bank[2 + i % 2][:, lo:], slot_view(at + 1, 4, 512)[:, k, cols],
                                                   yT[:, 4 * n + k, lo:], start=(k == 0), stop=(k == 3))
                        if d < 3:
                            ins.then_inc(*S.pv_done.inc())
                        else:
                            ins.then_inc(*S.weights_used.inc(2))
                        if i == 3:
                            norm.turn(pe)
                    pe.wait_ge(*S.dve.reach(len(jobs)))
                    for d in range(KD):
                        if d % 4 == 0:
                            arrived(pe, m0 + d // 4)
                        if d >= 4:
                            pe.wait_ge(*S.x_added.reach(d - 3))
                        for k in range(KD):
                            ins = nc.tensor.matmul(bank[4 + d % 4][:, lo:],
                                                   slot_view(m0 + d // 4, KD, 512)[:, k, (d % 4) * P:(d % 4 + 1) * P],
                                                   merged[:, k, lo:], start=(k == 0), stop=(k == KD - 1))
                        if d % 4 < 3:
                            ins.then_inc(*S.pT_done.inc())
                        else:
                            ins.then_inc(*S.weights_used.inc())

                @block.scalar
                def _(act):
                    norm.square(act)
                    for i, (n, c, d) in enumerate(jobs):
                        if i == 2:
                            norm.root(act)
                        f = VA["blog"] + n * KD + c * 4 + d
                        act.wait_ge(*S.pe.reach(i + 1))
                        if i >= 2:
                            act.wait_ge(*S.dve.reach(i - 1))
                        nc.scalar.activation(sig[:, i % 2, lo:], bank[i % 2][:, lo:], ACT.Sigmoid,
                                             bias=vA[:, l, f:f + 1]).then_inc(*S.act.inc())

                @block.vector
                def _(dve):
                    norm.centre(dve)
                    for i, (n, c, d) in enumerate(jobs):
                        if i in (1, 3, 5):
                            (norm.variance, norm.scale_and_gate, norm.store)[i // 2](dve)
                        m = merged[:, 4 * c + d, lo:]
                        dve.wait_ge(*S.act.reach(i + 1))
                        if d < 3:
                            dve.wait_ge(*S.pv_done.reach(i - i // 4 + 1))
                        else:
                            dve.wait_ge(S.weights_used.sem, n0 + 2 * (i // 4 + 1))
                        if n == 0:
                            nc.vector.tensor_tensor(m, sig[:, i % 2, lo:], bank[2 + i % 2][:, lo:], ALU.mult) \
                                .then_inc(*S.dve.inc())
                        else:
                            link(dve, S.dve_step, nc.vector.tensor_tensor(tmp[:, i % 2, lo:], sig[:, i % 2, lo:],
                                                                          bank[2 + i % 2][:, lo:], ALU.mult))
                            nc.vector.tensor_tensor(m, m, tmp[:, i % 2, lo:], ALU.add).then_inc(*S.dve.inc())
                    for d in range(KD):
                        if d % 4 < 3:
                            dve.wait_ge(*S.pT_done.reach(d - d // 4 + 1))
                        else:
                            dve.wait_ge(S.weights_used.sem, m0 + d // 4 + 1)
                        for s in range(lo // CT, 2):
                            sl = slice(s * CT, (s + 1) * CT)
                            ins = nc.vector.scalar_tensor_tensor(xT[:, d, sl], bank[4 + d % 4][:, sl],
                                                                 mod[:, l, 2 * KD + d, s:s + 1], xT[:, d, sl],
                                                                 ALU.mult, ALU.add)
                        ins.then_inc(*S.x_added.inc())

        SCATTER = (0, 4, 1, 5, 2, 6, 3, 7)
        OUT_BANKS = (0, 6, 7)
        h_tok = region(0, NT, D)
        select = region(4096, NT, E + 1, CAP)
        weight = region(6272, NT, E + 1)
        xs_all = region(10240, KD, E, 64)
        placed = region(0, 2, NT, P)
        selT = region(1024, 2, T)
        gate_s, hid = work[0:64, 2048:3072], work[0:64, 3072:4096]
        hidT = region(6400, 2, KD, 64)
        ys = region(7424, 2, 512)
        xs = region(8448, 2, KD, 64)

        def route(l, last):
            tiles = [2, 3] if last else [0, 1, 2, 3]
            t0, s0 = tiles[0], tiles[0] // 2
            nt = len(tiles)
            rows = [work[0:E, x:x + T] for x in (6400, 6912, 7424, 7936)]
            aff, rest, mask, pos = rows
            one_row = work[0:E, 8448:8448 + CT]
            posT = region(8960, NT, E)
            best = work[0:E, 9024:9032]
            router = region(9104, KD, E)
            top, tot, ex = region(9300, NT), region(9304, NT), region(9308, NT, E)
            gathers = [(d, s) for d in range(KD) for s in range(s0, 2)]

            def gathered_out(i):
                d, s = gathers[i]
                return (bank[2 + i % 4][:, :].rearrange("p (e c) -> p e c", c=CAP),
                        xs_all[:, d, :, CAP * (s - s0):CAP * (s - s0) + CAP])
            with stage() as block:
                @block.gpsimd
                def _(pool):
                    pool.dma_start(router, a["router_w"][l].rearrange("(k p) e -> p k e", p=P)) \
                        .then_inc(*S.small_loaded.inc(16))
                    nc.gpsimd.memset(one_row, 1.0).then_inc(*S.pool.inc())
                    nc.gpsimd.memset(select[:, :, :, :], 0.0).then_inc(*S.pool.inc())
                    nc.gpsimd.memset(weight[:, :, :], 0.0).then_inc(*S.pool.inc())

                @block.tensor
                def _(pe):
                    pe.wait_ge(*S.small_loaded.reach(16))
                    for i, t in enumerate(tiles):
                        for k in range(KD):
                            ins = nc.tensor.matmul(bank[0][:, t * E:(t + 1) * E], hT[:, k, t * P:(t + 1) * P],
                                                   router[:, k, :], start=(k == 0), stop=(k == KD - 1))
                    ins.then_inc(*S.pe.inc())
                    for i, t in enumerate(tiles):
                        for c in range(2):
                            b = 2 + (2 * i + c) % 4
                            if 2 * i + c >= 4:
                                pe.wait_ge(*S.act.reach(2 * i + c - 3))
                            for j in range(4):
                                ins = nc.tensor.transpose(bank[b][:, j * P:(j + 1) * P],
                                                          hT[:, 4 * c + j, t * P:(t + 1) * P], ident)
                            ins.then_inc(*S.pv_done.inc())
                    pe.wait_ge(*S.dve.reach(2))
                    for t in tiles:
                        ins = nc.tensor.transpose(bank[6][0:E, t * P:(t + 1) * P], weight[:, t, 0:E], ident)
                    ins.then_inc(*S.pe.inc())
                    pe.wait_ge(*S.dve.reach(3))
                    for t in tiles:
                        ins = nc.tensor.transpose(bank[7][:, t * E:(t + 1) * E], pos[:, t * P:(t + 1) * P],
                                                  ident[0:E, 0:E])
                    ins.then_inc(*S.pe.inc())
                    for i, (d, s) in enumerate(gathers):
                        if i < 2:
                            pe.wait_ge(*S.dve.reach(4))
                            pe.wait_ge(*S.act.reach(2 * nt))
                        if i >= 4:
                            pe.wait_ge(*(S.xs_ready if i % 2 else S.x_added).reach(i // 2 - 1))
                        for t in (0, 1):
                            ins = nc.tensor.matmul(bank[2 + i % 4][:, :], h_tok[:, 2 * s + t, d * P:(d + 1) * P],
                                                   select[:, 2 * s + t, 0:E, :].rearrange("p e c -> p (e c)"),
                                                   start=(t == 0), stop=(t == 1))
                        ins.then_inc(*S.gathered.inc())

                @block.scalar
                def _(act):
                    for i in range(2 * nt):
                        if i == 2 * nt - 1:
                            act.wait_ge(*S.dve.reach(1))
                            nc.scalar.activation(ex[:, t0:, :], ex[:, t0:, :], ACT.Exp).then_inc(*S.exp_ready.inc())
                        t, c = tiles[i // 2], i % 2
                        act.wait_ge(*S.pv_done.reach(i + 1))
                        nc.scalar.copy(h_tok[:, t, c * 512:(c + 1) * 512], bank[2 + i % 4][:, :]).then_inc(*S.act.inc())
                    for i in range(1, len(gathers), 2):
                        src, dst = gathered_out(i)
                        act.wait_ge(*S.gathered.reach(i + 1))
                        nc.scalar.copy(dst, src).then_inc(*S.xs_ready.inc())

                @block.vector
                def _(dve):
                    dve.wait_ge(*S.pe.reach(1))
                    lg = bank[0][:, t0 * E:NT * E].rearrange("p (t e) -> p t e", e=E)
                    link(dve, S.dve_step, nc.vector.reduce_max(top[:, t0:], lg, axis=AX.X))
                    nc.vector.tensor_tensor(ex[:, t0:, :], lg, top[:, t0:].unsqueeze(2).broadcast_to([P, nt, E]),
                                            ALU.subtract).then_inc(*S.dve.inc())
                    dve.wait_ge(*S.exp_ready.reach(1))
                    link(dve, S.dve_step, nc.vector.reduce_sum(tot[:, t0:], ex[:, t0:, :], axis=AX.X))
                    link(dve, S.dve_step, nc.vector.reciprocal(tot[:, t0:], tot[:, t0:]))
                    dve.wait_ge(*S.pool.reach(3))
                    nc.vector.tensor_tensor(weight[:, t0:, 0:E], ex[:, t0:, :],
                                            tot[:, t0:].unsqueeze(2).broadcast_to([P, nt, E]),
                                            ALU.mult).then_inc(*S.dve.inc())
                    dve.wait_ge(*S.pe.reach(2))
                    lo = t0 * P
                    nc.vector.tensor_copy(aff[:, lo:], bank[6][0:E, lo:])
                    link(dve, S.dve_step, nc.vector.tensor_copy(rest[:, lo:], bank[6][0:E, lo:]))
                    for s in range(s0, 2):
                        r = rest[:, s * CT:(s + 1) * CT]
                        for _ in range(CAP // 8):
                            link(dve, S.dve_step, nc.vector.max(best, r))
                            link(dve, S.dve_step, nc.vector.match_replace(r, best, r, -1.0))
                    link(dve, S.dve_step, nc.vector.tensor_scalar(mask[:, lo:], rest[:, lo:], 0.0, None, ALU.is_lt))
                    for s in range(s0, 2):
                        sl = slice(s * CT, (s + 1) * CT)
                        ins = nc.vector.tensor_tensor_scan(pos[:, sl], one_row, mask[:, sl], 0.0, ALU.mult, ALU.add)
                    link(dve, S.dve_step, ins)
                    nc.vector.tensor_tensor(pos[:, lo:], pos[:, lo:], mask[:, lo:], ALU.mult).then_inc(*S.dve.inc())
                    dve.wait_ge(*S.pe.reach(3))
                    link(dve, S.dve_step, nc.vector.tensor_copy(
                        posT[:, t0:, :], bank[7][:, t0 * E:NT * E].rearrange("p (t e) -> p t e", e=E)))
                    for t in tiles:
                        ins = nc.vector.tensor_tensor(select[:, t, 0:E, :],
                                                      posT[:, t, :].unsqueeze(2).broadcast_to([P, E, CAP]),
                                                      slot_no[:, :].unsqueeze(1).broadcast_to([P, E, CAP]),
                                                      ALU.is_equal)
                    ins.then_inc(*S.dve.inc())
                    for i in range(0, len(gathers), 2):
                        src, dst = gathered_out(i)
                        dve.wait_ge(*S.gathered.reach(i + 1))
                        nc.vector.tensor_copy(dst, src).then_inc(*S.x_added.inc())

        def experts(l, last):
            tiles = [2, 3] if last else [0, 1, 2, 3]
            t0, s0 = tiles[0], tiles[0] // 2
            ns, nt, lo = 2 - s0, len(tiles), t0 * P
            M = CAP * ns
            n0 = first["moe", l]

            def weights_at(j, k4, cols):
                return slot_view(n0 + j, k4, cols)

            with stage() as block:
                @block.sync
                def _(sp):
                    with sp.Fori(0, E - 1) as e:
                        for j in range(6):
                            sp.wait_ge(S.weights_used.sem, n0 + 6 * e + j + 1)
                            src = a[("exp_w1", "exp_w3", "exp_w1", "exp_w3", "exp_w2", "exp_w2")[j]][l]
                            k4 = (0, 0, 1, 1, 0, 1)[j]
                            sp.dma_start(weights_at(j, 4, 1024),
                                         src[bass.ds(e + 1, 1), k4 * 512:(k4 + 1) * 512, :]
                                         .rearrange("e (k p) n -> p (e k) n", p=P)) \
                                .then_inc(slot_loaded[(n0 + j) % SLOTS], 16)
                    for n in range(n0 + 6 * E, n0 + 6 * E + SLOTS):
                        load(sp, n)

                @block.gpsimd
                def _(pool):
                    def stage_in(e, b):
                        for half in range(2):
                            for s in range(s0, 2):
                                at = 64 * half + CAP * (s - s0)
                                ins = nc.gpsimd.tensor_tensor(
                                    placed[:, b, 2 * s:2 * s + 2, at:at + CAP],
                                    select[:, 2 * s:2 * s + 2, bass.ds(e, 1), :].rearrange("p t e c -> p t (e c)"),
                                    weight[:, 2 * s:2 * s + 2, bass.ds(e, 1)].broadcast_to([P, 2, CAP]), ALU.mult)
                        return ins

                    def tokens_in(e, b):
                        nc.gpsimd.tensor_copy(xs[:, b, :, 0:M],
                                              xs_all[:, :, bass.ds(e, 1), 0:M].rearrange("p k e c -> p k (e c)"))

                    nc.gpsimd.memset(placed[:, :, :, :], 0.0).then_inc(*S.pool.inc())
                    pool.wait_ge(*S.pool.latest())
                    for e in range(2):
                        tokens_in(e, e)
                        stage_in(e, e).then_inc(S.sel_ready.sem, 1)
                    with pool.Fori(0, E // 2 - 1) as i:
                        for j in range(2):
                            pool.wait_ge(S.selT_done.sem, S.selT_done.base + 2 * i + j + 2)
                            tokens_in(2 * i + 2 + j, j)
                            stage_in(2 * i + 2 + j, j).then_inc(S.sel_ready.sem, 1)
                    pool.wait_ge(*S.selT_done.reach(E))
                    stage_in(E, 0).then_inc(S.sel_ready.sem, 1)

                @block.tensor
                def _(pe):
                    def turn_selection(b):
                        for t in tiles:
                            ins = nc.tensor.transpose(bank[1][:, t * P:(t + 1) * P], placed[:, b, t, :], ident)
                        ins.then_inc(S.selT_done.sem, 1)

                    def scatter(e, b):
                        pe.wait_ge(S.ys_ready.sem, S.ys_ready.base + e + 2)
                        for i, d in enumerate(SCATTER):
                            half = 64 * (d // 4)
                            pe.wait_ge(S.x_added.sem, S.x_added.base + 8 * e + 9 + max(i - 2, 0))
                            nc.tensor.matmul(bank[OUT_BANKS[i % 3]][:, lo:], ys[half:half + M, b, (d % 4) * P:(d % 4 + 1) * P],
                                             selT[half:half + M, b, lo:], start=True, stop=True) \
                                .then_inc(S.scattered.sem, 1)

                    pe.wait_ge(*S.sel_ready.reach(1))
                    turn_selection(0)
                    with pe.Fori(0, E // 2) as i:
                        for b in range(2):
                            e = 2 * i + b
                            pe.wait_ge(S.sel_ready.sem, S.sel_ready.base + e + 1)
                            pe.wait_ge(S.hid_ready.sem, S.hid_ready.base + 2 * e + 2)
                            for kh in range(2):
                                for j in (2 * kh, 2 * kh + 1):
                                    pe.wait_ge(slot_loaded[(n0 + j) % SLOTS], 16 * ((n0 + j) // SLOTS + 1) + 16 * e)
                                w1, w3 = weights_at(2 * kh, 4, 1024), weights_at(2 * kh + 1, 4, 1024)
                                for c in range(2):
                                    for k in range(4):
                                        st, en = kh == 0 and k == 0, kh == 1 and k == 3
                                        x = xs[:, b, 4 * kh + k, 0:M]
                                        nc.tensor.matmul(bank[2 + c][0:M, :], x, w1[:, k, c * 512:(c + 1) * 512],
                                                         start=st, stop=en)
                                        ins = nc.tensor.matmul(bank[2 + c][64:64 + M, :], x,
                                                               w3[:, k, c * 512:(c + 1) * 512], start=st, stop=en)
                                    if kh == 1 and c == 0:
                                        ins.then_inc(S.w13_done.sem, 1)
                                ins.then_inc(S.weights_used.sem, 2)
                            scatter(e - 1, 1 - b)
                            pe.wait_ge(S.sel_ready.sem, S.sel_ready.base + e + 2)
                            pe.wait_ge(S.hid_ready.sem, S.hid_ready.base + 2 * e + 4)
                            pe.wait_ge(S.hidT_ready.sem, S.hidT_ready.base + e + 1)
                            turn_selection(1 - b)
                            for k in range(KD):
                                ins = nc.tensor.transpose(bank[4][:, k * 64:k * 64 + M], hid[0:M, k * P:(k + 1) * P],
                                                          ident[0:M, 0:M])
                            ins.then_inc(S.hidT_done.sem, 1)
                            pe.wait_ge(S.hidT_ready.sem, S.hidT_ready.base + e + 2)
                            for kh in range(2):
                                j = 4 + kh
                                pe.wait_ge(slot_loaded[(n0 + j) % SLOTS], 16 * ((n0 + j) // SLOTS + 1) + 16 * e)
                                w2 = weights_at(j, 4, 1024)
                                for k in range(4):
                                    for c in range(2):
                                        ins = nc.tensor.matmul(bank[5][64 * c:64 * c + M, :], hidT[:, b, 4 * kh + k, 0:M],
                                                               w2[:, k, c * 512:(c + 1) * 512],
                                                               start=(kh == 0 and k == 0), stop=(kh == 1 and k == 3))
                                ins.then_inc(S.weights_used.sem, 1)
                    scatter(E - 1, 1)

                @block.scalar
                def _(act):
                    with act.Fori(0, E // 2) as i:
                        for b in range(2):
                            e = 2 * i + b
                            for c in range(2):
                                if c == 0:
                                    act.wait_ge(S.w13_done.sem, S.w13_done.base + e + 1)
                                else:
                                    act.wait_ge(S.weights_used.sem, n0 + 6 * e + 4)
                                nc.scalar.activation(gate_s[0:M, c * 512:(c + 1) * 512], bank[2 + c][0:M, :], ACT.Silu) \
                                    .then_inc(S.silu_done.sem, 1)
                            act.wait_ge(S.hidT_done.sem, S.hidT_done.base + e + 2)
                            nc.scalar.copy(hidT[:, b, :, 0:M], bank[4][:, :].rearrange("p (k c) -> p k c", c=64)[:, :, 0:M]) \
                                .then_inc(S.hidT_ready.sem, 1)
                            act.wait_ge(S.weights_used.sem, n0 + 6 * e + 6)
                            for half in (0, 64):
                                ins = nc.scalar.copy(ys[half:half + M, b, :], bank[5][half:half + M, :])
                            ins.then_inc(S.ys_ready.sem, 1)

                @block.vector
                def _(dve):
                    def add_to_x(e):
                        for i, d in enumerate(SCATTER):
                            dve.wait_ge(S.scattered.sem, S.scattered.base + 8 * e + 9 + i)
                            for s in range(s0, 2):
                                sl = slice(s * CT, (s + 1) * CT)
                                ins = nc.vector.scalar_tensor_tensor(xT[:, d, sl], bank[OUT_BANKS[i % 3]][:, sl],
                                                                     mod[:, l, 5 * KD + d, s:s + 1], xT[:, d, sl],
                                                                     ALU.mult, ALU.add)
                            ins.then_inc(S.x_added.sem, 1)

                    def selT_copy(e, b):
                        dve.wait_ge(S.selT_done.sem, S.selT_done.base + e + 1)
                        nc.vector.tensor_copy(selT[:, b, lo:], bank[1][:, lo:])

                    nc.vector.memset(ys[:, 1, :], 0.0)
                    nc.vector.memset(selT[:, 1, :], 0.0).then_inc(S.ys_ready.sem, 1)
                    nc.vector.engine_nop().then_inc(S.x_added.sem, 1)
                    nc.vector.engine_nop().then_inc(S.hid_ready.sem, 2)
                    nc.vector.engine_nop().then_inc(S.hidT_ready.sem, 1)
                    nc.vector.engine_nop().then_inc(S.hidT_done.sem, 1)
                    selT_copy(0, 0)
                    with dve.Fori(0, E // 2) as i:
                        for b in range(2):
                            e = 2 * i + b
                            dve.wait_ge(S.hidT_done.sem, S.hidT_done.base + e + 1)
                            for c in range(2):
                                cols = slice(c * 512, (c + 1) * 512)
                                dve.wait_ge(S.silu_done.sem, S.silu_done.base + 2 * e + c + 1)
                                nc.vector.tensor_tensor(hid[0:M, cols], bank[2 + c][64:64 + M, :], gate_s[0:M, cols],
                                                        ALU.mult).then_inc(S.hid_ready.sem, 1)
                            add_to_x(e - 1)
                            selT_copy(e + 1, 1 - b)
                    add_to_x(E - 1)
            S.sel_ready.total += E + 1
            S.selT_done.total += E + 1
            S.hid_ready.total += 2 * E + 2
            S.w13_done.total += E
            S.silu_done.total += 2 * E
            S.weights_used.total += 6 * E
            S.hidT_done.total += E + 1
            S.hidT_ready.total += E + 1
            S.ys_ready.total += E + 1
            S.scattered.total += 8 * (E + 1)
            S.x_added.total += 8 * (E + 1) + 1

        def store_latents():
            rows = region(0, 2, D)
            with stage() as block:
                @block.tensor
                def _(pe):
                    for i in range(4):
                        for j in range(4):
                            ins = nc.tensor.transpose(bank[i][:, j * P:(j + 1) * P],
                                                      xT[:, 4 * (i % 2) + j, CT + (i // 2) * P:CT + (i // 2 + 1) * P], ident)
                        ins.then_inc(*S.pe.inc())

                @block.vector
                def _(dve):
                    for i in range(4):
                        dve.wait_ge(*S.pe.reach(i + 1))
                        nc.vector.tensor_copy(rows[:, i // 2, (i % 2) * 512:(i % 2 + 1) * 512], bank[i][:, :]) \
                            .then_inc(*S.dve.inc())

                @block.sync
                def _(sp):
                    dst = out.rearrange("b (t p) d -> p (b t) d", p=P)
                    for t in range(2):
                        sp.wait_ge(*S.dve.reach(2 * t + 2))
                        sp.dma_start(dst[:, t, :], rows[:, t, :]).then_inc(*S.stored.inc(16))
                    sp.wait_ge(*S.stored.reach(32))

        for l in range(DEPTH):
            last = l == DEPTH - 1
            q0 = CT if last else 0
            normalise(l, 0, 0)
            project_a(l, last)
            mlstm(l, last)
            project_b(l, last)
            mla_heads(l, last)
            mla_attention(l, last)
            project_c(l, last)
            retention(l, last)
            merge_branches(l, last)
            normalise(l, 1, q0)
            route(l, last)
            experts(l, last)
        store_latents()


_INS = ["x", "c", "ctx", "c_ctx", "ada_w", "ada_b", "norm1_w", "norm2_w", "w_in", "b_in", "conv_w", "conv_b",
        "ml_norm_w", "mla_qa_norm", "mla_wq_b", "mla_kva_norm", "mla_wkv_b", "q_norm_w", "k_norm_w", "ret_norm_w",
        "w_branch", "w_out", "router_w", "exp_w1", "exp_w3", "exp_w2"]


def shape_constants(np):
    i = np.arange(P)
    f32 = np.float32
    before = (i[:, None] <= i[None, :]).astype(f32)
    after = (i[:, None] >= i[None, :]).astype(f32)
    eye = np.eye(P, dtype=f32)
    big = f32(-1e30)
    half = ROPE // 4
    inv = (f32(10000.0) ** (-np.arange(half, dtype=f32) / f32(half))).astype(f32)
    tok = np.arange(LT)
    angle = [(v.astype(f32)[:, None] * inv).astype(f32) for v in (tok // 64, tok % 64)]
    cos, sin = [np.cos(v).astype(f32) for v in angle], [np.sin(v).astype(f32) for v in angle]
    rope = np.stack([np.concatenate([cos[0], cos[0], cos[1], cos[1]], 1),
                     np.concatenate([-sin[0], sin[0], -sin[1], sin[1]], 1)], 1)
    rope = rope.reshape(2, P, 2, ROPE).transpose(1, 0, 2, 3)
    g = np.log1p(-np.exp2(-5.0 - np.arange(H)))
    dt = (np.arange(3 * P)[None, :] - P - i[:, None]).astype(np.float64)
    decay = np.zeros((H, P, 2, 3 * P))
    for h in range(H):
        gf, gb = g[h], g[H - 1 - h]
        decay[h, :, 0] = np.where(dt >= 0, np.exp(np.maximum(dt, 0) * gf), 0) + \
            np.where(dt <= 0, np.exp(np.maximum(-dt, 0) * gb), 0)
        decay[h, :, 1] = np.exp((CT + dt) * gf) + np.exp((CT - dt) * gb)
    return {
        "consts": np.concatenate([eye, np.ones((P, P), f32), before, after], 1),
        "masks": np.concatenate([eye, big * (1 - before), big * (1 - after)], 1),
        "rope": rope.astype(f32),
        "slot_no": np.tile(np.arange(1, CAP + 1, dtype=f32), (P, 1)),
        "decay": (decay * RK ** -0.5).astype(f32),
    }


def kernel(**inputs):
    import numpy as np
    import concourse.bacc as bacc
    from concourse.bass_utils import run_bass_kernel_spmd

    nc = bacc.Bacc("TRN2", target_bir_lowering=False, num_devices=1)
    arrays = {name: np.ascontiguousarray(inputs[name]) for name in _INS}
    arrays.update({k: np.ascontiguousarray(v) for k, v in shape_constants(np).items()})
    aps = {name: nc.dram_tensor(f"in_{name}", v.shape, mybir.dt.from_np(v.dtype), kind="ExternalInput").ap()
           for name, v in arrays.items()}
    out = nc.dram_tensor("out_latents", (1, LT, D), F32, kind="ExternalOutput").ap()
    build_program(nc, aps, out)
    r = run_bass_kernel_spmd(nc, [{f"in_{name}": v for name, v in arrays.items()}], core_ids=[0])
    return r.results[0]["out_latents"]
```

```python
import concourse.bass as bass
from concourse import mybir
from contextlib import ExitStack

F32 = mybir.dt.float32
BF16 = mybir.dt.bfloat16
ALU = mybir.AluOpType
ACT = mybir.ActivationFunctionType
AX = mybir.AxisListType

P = 128
D = 1024
KD = D // P
CT, LT = 256, 256
T = CT + LT
NT = T // P
DEPTH = 2
H = 8
W = 512
DH = 64
Q_LORA, KV_LORA, NOPE, ROPE, QK = 384, 256, 64, 32, 96
RK = 32
E, FF, CAP = 16, 1024, 32
EPS = 1e-6
C_QK, C_V, C_O, C_G, C_QL, C_KV = 0, 1024, 1536, 2048, 2080, 2464
C_RQ, C_RV, C_RG, C_LOG = 2752, 3264, 3776, 4288
SLOTS, SLOT = 6, 4096
C_SLOT = 4
VA = dict(ada=0, n1=48, n2=56, bqk=64, blog=72, cb=96)
VA_N = 104
VB = dict(cw=0, qa=40, kva=43, mln=45, retn=49)
VB_N = 53


class Signal:

    def __init__(self, sem):
        self.sem, self.base, self.total = sem, 0, 0

    def inc(self, n=1):
        self.total += n
        return self.sem, n

    def reach(self, n):
        return self.sem, self.base + n

    def latest(self):
        return self.sem, self.total


def token_runs(tiles):
    runs = []
    for t in tiles:
        if runs and runs[-1][0] + runs[-1][1] == t:
            runs[-1][1] += 1
        else:
            runs.append([t, 1])
    return runs


def seen_by(direction, s, last):
    if direction == 0:
        tiles = range(s, NT)
    else:
        tiles = {0: (0, 2, 3), 1: (0, 1, 2, 3), 2: (2,), 3: (2, 3)}[s]
    return [t for t in tiles if not last or t >= 2]


def build_program(nc, a, out):
    ctx = ExitStack()
    with ctx:
        def sb(name, shape, dt=F32):
            return ctx.enter_context(nc.sbuf_tensor(name, shape, dt))

        ring = sb("ring", [P, SLOTS, SLOT])
        xT = sb("xT", [P, KD, T])
        hT = sb("hT", [P, KD, T])
        work = sb("work", [P, 12544 + 6144])
        consts = sb("consts", [P, 2 * P])
        cbf = sb("cbf", [P, 3 * P], BF16)
        pick3 = sb("pick3", [P, H], BF16)
        rope = sb("rope", [P, 2, 2, ROPE])
        slot_no = sb("slot_no", [P, CAP])
        condT = sb("condT", [P, KD, 32])
        vA = sb("vA", [P, DEPTH, VA_N])
        vB = sb("vB", [P, DEPTH, VB_N])
        mod = sb("mod", [P, DEPTH, 48, 2])
        scale12 = sb("scale12", [P, DEPTH, 2, KD, 2])
        eps = sb("eps", [P, 1])
        gate_bias = sb("gate_bias", [P, 1])
        bank = [ctx.enter_context(nc.psum_tensor(f"bank{i}", [P, 512], F32)) for i in range(8)]

        ident, ones = consts[:, 0:P], consts[:, P:2 * P]
        identb, neg_f, neg_b = cbf[:, 0:P], cbf[:, P:2 * P], cbf[:, 2 * P:3 * P]

        class Signals:
            def __init__(self, names):
                self.all = [Signal(ctx.enter_context(nc.semaphore(name))) for name in names]
                (self.pe, self.act, self.dve, self.pool, self.weights_used, self.small_loaded, self.stored,
                 self.rows_ready, self.w_ready, self.p_ready, self.pv_done, self.scores_ready, self.num_read,
                 self.dve_step, self.act_step, self.even_table, self.odd_table, self.sel_ready, self.gathered,
                 self.selT_done, self.w13_done, self.silu_done, self.hid_ready, self.hidT_done,
                 self.hidT_ready, self.ys_ready, self.scattered, self.x_added, self.xs_ready,
                 self.selT_ready, self.max_ready, self.exp_ready, self.pT_done, self.pT_ready, self.gate_pe,
                 self.gate_act, self.gate_dve, self.masked_ready, self.norm_pe, self.norm_act,
                 self.norm_dve, self.x_loaded, self.mod_rows_ready, self.mod_turned, self.mod_added,
                 self.vectors_turned, self.branch_done, self.rms_act, self.rms_pe, self.rms_dve,
                 self.h_ready, self.vectors_loaded) = self.all

        S = Signals(("pe", "act", "dve", "pool", "weights_used", "small_loaded", "stored", "rows_ready",
            "w_ready", "p_ready", "pv_done", "scores_ready", "num_read", "dve_step", "act_step",
            "even_table", "odd_table", "sel_ready", "gathered", "selT_done", "w13_done", "silu_done",
            "hid_ready", "hidT_done", "hidT_ready", "ys_ready", "scattered", "x_added",
            "xs_ready", "selT_ready", "max_ready", "exp_ready", "pT_done", "pT_ready", "gate_pe", "gate_act",
            "gate_dve", "masked_ready", "norm_pe", "norm_act", "norm_dve",
            "x_loaded", "mod_rows_ready", "mod_turned", "mod_added", "vectors_turned",
            "branch_done", "rms_act", "rms_pe", "rms_dve", "h_ready", "vectors_loaded"))
        slot_loaded = [ctx.enter_context(nc.semaphore(f"slot_loaded{i}")) for i in range(SLOTS)]

        def link(eng, sig, ins):
            ins.then_inc(*sig.inc())
            eng.wait_ge(*sig.latest())

        def stage():
            for s in S.all:
                s.base = s.total
            return nc.Block(no_gpsimd_drain=True)

        def region(at, *shape):
            n = 1
            for x in shape:
                n *= x
            v = work[:, at:at + n]
            if len(shape) == 2:
                return v.rearrange("p (a b) -> p a b", a=shape[0])
            if len(shape) == 3:
                return v.rearrange("p (a b c) -> p a b c", a=shape[0], b=shape[1])
            if len(shape) == 4:
                return v.rearrange("p (a b c d) -> p a b c d", a=shape[0], b=shape[1], c=shape[2])
            return v

        YA, YB, YC = 12544, 12544 + 2048, 12544 + 4096

        loads = []
        first = {}

        slot_of, last_user, turn_of = [], [], []
        in_slot = [[] for _ in range(SLOTS)]

        def add(key, srcs, slots=range(SLOTS)):
            first[key] = len(loads)
            for src in srcs:
                slot = min(slots, key=lambda i: in_slot[i][-1] if in_slot[i] else i - SLOTS)
                slot_of.append(slot)
                last_user.append(in_slot[slot][-1] if in_slot[slot] else None)
                turn_of.append(len(in_slot[slot]))
                in_slot[slot].append(len(loads))
                loads.append(src)

        def k_major(src):
            return src.rearrange("(k p) n -> p k n", p=P)

        def add_modulation(l, r):
            ada = k_major(a["ada_w"][l])
            add(("ada", l, r), [ada[:, :, j * 512:(j + 1) * 512] for j in range(4 * r, 4 * r + 4)])

        add_modulation(0, 0)
        for l in range(DEPTH):
            w_in = k_major(a["w_in"][l])

            def add_w_in(key, c, n, slots=range(SLOTS)):
                add((key, l), [w_in[:, :, c:c + n]], slots)

            add_w_in("g", C_G, 64)
            add_w_in("qk", C_QK, 512)
            add_w_in("qk2", C_QK + 512, 512)
            if l == 0:
                add_modulation(0, 1)
            add_w_in("v", C_V, 512)
            if l == 0:
                add_modulation(0, 2)
            add_w_in("o", C_O, 512)
            add(("b", l), [w_in[:, :, c:c + n] for c, n in ((C_QL, 384), (C_KV, 288))])
            add(("bh", l), [k_major(a["mla_wq_b"][l]), k_major(a["mla_wkv_b"][l])])
            for key, c in (("rqk", C_RQ), ("rv", C_RV), ("rg", C_RG)):
                add_w_in(key, c, 512, range(C_SLOT))
            for i in range(6):
                n, c = divmod(i, 2)
                col = C_LOG + n * D + c * 512
                add(("merge", l, i), [w_in[:, :, col:col + 512],
                                      k_major(a["w_branch"][l, n])[:, :, c * 512:(c + 1) * 512]],
                    range(C_SLOT if i < 4 else SLOTS))
                if l == 0 and i >= 3:
                    add_modulation(1, i - 3)
            add(("out", l), [k_major(a["w_out"][l])[:, :, c * 512:(c + 1) * 512] for c in range(2)])
            experts = []
            for e in range(E):
                w1, w3, w2 = (k_major(a[x][l, e]) for x in ("exp_w1", "exp_w3", "exp_w2"))
                experts += [w1[:, 0:4], w3[:, 0:4], w1[:, 4:8], w3[:, 4:8], w2[:, 0:4], w2[:, 4:8]]
            add(("moe", l), experts)

        def slot_view(n, k, cols):
            return ring[:, slot_of[n], 0:k * cols].rearrange("p (k n) -> p k n", k=k)

        issued = [0]

        def run_ahead(sp, next_key, slots=range(SLOTS), until=None):
            end = first[next_key] if next_key in first else len(loads)
            while issued[0] < (first[until] if until else len(loads)):
                n = issued[0]
                if (last_user[n] is not None and last_user[n] >= end) or slot_of[n] not in slots:
                    break
                if last_user[n] is not None:
                    sp.wait_ge(S.weights_used.sem, last_user[n] + 1)
                sp.dma_start(slot_view(n, loads[n].shape[1], loads[n].shape[2]), loads[n]) \
                    .then_inc(slot_loaded[slot_of[n]], 16)
                issued[0] += 1

        def loaded_count(n):
            return slot_loaded[slot_of[n]], 16 * (turn_of[n] + 1)

        def arrived(pe, n):
            pe.wait_ge(*loaded_count(n))

        class Vectors:

            def __init__(self, l, at):
                self.l = l
                self.rows_a, self.rows_b = work[0:VA_N, at:at + P], work[0:VB_N, at + P:at + 2 * P]

            def load(self, pool):
                l = self.l

                def rows(dst, at, src):
                    pool.dma_start(dst[at:at + src.shape[0], :], src).then_inc(*S.small_loaded.inc(16))

                def cut(v):
                    return v.rearrange("(r p) -> r p", p=P)

                rows(self.rows_a, VA["ada"], cut(a["ada_b"][l]))
                rows(self.rows_a, VA["n1"], cut(a["norm1_w"][l]))
                rows(self.rows_a, VA["n2"], cut(a["norm2_w"][l]))
                rows(self.rows_a, VA["bqk"], cut(a["b_in"][l, C_QK:C_QK + 1024]))
                rows(self.rows_a, VA["blog"], cut(a["b_in"][l, C_LOG:C_LOG + 3 * D]))
                rows(self.rows_a, VA["cb"], cut(a["conv_b"][l]))
                rows(self.rows_b, VB["cw"], a["conv_w"][l].rearrange("j (r p) -> (j r) p", p=P))
                rows(self.rows_b, VB["qa"], cut(a["mla_qa_norm"][l]))
                rows(self.rows_b, VB["kva"], cut(a["mla_kva_norm"][l]))
                rows(self.rows_b, VB["mln"], cut(a["ml_norm_w"][l]))
                rows(self.rows_b, VB["retn"], cut(a["ret_norm_w"][l]))

            def turn(self, pe, b):
                nc.tensor.transpose(b[:, 0:VA_N], self.rows_a, ident[0:VA_N, 0:VA_N])
                nc.tensor.transpose(b[:, P:P + VB_N], self.rows_b, ident[0:VB_N, 0:VB_N]) \
                    .then_inc(*S.vectors_turned.inc())

            def store(self, dve, b):
                dve.wait_ge(*S.vectors_turned.reach(1))
                nc.vector.tensor_copy(vA[:, self.l, :], b[:, 0:VA_N])
                link(dve, S.dve_step, nc.vector.tensor_copy(vB[:, self.l, :], b[:, P:P + VB_N]))

        class Modulation:

            def __init__(self, l, r, i, at, product_bank, turn_bank):
                self.l, self.r, self.i = l, r, i
                self.rows = region(at, 512)
                self.a, self.b = product_bank, turn_bank
                self.n0 = first["ada", l, r]

            def product(self, pe):
                if self.i:
                    pe.wait_ge(*S.mod_rows_ready.reach(self.i))
                for j in range(4):
                    arrived(pe, self.n0 + j)
                for k in range(KD):
                    for j in range(4):
                        ins = nc.tensor.matmul(self.a[32 * j:32 * j + 32, :], condT[:, k, :],
                                               slot_view(self.n0 + j, KD, 512)[:, k, :],
                                               start=(k == 0), stop=(k == KD - 1))
                ins.then_inc(*S.weights_used.inc(4))

            def copy_rows(self, act):
                if self.i:
                    act.wait_ge(*S.mod_turned.reach(self.i))
                act.wait_ge(S.weights_used.sem, self.n0 + 4)
                nc.scalar.copy(self.rows, self.a[:, :]).then_inc(*S.mod_rows_ready.inc())

            def turn(self, pe):
                pe.wait_ge(*S.mod_rows_ready.reach(self.i + 1))
                if self.i:
                    pe.wait_ge(*S.mod_added.reach(self.i))
                for i in range(4):
                    ins = nc.tensor.transpose(self.b[:, i * P:(i + 1) * P], self.rows[:, i * P:(i + 1) * P], ident)
                ins.then_inc(*S.mod_turned.inc())

            def add(self, dve):
                dve.wait_ge(*S.mod_turned.reach(self.i + 1))
                for j in range(4):
                    at = 16 * self.r + 4 * j
                    ins = nc.vector.tensor_tensor(
                        mod[:, self.l, at:at + 4, :],
                        self.b[:, :].rearrange("p (i w) -> p i w", i=4)[:, :, 32 * j:32 * j + 2],
                        vA[:, self.l, at:at + 4].unsqueeze(2).broadcast_to([P, 4, 2]), ALU.add)
                ins.then_inc(*S.mod_added.inc())
                dve.wait_ge(*S.mod_added.latest())
                if self.r != 1:
                    i, item = (0, 1) if self.r == 0 else (1, 4)
                    w = vA[:, self.l, VA["n1" if i == 0 else "n2"]:][:, 0:KD].unsqueeze(2).broadcast_to([P, KD, 2])
                    link(dve, S.dve_step, nc.vector.scalar_tensor_tensor(
                        scale12[:, self.l, i, :, :], mod[:, self.l, item * KD:(item + 1) * KD, :], 1.0, w,
                        ALU.add, ALU.mult))

        class Normalise:

            def __init__(self, l, which, q0, at, b):
                self.l, self.which, self.q0, self.bank = l, which, q0, b
                self.square = region(at, KD, T)
                self.dev, self.inv = region(YA + 1024, T), region(YA + 1536, T)

            def squares(self, act, x_ready=None):
                for k in range(KD):
                    if x_ready is not None:
                        act.wait_ge(*x_ready.reach(k + 1))
                    nc.scalar.activation(self.square[:, k, self.q0:], xT[:, k, self.q0:], ACT.Square) \
                        .then_inc(*S.rms_act.inc())

            def total(self, pe):
                for k in range(KD):
                    pe.wait_ge(*S.rms_act.reach(k + 1))
                    ins = nc.tensor.matmul(self.bank[:, self.q0:], ones, self.square[:, k, self.q0:],
                                           start=(k == 0), stop=(k == KD - 1))
                ins.then_inc(*S.rms_pe.inc())

            def root(self, act):
                act.wait_ge(*S.rms_pe.reach(1))
                nc.scalar.activation(self.dev[:, self.q0:], self.bank[:, self.q0:], ACT.Sqrt, scale=1.0 / D,
                                     bias=eps[:, 0:1]).then_inc(*S.rms_act.inc())

            def inverse(self, dve):
                dve.wait_ge(*S.rms_act.reach(KD + 1))
                link(dve, S.dve_step, nc.vector.reciprocal(self.inv[:, self.q0:], self.dev[:, self.q0:]))

            def scale(self, dve):
                for k in range(KD):
                    for s in range(self.q0 // CT, 2):
                        sl = slice(s * CT, (s + 1) * CT)
                        ins = nc.vector.scalar_tensor_tensor(hT[:, k, sl], xT[:, k, sl],
                                                             scale12[:, self.l, self.which, k, s:s + 1],
                                                             self.inv[:, sl], ALU.mult, ALU.mult)
                    ins.then_inc(*S.rms_dve.inc())

            def shift(self, act):
                for k in range(KD):
                    act.wait_ge(*S.rms_dve.reach(k + 1))
                    for s in range(self.q0 // CT, 2):
                        sl = slice(s * CT, (s + 1) * CT)
                        at = 3 * self.which * KD + k
                        ins = nc.scalar.activation(hT[:, k, sl], hT[:, k, sl], ACT.Identity,
                                                   bias=mod[:, self.l, at, s:s + 1])
                    ins.then_inc(*S.h_ready.inc())

        x_rows = region(0, NT, D)
        cond_rows = work[0:2 * KD, 4096:4096 + P]
        mask_in = work[:, 4224:4224 + 3 * P]
        with stage() as block:
            vectors = Vectors(0, 4608)
            shifts = Modulation(0, 0, 0, 5120, bank[4], bank[5])
            norm = Normalise(0, 0, 0, 6144, bank[7])

            @block.sync
            def _(sp):
                for dst, src in (
                        (consts[:, :], a["consts"]),
                        (cond_rows[0:KD, :], a["c_ctx"].rearrange("(k p) -> k p", p=P)),
                        (cond_rows[KD:2 * KD, :], a["c"].rearrange("b (k p) -> (b k) p", p=P)),
                        (x_rows[:, 0:2, :], a["ctx"].rearrange("b (t p) d -> p (b t) d", p=P)),
                        (x_rows[:, 2:4, :], a["x"].rearrange("b (t p) d -> p (b t) d", p=P))):
                    sp.dma_start(dst, src).then_inc(*S.x_loaded.inc(16))
                run_ahead(sp, ("g", 0), until=("g", 0))
                sp.wait_ge(*S.small_loaded.reach(16 * 14))
                run_ahead(sp, ("g", 0))

            @block.gpsimd
            def _(pool):
                nc.gpsimd.memset(condT[:, :, :], 0.0).then_inc(*S.pool.inc())
                nc.gpsimd.memset(eps[:, :], EPS).then_inc(*S.pool.inc())
                vectors.load(pool)
                for dst, src in ((mask_in, a["masks"]), (rope[:, :, :, :], a["rope"]), (slot_no[:, :], a["slot_no"])):
                    pool.dma_start(dst, src).then_inc(*S.small_loaded.inc(16))

            @block.tensor
            def _(pe):
                pe.wait_ge(*S.x_loaded.reach(16 * 5))
                nc.tensor.transpose(bank[7][:, 0:2 * KD], cond_rows, ident[0:2 * KD, 0:2 * KD]) \
                    .then_inc(*S.pe.inc())
                for k in range(KD):
                    if k >= 4:
                        pe.wait_ge(*S.dve.reach(k - 3))
                    for t in range(NT):
                        ins = nc.tensor.transpose(bank[k % 4][:, t * P:(t + 1) * P],
                                                  x_rows[:, t, k * P:(k + 1) * P], ident)
                    ins.then_inc(*S.pe.inc())
                pe.wait_ge(*S.act.reach(1))
                norm.total(pe)
                shifts.product(pe)
                pe.wait_ge(*S.small_loaded.reach(16 * 14))
                vectors.turn(pe, bank[6])
                shifts.turn(pe)

            @block.scalar
            def _(act):
                act.wait_ge(*S.pool.reach(2))
                act.wait_ge(*S.pe.reach(1))
                nc.scalar.activation(condT[:, :, 0:2], bank[7][:, 0:2 * KD].rearrange("p (s k) -> p k s", s=2),
                                     ACT.Silu).then_inc(*S.act.inc())
                norm.squares(act, x_ready=S.dve)
                norm.root(act)
                shifts.copy_rows(act)

            @block.vector
            def _(dve):
                for k in range(KD):
                    dve.wait_ge(*S.pe.reach(k + 2))
                    nc.vector.tensor_copy(xT[:, k, :], bank[k % 4][:, :]).then_inc(*S.dve.inc())
                norm.inverse(dve)
                dve.wait_ge(*S.small_loaded.reach(16 * 14))
                link(dve, S.dve_step, nc.vector.tensor_copy(cbf[:, :], mask_in))
                link(dve, S.dve_step, nc.vector.tensor_tensor(pick3[:, :], identb[:, 0:H], identb[:, 32:32 + H],
                                                              ALU.add))
                nc.vector.tensor_tensor(pick3[:, :], pick3[:, :], identb[:, 64:64 + H], ALU.add)
                vectors.store(dve, bank[6])
                shifts.add(dve)

        def token_major(pe, jobs, banks, g=0):
            for job in jobs:
                n, cols, tiles = job[:3]
                arrived(pe, n)
                for i, t in enumerate(tiles):
                    if g >= banks:
                        pe.wait_ge(*S.dve.reach(g - banks + 1))
                    for k in range(KD):
                        ins = nc.tensor.matmul(bank[g % banks][:, 0:cols], hT[:, k, t * P:(t + 1) * P],
                                               slot_view(n, KD, cols)[:, k, :], start=(k == 0), stop=(k == KD - 1))
                    if i < len(tiles) - 1:
                        ins.then_inc(*S.pe.inc())
                    else:
                        ins.then_inc(*S.weights_used.inc())
                    g += 1

        yT = region(YA, 12, T)

        def add_bias(dve, banks, jobs, bias, after={}):
            g = 0
            for j, (n, cols, tiles, b0, dst) in enumerate(jobs):
                for i, t in enumerate(tiles):
                    if i < len(tiles) - 1:
                        dve.wait_ge(*S.pe.reach(g - j + 1))
                    else:
                        dve.wait_ge(S.weights_used.sem, n + 1)
                    src, b = bank[g % banks][:, 0:cols], bias[:, b0:b0 + cols]
                    o = dst(t)
                    if o.ndim == 3:
                        src = src.rearrange("p (h d) -> p h d", h=H)
                        b = b.rearrange("p (h d) -> p h d", h=H)
                    nc.vector.tensor_tensor(o, src, b, ALU.add).then_inc(*S.dve.inc())
                    if g in after:
                        after[g](dve)
                    g += 1

        def load_bias(pool, l, dst, col, n):
            pool.dma_start(dst, a["b_in"][l, col:col + n].partition_broadcast(P)) \
                .then_inc(*S.small_loaded.inc(16))

        qkT = region(0, 8, T)
        v_aug = region(4096, NT, H, DH + 1)
        o_gate = region(6176, NT, W)
        bias_a = region(8224, 1024)
        c_tok, e_tok = region(9920, NT, 64), region(10176, NT, 64)
        c_rows, d_rows = (work[0:64, x:x + T] for x in (10432, 11456))
        stack = work[:, 10944:11456].bitcast(BF16).rearrange("p (d t) -> p d t", d=2)
        h_sum = region(YC, NT, H, DH)
        pad = region(YB, 2, 2, CT + 4)
        conv = region(YA, 2, T)

        def project_a(l, last):
            n_g, n_qk, n_v = (first[key, l] for key in ("g", "qk", "v"))
            jobs = [(n_v, 512, range(NT), 0, lambda t: v_aug[:, t, :, 0:DH])]
            rounds = [] if l else [Modulation(0, 1, 0, YC, bank[2], bank[3]), Modulation(0, 2, 1, YC, bank[2], bank[3])]
            norm = Normalise(l, 0, 0, 0, bank[5])
            pre, low, mag = region(YC, T), region(YC + 512, T), region(YC + 1024, T)
            cum = work[0:64, YC + 1536:YC + 2048]
            m_rows = work[0:64, YC:YC + T]
            hi, mid = (work[0:64, x:x + T // 2].bitcast(BF16) for x in (YC + 512, YC + 768))
            with stage() as block:
                @block.sync
                def _(sp):
                    run_ahead(sp, ("o", l))

                @block.gpsimd
                def _(pool):
                    for g in range(4):
                        pool.dma_start(gate_bias[32 * g:32 * g + 32, :],
                                       a["b_in"][l, C_G + H * g:C_G + H * g + 32].rearrange("(p o) -> p o", o=1)) \
                            .then_inc(*S.vectors_loaded.inc(16))
                    load_bias(pool, l, bias_a, C_V, 1024)
                    nc.gpsimd.memset(pad[:, :, :, :], 0.0).then_inc(*S.pool.inc())
                    nc.gpsimd.memset(v_aug[:, :, :, DH:DH + 1], 1.0).then_inc(*S.pool.inc())
                    nc.gpsimd.memset(stack[:, :, :], 0.0).then_inc(*S.pool.inc())

                @block.tensor
                def _(pe):
                    if l:
                        norm.total(pe)
                    arrived(pe, n_g)
                    for k in range(KD):
                        pe.wait_ge(*S.h_ready.reach(k + 1))
                        for g in range(4):
                            ins = nc.tensor.matmul(bank[4][32 * g:32 * g + 32, :],
                                                   slot_view(n_g, KD, 64)[:, k, H * g:H * g + 32], hT[:, k, :],
                                                   start=(k == 0), stop=(k == KD - 1))
                    ins.then_inc(*S.weights_used.inc())
                    for f in range(8):
                        if f % 4 == 0:
                            arrived(pe, n_qk + f // 4)
                        if f >= 2:
                            pe.wait_ge(*S.act.reach(max(1, 2 * f - 4)))
                        t0 = CT if last and f < 4 else 0
                        for k in range(KD):
                            ins = nc.tensor.matmul(bank[6 + f % 2][:, t0:], slot_view(n_qk + f // 4, KD, 512)[:, k, (f % 4) * P:(f % 4 + 1) * P],
                                                   hT[:, k, t0:], start=(k == 0), stop=(k == KD - 1))
                        if f % 4 < 3:
                            ins.then_inc(*S.pv_done.inc())
                        else:
                            ins.then_inc(*S.weights_used.inc())
                        if f == 2:
                            pe.wait_ge(*S.gate_dve.reach(3))
                            for i, rows in enumerate((c_rows, d_rows)):
                                for t in range(NT):
                                    ins = nc.tensor.transpose(bank[4 + i][:, t * 64:(t + 1) * 64],
                                                              rows[:, t * P:(t + 1) * P], ident[0:64, 0:64])
                            ins.then_inc(*S.gate_pe.inc())
                    if rounds:
                        rounds[0].product(pe)
                    token_major(pe, jobs, 2)
                    if rounds:
                        rounds[0].turn(pe)
                        rounds[1].product(pe)
                        rounds[1].turn(pe)

                @block.scalar
                def _(act):
                    if l:
                        norm.squares(act)
                        norm.root(act)
                    norm.shift(act)
                    act.wait_ge(S.weights_used.sem, n_g + 1)
                    act.wait_ge(*S.vectors_loaded.reach(16 * 4))
                    nc.scalar.activation(pre, bank[4][:, :], ACT.Identity, bias=gate_bias[:, 0:1]) \
                        .then_inc(*S.gate_act.inc())
                    act.wait_ge(*S.gate_dve.reach(1))
                    link(act, S.act_step, nc.scalar.activation(mag, mag, ACT.Exp, scale=-1.0))
                    nc.scalar.activation(mag, mag, ACT.Ln, bias=1.0).then_inc(*S.gate_act.inc())
                    for d in range(2):
                        nc.scalar.copy(c_rows[32 * d:32 * d + 32, :], pre[64 * d:64 * d + 32, :])
                    act.wait_ge(*S.gate_dve.reach(2))
                    for d in range(2):
                        ins = nc.scalar.copy(cum[32 * d:32 * d + 32, :], low[64 * d + 32:64 * d + 64, :])
                    ins.then_inc(*S.gate_act.inc())
                    act.wait_ge(*S.pool.reach(1))
                    for f in range(9):
                        if f == 2:
                            act.wait_ge(*S.gate_dve.reach(3))
                            act.wait_ge(*S.pool.reach(3))
                            for i, part in enumerate((hi, mid, m_rows)):
                                for d in range(2):
                                    nc.scalar.copy(stack[32 * i:32 * i + 32, d, :], part[32 * d:32 * d + 32, :])
                        if f == 4:
                            act.wait_ge(*S.gate_pe.reach(1))
                            nc.scalar.activation(e_tok, bank[5][:, 0:256].rearrange("p (t r) -> p t r", t=NT), ACT.Exp)
                        if f < 8:
                            if f % 4 < 3:
                                act.wait_ge(*S.pv_done.reach(f - f // 4 + 1))
                            else:
                                act.wait_ge(S.weights_used.sem, n_qk + f // 4 + 1)
                            if f >= 2:
                                act.wait_ge(*S.p_ready.reach(f - 1))
                            for s in range(1 if last and f < 4 else 0, 2):
                                ins = nc.scalar.activation(pad[:, f % 2, s, 2:2 + CT],
                                                           bank[6 + f % 2][:, s * CT:(s + 1) * CT], ACT.Identity,
                                                           bias=vA[:, l, VA["bqk"] + f:VA["bqk"] + f + 1])
                            ins.then_inc(*S.act.inc())
                        if f >= 1:
                            g = f - 1
                            t0 = CT if last and g < 4 else 0
                            act.wait_ge(*S.p_ready.reach(g + 1))
                            nc.scalar.activation(qkT[:, g, t0:], conv[:, g % 2, t0:], ACT.Silu,
                                                 bias=vA[:, l, VA["cb"] + g:VA["cb"] + g + 1]).then_inc(*S.act.inc())
                    for r in rounds:
                        r.copy_rows(act)

                @block.vector
                def _(dve):
                    if l:
                        norm.inverse(dve)
                    norm.scale(dve)
                    dve.wait_ge(*S.gate_act.reach(1))
                    link(dve, S.dve_step, nc.vector.tensor_scalar(low, pre, 0.0, None, ALU.min))
                    nc.vector.scalar_tensor_tensor(mag, low, -2.0, pre, ALU.mult, ALU.add).then_inc(*S.gate_dve.inc())
                    dve.wait_ge(*S.gate_act.reach(2))
                    link(dve, S.dve_step, nc.vector.tensor_tensor(mag, mag, low, ALU.subtract))
                    one = ones[:, 0:1].broadcast_to([P, T])
                    nc.vector.tensor_tensor_scan(low[32:64, :], one[32:64, :], mag[32:64, :], 0.0, ALU.mult, ALU.add)
                    b, sb_, ob = mag[96:128, :], low[96:128, :], one[96:128, :]
                    link(dve, S.dve_step, nc.vector.tensor_tensor_scan(
                        sb_[:, CT - 1::-1], ob[:, 0:CT], b[:, CT - 1::-1], 0.0, ALU.mult, ALU.add))
                    nc.vector.tensor_tensor_scan(
                        sb_[:, T - 1:CT - 1:-1], ob[:, 0:LT], b[:, T - 1:CT - 1:-1], sb_[:, 0:1],
                        ALU.mult, ALU.add).then_inc(*S.gate_dve.inc())
                    dve.wait_ge(*S.gate_act.reach(3))
                    link(dve, S.dve_step, nc.vector.tensor_tensor(c_rows, c_rows, cum, ALU.add))
                    nc.vector.tensor_tensor_scan(m_rows[0:32, :], c_rows[0:32, :], c_rows[0:32, :], 0.0,
                                                 ALU.max, ALU.max)
                    b, mb = c_rows[32:64, :], m_rows[32:64, :]
                    link(dve, S.dve_step, nc.vector.tensor_tensor_scan(
                        mb[:, CT - 1::-1], b[:, CT - 1::-1], b[:, CT - 1::-1], 0.0, ALU.max, ALU.max))
                    link(dve, S.dve_step, nc.vector.tensor_tensor_scan(
                        mb[:, T - 1:CT - 1:-1], b[:, T - 1:CT - 1:-1], b[:, T - 1:CT - 1:-1], mb[:, 0:1],
                        ALU.max, ALU.max))
                    link(dve, S.dve_step, nc.vector.tensor_scalar(m_rows, m_rows, -1.0, None, ALU.mult))
                    nc.vector.tensor_tensor(d_rows, cum, m_rows, ALU.add)
                    link(dve, S.dve_step, nc.vector.tensor_copy(hi, m_rows))
                    link(dve, S.dve_step, nc.vector.tensor_tensor(m_rows, m_rows, hi, ALU.subtract))
                    link(dve, S.dve_step, nc.vector.tensor_copy(mid, m_rows))
                    nc.vector.tensor_tensor(m_rows, m_rows, mid, ALU.subtract).then_inc(*S.gate_dve.inc())
                    for f in range(8):
                        dve.wait_ge(*S.act.reach(1 if f == 0 else 2 * f))
                        if f >= 2:
                            dve.wait_ge(*S.act.reach(2 * f - 1))
                        s0 = 1 if last and f < 4 else 0
                        o = conv[:, f % 2, s0 * CT:].rearrange("p (s t) -> p s t", t=CT)
                        for j in range(5):
                            x = pad[:, f % 2, s0:, j:j + CT]
                            w = vB[:, l, VB["cw"] + j * 8 + f:VB["cw"] + j * 8 + f + 1]
                            if j == 0:
                                ins = nc.vector.tensor_scalar(o, x, w, None, ALU.mult)
                            else:
                                ins = nc.vector.scalar_tensor_tensor(o, x, w, o, ALU.mult, ALU.add)
                            if j < 4:
                                link(dve, S.dve_step, ins)
                        ins.then_inc(*S.p_ready.inc())
                        if f == 3:
                            dve.wait_ge(*S.gate_pe.reach(1))
                            nc.vector.tensor_copy(c_tok, bank[4][:, 0:256].rearrange("p (t r) -> p t r", t=NT))
                    dve.wait_ge(*S.small_loaded.reach(16))
                    dve.wait_ge(*S.pool.reach(2))
                    add_bias(dve, 2, jobs, bias_a)
                    for r in rounds:
                        r.add(dve)

        def mlstm(l, last):
            w_ring, p_ring = region(YA, 4, T), region(YB, 4, T)
            small = region(YA - 512, 512)
            t0 = 2 if last else 0
            nq = NT - t0
            items = [[(s, seen_by(d, s, last)) for s in range(NT)] for d in range(2)]
            ends = [0]
            for u in range(2 * H):
                ends.append(ends[-1] + len(items[u % 2]))
            lo = t0 * P

            def num(u):
                return bank[6 + u % 2][:, 0:NT * (DH + 1)].rearrange("p (t c) -> p t c", t=NT)

            def score(s):
                return bank[s][:, :] if s < 2 else bank[2][:, (s - 2) * 256:(s - 1) * 256]

            def score_at(s, t, n):
                off = t if s < 2 else t - 2
                return score(s)[:, off * P:(off + n) * P]

            n_o = first["o", l]
            steps = KD * nq // (2 * H)

            with stage() as block:
                @block.sync
                def _(sp):
                    run_ahead(sp, ("b", l))

                @block.tensor
                def _(pe):
                    def output_gate(first_step, last_step):
                        for step in range(first_step, last_step):
                            g, k = divmod(step, KD)
                            t = t0 + g
                            if step == 0:
                                arrived(pe, n_o)
                            if k == 0 and g:
                                pe.wait_ge(*S.dve.reach(g))
                            ins = nc.tensor.matmul(bank[4][:, :], hT[:, k, t * P:(t + 1) * P],
                                                   slot_view(n_o, KD, 512)[:, k, :], start=(k == 0), stop=(k == KD - 1))
                            if k == KD - 1 and g < nq - 1:
                                ins.then_inc(*S.pe.inc())
                            if k == KD - 1 and g == nq - 1:
                                ins.then_inc(*S.weights_used.inc())

                    def minus_m(b, u, stop):
                        h, d = divmod(u, 2)
                        return nc.tensor.matmul(b[:, lo:], pick3[:, h:h + 1].broadcast_to([P, P]),
                                                stack[:, d, lo:], start=True, stop=stop)

                    def rows(u):
                        if u:
                            pe.wait_ge(*S.w_ready.reach(ends[u]))
                        minus_m(bank[3], u, True).then_inc(*S.rows_ready.inc())

                    def masked_rows(u):
                        minus_m(bank[5], u, False)
                        nc.tensor.matmul(bank[5][:, lo:], identb,
                                         (neg_b if u % 2 else neg_f).unsqueeze(1).broadcast_to([P, nq, P]),
                                         start=False, stop=True).then_inc(*S.masked_ready.inc())

                    def scores(h, s):
                        at = DH * (h % 2)
                        q, k = qkT[at:at + DH, h // 2, :], qkT[at:at + DH, 4 + h // 2, :]
                        nc.tensor.matmul(score(s)[:, (lo if s < 2 else 0):], k[:, s * P:(s + 1) * P],
                                         q[:, max(lo, CT if s >= 2 else 0):], start=True, stop=True) \
                            .then_inc(*S.scores_ready.inc())

                    rows(0)
                    masked_rows(0)
                    for s in range(NT):
                        scores(0, s)
                    n = 0
                    for u in range(2 * H):
                        h, d = divmod(u, 2)
                        if u + 1 < 2 * H:
                            rows(u + 1)
                            masked_rows(u + 1)
                        output_gate(steps * u, steps * (u + 1))
                        if u >= 2:
                            pe.wait_ge(*S.num_read.reach(u - 1))
                        for i, (s, tiles) in enumerate(items[d]):
                            pe.wait_ge(*S.p_ready.reach(n + 1))
                            for j, t in enumerate(tiles):
                                ins = nc.tensor.matmul(num(u)[:, t, :], p_ring[:, n % 4, t * P:(t + 1) * P],
                                                       v_aug[:, s, h, :], start=(i == 0 and j == 0),
                                                       stop=(i == NT - 1 and j == len(tiles) - 1),
                                                       skip_group_check=True)
                            ins.then_inc(*S.pv_done.inc())
                            n += 1
                            if d == 1 and h + 1 < H:
                                for s2 in {0: (0,), 1: (1,), 2: (), 3: (2, 3)}[i]:
                                    scores(h + 1, s2)

                @block.scalar
                def _(act):
                    n = 0
                    for u in range(2 * H):
                        h, d = divmod(u, 2)
                        act.wait_ge(*S.rows_ready.reach(u + 1))
                        act.wait_ge(*S.masked_ready.reach(u + 1))
                        for s, tiles in items[d]:
                            if n >= 4:
                                act.wait_ge(*S.p_ready.reach(n - 3))
                            bias = c_tok[:, s, 32 * d + h:32 * d + h + 1]
                            ins = None
                            for t, k in token_runs([x for x in tiles if x != s]):
                                ins = nc.scalar.activation(w_ring[:, n % 4, t * P:(t + k) * P],
                                                           bank[3][:, t * P:(t + k) * P], ACT.Exp, bias=bias)
                            if s in tiles:
                                ins = nc.scalar.activation(w_ring[:, n % 4, s * P:(s + 1) * P],
                                                           bank[5][:, s * P:(s + 1) * P], ACT.Exp, bias=bias)
                            ins.then_inc(*S.w_ready.inc())
                            n += 1

                @block.vector
                def _(dve):
                    def finish(u):
                        h, d = divmod(u, 2)
                        dve.wait_ge(*S.pv_done.reach(ends[u + 1]))
                        den = num(u)[:, t0:, DH:DH + 1]
                        e = e_tok[:, t0:, 32 * d + h:32 * d + h + 1]
                        big = small[:, 0:nq].unsqueeze(2)
                        link(dve, S.dve_step, nc.vector.scalar_tensor_tensor(big, den, -1.0, e, ALU.mult, ALU.max))
                        link(dve, S.dve_step, nc.vector.tensor_tensor(big, big, den, ALU.max))
                        link(dve, S.dve_step, nc.vector.reciprocal(big, big))
                        o = h_sum[:, t0:, h, :]
                        tmp = small[:, 128:128 + nq * DH].rearrange("p (t c) -> p t c", t=nq)
                        ins = nc.vector.tensor_tensor(tmp if d else o, num(u)[:, t0:, 0:DH],
                                                      big.broadcast_to([P, nq, DH]), ALU.mult)
                        ins.then_inc(*S.num_read.inc())
                        if d:
                            dve.wait_ge(*S.num_read.latest())
                            link(dve, S.dve_step, nc.vector.tensor_tensor(o, o, tmp, ALU.add))

                    def gate_bias_in(g):
                        if g < nq - 1:
                            dve.wait_ge(*S.pe.reach(g + 1))
                        else:
                            dve.wait_ge(S.weights_used.sem, n_o + 1)
                        nc.vector.tensor_tensor(o_gate[:, t0 + g, :], bank[4][:, :], bias_a[:, 512:1024], ALU.add) \
                            .then_inc(*S.dve.inc())

                    n = 0
                    for u in range(2 * H):
                        h, d = divmod(u, 2)
                        if u and steps * u % KD == 0:
                            gate_bias_in(steps * u // KD - 1)
                        for i, (s, tiles) in enumerate(items[d]):
                            if d == 0:
                                dve.wait_ge(*S.scores_ready.reach(NT * h + (s + 1 if s < 2 else NT)))
                            dve.wait_ge(*S.w_ready.reach(n + 1))
                            if n >= 4:
                                dve.wait_ge(*S.pv_done.reach(n - 3))
                            for t, k in token_runs(tiles):
                                ins = nc.vector.scalar_tensor_tensor(
                                    p_ring[:, n % 4, t * P:(t + k) * P], score_at(s, t, k), DH ** -0.5,
                                    w_ring[:, n % 4, t * P:(t + k) * P], ALU.mult, ALU.mult)
                            ins.then_inc(*S.p_ready.inc())
                            n += 1
                            if i == 1 and u:
                                finish(u - 1)
                    gate_bias_in(nq - 1)
                    finish(2 * H - 1)

        class HeadNorm:

            def __init__(self, l, last, h, gate, sq, y_out, vec):
                self.l = l
                self.t0 = 2 if last else 0
                self.nq = NT - self.t0
                self.n = self.nq * H
                self.flat = h.rearrange("p t h d -> p t (h d)")
                self.x = h[:, self.t0:].rearrange("p t h d -> p (t h) d")
                self.sq = sq[:, self.t0:].rearrange("p t (h d) -> p (t h) d", h=H)
                self.gate = gate[:, self.t0:].rearrange("p t (h d) -> p (t h) d", h=H)
                self.mean, self.var, self.dev = (region(YA - 512, 4, 32)[:, i, 0:self.n] for i in range(3))
                self.y_out, self.vec = y_out, vec

            def wide(self, v):
                return v.unsqueeze(2).broadcast_to([P, self.n, DH])

            def centre(self, dve):
                link(dve, S.dve_step, nc.vector.reduce_sum(self.mean, self.x, axis=AX.X))
                link(dve, S.dve_step, nc.vector.tensor_scalar(self.mean, self.mean, 1.0 / DH, None, ALU.mult))
                nc.vector.tensor_tensor(self.x, self.x, self.wide(self.mean), ALU.subtract) \
                    .then_inc(*S.norm_dve.inc())

            def square(self, act):
                act.wait_ge(*S.norm_dve.reach(1))
                nc.scalar.activation(self.sq, self.x, ACT.Square).then_inc(*S.norm_act.inc())

            def variance(self, dve):
                dve.wait_ge(*S.norm_act.reach(1))
                nc.vector.reduce_sum(self.var, self.sq, axis=AX.X).then_inc(*S.norm_dve.inc())

            def root(self, act):
                act.wait_ge(*S.norm_dve.reach(2))
                nc.scalar.activation(self.dev, self.var, ACT.Sqrt, scale=1.0 / DH, bias=eps[:, 0:1]) \
                    .then_inc(*S.norm_act.inc())

            def scale_and_gate(self, dve):
                dve.wait_ge(*S.norm_act.reach(2))
                link(dve, S.dve_step, nc.vector.reciprocal(self.var, self.dev))
                link(dve, S.dve_step, nc.vector.tensor_tensor(self.x, self.x, self.wide(self.var), ALU.mult))
                nc.vector.tensor_tensor(self.x, self.x, self.gate, ALU.mult).then_inc(*S.norm_dve.inc())

            def turn(self, pe):
                pe.wait_ge(*S.norm_dve.reach(3))
                for i in range(self.nq):
                    for f in range(4):
                        ins = nc.tensor.transpose(bank[4 + i][:, f * P:(f + 1) * P],
                                                  self.flat[:, self.t0 + i, f * P:(f + 1) * P], ident)
                    ins.then_inc(*S.norm_pe.inc())

            def store(self, dve):
                for i in range(self.nq):
                    dve.wait_ge(*S.norm_pe.reach(i + 1))
                    t = self.t0 + i
                    nc.vector.tensor_tensor(yT[:, self.y_out:self.y_out + 4, t * P:(t + 1) * P],
                                            bank[4 + i][:, :].rearrange("p (f t) -> p f t", f=4),
                                            vB[:, self.l, VB[self.vec]:VB[self.vec] + 4].unsqueeze(2).broadcast_to([P, 4, P]),
                                            ALU.mult).then_inc(*S.norm_dve.inc())

        qT, kT = region(0, H, T), region(4096, H, T)
        bias_b = region(5248, 672)
        q_lat, kv_lat = region(YB, NT, Q_LORA), region(4096, NT, KV_LORA + ROPE)
        k_rope = region(12288, NT, ROPE)
        qlT, kvT = region(8192, 3, T), region(9728, 2, T)
        v_mla = region(YC, NT, H, DH)

        def project_b(l, last):
            q_tiles = [2, 3] if last else [0, 1, 2, 3]
            n0 = first["b", l]
            jobs = [(n0, Q_LORA, q_tiles, 0, lambda t: q_lat[:, t, :]),
                    (n0 + 1, KV_LORA + ROPE, range(NT), Q_LORA, lambda t: kv_lat[:, t, :])]
            sums, roots = region(12416, 8), region(12424, 8)
            squares = region(10752, 2, 512)
            lows = [(q_lat, Q_LORA, t, i) for i, t in enumerate(q_tiles)] + \
                   [(kv_lat, KV_LORA, t, 4 + t) for t in range(NT)]
            norm = HeadNorm(l, last, h_sum, o_gate, region(0, NT, W), 0, "mln")
            with stage() as block:
                @block.sync
                def _(sp):
                    run_ahead(sp, ("bh", l))

                @block.gpsimd
                def _(pool):
                    load_bias(pool, l, bias_b, C_QL, 672)
                    nc.gpsimd.memset(sums, 1.0).then_inc(*S.pool.inc())

                @block.tensor
                def _(pe):
                    token_major(pe, jobs[:1], 4)
                    norm.turn(pe)
                    token_major(pe, jobs[1:], 4, len(q_tiles))
                    pe.wait_ge(*S.norm_dve.reach(3 + len(q_tiles)))
                    for i, (src, width, t, _) in enumerate(lows):
                        pe.wait_ge(*S.p_ready.reach(i + 1))
                        if i >= 4:
                            pe.wait_ge(*S.act.reach(i - 3))
                        for f in range(width // P):
                            ins = nc.tensor.transpose(bank[4 + i % 4][:, f * P:(f + 1) * P],
                                                      src[:, t, f * P:(f + 1) * P], ident)
                        ins.then_inc(*S.pv_done.inc())

                @block.vector
                def _(dve):
                    norm.centre(dve)
                    dve.wait_ge(*S.small_loaded.reach(16))
                    add_bias(dve, 4, jobs, bias_b, after={0: norm.variance, 1: norm.scale_and_gate,
                                                          2 if last else 3: norm.store})
                    dve.wait_ge(*S.dve.latest())
                    nc.vector.tensor_copy(k_rope, kv_lat[:, :, KV_LORA:])
                    dve.wait_ge(*S.exp_ready.reach(1))
                    link(dve, S.dve_step, nc.vector.reciprocal(roots, roots))
                    for src, width, t, j in lows:
                        nc.vector.tensor_scalar(src[:, t, 0:width], src[:, t, 0:width], roots[:, j:j + 1], None,
                                                ALU.mult).then_inc(*S.p_ready.inc())

                @block.scalar
                def _(act):
                    nc.scalar.activation(norm.gate, norm.gate, ACT.Sigmoid)
                    norm.square(act)
                    act.wait_ge(*S.pool.reach(1))
                    for i, (src, width, t, j) in enumerate(lows):
                        if i == 1:
                            norm.root(act)
                        act.wait_ge(*S.dve.reach(i + 1))
                        if i:
                            act.wait_ge(*S.w_ready.reach(i))
                        nc.scalar.activation(squares[:, 0, 0:width], src[:, t, 0:width], ACT.Square,
                                             scale=width ** -0.5, accum_out=sums[:, j:j + 1]) \
                            .then_inc(*S.w_ready.inc())
                    act.wait_ge(*S.w_ready.latest())
                    nc.scalar.activation(roots, sums, ACT.Sqrt, bias=eps[:, 0:1]).then_inc(*S.exp_ready.inc())
                    for i, (src, width, t, j) in enumerate(lows):
                        act.wait_ge(*S.pv_done.reach(i + 1))
                        dst, vec = (qlT, "qa") if width == Q_LORA else (kvT, "kva")
                        for f in range(width // P):
                            ins = nc.scalar.activation(dst[:, f, t * P:(t + 1) * P], bank[4 + i % 4][:, f * P:(f + 1) * P],
                                                       ACT.Copy, scale=vB[:, l, VB[vec] + f:VB[vec] + f + 1])
                        ins.then_inc(*S.act.inc())

        def rope_halves(src, dst, tmp, tab, heads):
            cos, sin = (tab[:, i, :].unsqueeze(1).broadcast_to([P, heads, ROPE]) for i in range(2))
            s5 = src.rearrange("p h (a b c) -> p h a b c", a=2, b=2)
            t5 = tmp.rearrange("p h (a b c) -> p h a b c", a=2, b=2)
            n5 = tab[:, 1, :].rearrange("p (a b c) -> p a b c", a=2, b=2)
            for part in range(2):
                for half in range(2):
                    nc.vector.tensor_tensor(t5[:, :, part, half, :], s5[:, :, part, 1 - half, :],
                                            n5[:, part, half, :].unsqueeze(1).broadcast_to([P, heads, 8]), ALU.mult)
            return nc.vector.tensor_tensor(dst, src, cos, ALU.mult)

        def mla_heads(l, last):
            q_tiles = [2, 3] if last else [0, 1, 2, 3]
            n0 = first["bh", l]
            wq = slot_view(n0, 3, H * QK)
            wkv = slot_view(n0 + 1, 2, H * (NOPE + DH))
            head = region(10752, 2, H, QK)
            sq, tmp = region(YB, H, QK), region(YB + 768, H, ROPE)
            norm_w = region(YB + 1024, 2, QK)
            st = region(YB + 1216, 4, H)
            normed = region(YB + 1248, H, QK)
            jobs = [("q", t) for t in q_tiles] + [("k", t) for t in range(NT)]
            with stage() as block:
                @block.sync
                def _(sp):
                    run_ahead(sp, ("rqk", l), range(C_SLOT))

                @block.gpsimd
                def _(pool):
                    for i, x in enumerate(("q_norm_w", "k_norm_w")):
                        pool.dma_start(norm_w[:, i, :], a[x][l].partition_broadcast(P)) \
                            .then_inc(*S.small_loaded.inc(16))

                @block.tensor
                def _(pe):
                    def product(i):
                        kind, t = jobs[i]
                        if i == 0:
                            arrived(pe, n0)
                        if i == len(q_tiles):
                            arrived(pe, n0 + 1)
                        if i >= 2:
                            pe.wait_ge(*S.num_read.reach(i - 1))
                        src, w, ks, cols = (qlT, wq, 3, 384) if kind == "q" else (kvT, wkv, 2, 512)
                        for c in range(2):
                            for k in range(ks):
                                ins = nc.tensor.matmul(bank[2 * (i % 2) + c][:, 0:cols], src[:, k, t * P:(t + 1) * P],
                                                       w[:, k, c * cols:(c + 1) * cols], start=(k == 0),
                                                       stop=(k == ks - 1))
                        if i + 1 in (len(q_tiles), len(jobs)):
                            ins.then_inc(*S.weights_used.inc())
                        else:
                            ins.then_inc(*S.pe.inc())

                    product(0)
                    for i, (kind, t) in enumerate(jobs):
                        if i + 1 < len(jobs):
                            product(i + 1)
                        pe.wait_ge(*S.dve.reach(i + 1))
                        for h in range(H):
                            if h % 4 == 0 and i:
                                pe.wait_ge(*S.act.reach(2 * i - 1 + h // 4))
                            ins = nc.tensor.transpose(bank[4 + h // 4][0:QK, (h % 4) * P:(h % 4 + 1) * P],
                                                      head[:, i % 2, h, :], ident)
                            if h % 4 == 3:
                                ins.then_inc(*S.pv_done.inc())

                @block.scalar
                def _(act):
                    def heads_in(i):
                        kind, t = jobs[i]
                        if i + 1 in (len(q_tiles), len(jobs)):
                            act.wait_ge(S.weights_used.sem, n0 + (1 if i < len(q_tiles) else 2))
                        else:
                            act.wait_ge(*S.pe.reach(i + 1 - (i >= len(q_tiles))))
                        if i >= 2:
                            act.wait_ge(*S.pv_done.reach(2 * i - 2))
                        x = head[:, i % 2, :, :]
                        if kind == "k":
                            nc.scalar.copy(x[:, :, NOPE:], k_rope[:, t, :].unsqueeze(1).broadcast_to([P, H, ROPE]))
                        for c in range(2):
                            b = bank[2 * (i % 2) + c]
                            hs = slice(4 * c, 4 * c + 4)
                            if kind == "q":
                                ins = nc.scalar.copy(x[:, hs, :], b[:, 0:384].rearrange("p (h d) -> p h d", h=4))
                            else:
                                b4 = b[:, :].rearrange("p (h d) -> p h d", h=4)
                                nc.scalar.copy(x[:, hs, 0:NOPE], b4[:, :, 0:NOPE])
                                ins = nc.scalar.copy(v_mla[:, t, hs, :], b4[:, :, NOPE:])
                        ins.then_inc(*S.num_read.inc())
                        act.wait_ge(*S.num_read.latest())
                        nc.scalar.activation(sq, x, ACT.Square).then_inc(*S.w_ready.inc())

                    heads_in(0)
                    for i, (kind, t) in enumerate(jobs):
                        act.wait_ge(*S.p_ready.reach(i + 1))
                        nc.scalar.activation(st[:, 1, :], st[:, 0, :], ACT.Sqrt, scale=1.0 / QK, bias=eps[:, 0:1]) \
                            .then_inc(*S.exp_ready.inc())
                        if i + 1 < len(jobs):
                            heads_in(i + 1)
                        dst = qT if kind == "q" else kT
                        for c in range(2):
                            act.wait_ge(*S.pv_done.reach(2 * i + c + 1))
                            nc.scalar.copy(dst[0:QK, 4 * c:4 * c + 4, t * P:(t + 1) * P],
                                           bank[4 + c][0:QK, :].rearrange("p (h t) -> p h t", h=4)) \
                                .then_inc(*S.act.inc())

                @block.vector
                def _(dve):
                    dve.wait_ge(*S.small_loaded.reach(32))
                    for i, (kind, t) in enumerate(jobs):
                        x = head[:, i % 2, :, :]
                        dve.wait_ge(*S.w_ready.reach(i + 1))
                        nc.vector.reduce_sum(st[:, 0, :], sq, axis=AX.X).then_inc(*S.p_ready.inc())
                        dve.wait_ge(*S.exp_ready.reach(i + 1))
                        link(dve, S.dve_step, nc.vector.reciprocal(st[:, 2, :], st[:, 1, :]))
                        link(dve, S.dve_step, nc.vector.tensor_tensor(
                            normed, x, st[:, 2, :].unsqueeze(2).broadcast_to([P, H, QK]), ALU.mult))
                        w = norm_w[:, 0 if kind == "q" else 1, :].unsqueeze(1).broadcast_to([P, H, QK])
                        if t < 2:
                            nc.vector.tensor_tensor(x, normed, w, ALU.mult).then_inc(*S.dve.inc())
                        else:
                            nc.vector.tensor_tensor(x[:, :, 0:NOPE], normed[:, :, 0:NOPE], w[:, :, 0:NOPE], ALU.mult)
                            turning = normed[:, :, NOPE:]
                            link(dve, S.dve_step, nc.vector.tensor_tensor(turning, turning, w[:, :, NOPE:], ALU.mult))
                            link(dve, S.dve_step, rope_halves(turning, x[:, :, NOPE:], tmp, rope[:, t - 2], H))
                            nc.vector.tensor_tensor(x[:, :, NOPE:], x[:, :, NOPE:], tmp, ALU.add) \
                                .then_inc(*S.dve.inc())

        slot_a, slot_b = ring[:, C_SLOT, :], ring[:, C_SLOT + 1, :]
        rqk = slot_a[:, 0:2048].rearrange("p (t w) -> p t w", t=NT)
        v_ret = slot_a[:, 2048:4096].rearrange("p (t h d) -> p t h d", t=NT, h=H)
        s_gate = slot_b[:, 0:2048].rearrange("p (t w) -> p t w", t=NT)
        bias_c, spare = slot_b[:, 2048:3584], slot_b[:, 3584:4096]
        rT = region(2048, 4, T)
        h_ret = region(0, NT, H, DH)
        decay = region(8192, 2, 2, 3 * P)
        ret_ring = region(9728, 4, T)

        def attention_and_project_c(l, last):
            q_tiles = [2, 3] if last else [0, 1, 2, 3]
            probs, pT = region(8192, 2, T), region(9216, 2, T)
            y = region(10240, NT, W)
            st = region(12416, 2, 4)
            jobs = [(t, h) for t in q_tiles for h in range(H)]
            scale = QK ** -0.5
            n_qk, n_v, n_g = (first[key, l] for key in ("rqk", "rv", "rg"))
            tiles = [(n_qk, t, 0, rqk[:, t, :]) for t in range(NT)] + \
                    [(n_v, t, 512, slot_a[:, 2048 + t * W:2048 + (t + 1) * W]) for t in range(NT)] + \
                    [(n_g, t, 1024, s_gate[:, t, :]) for t in q_tiles]
            per_job = KD * len(tiles) // len(jobs)

            def keys(t):
                return CT if t < 2 else T

            with stage() as block:
                @block.sync
                def _(sp):
                    run_ahead(sp, ("merge", l, 0), range(C_SLOT))

                @block.gpsimd
                def _(pool):
                    load_bias(pool, l, bias_c, C_RQ, 1536)

                @block.tensor
                def _(pe):
                    def project(first_step, last_step):
                        for step in range(first_step, last_step):
                            g, k = divmod(step, KD)
                            n, t = tiles[g][:2]
                            if k == 0:
                                arrived(pe, n)
                                if g >= 2:
                                    pe.wait_ge(*S.dve.reach(g - 1))
                            ins = nc.tensor.matmul(bank[6 + g % 2][:, :], hT[:, k, t * P:(t + 1) * P],
                                                   slot_view(n, KD, 512)[:, k, :], start=(k == 0), stop=(k == KD - 1))
                            if k == KD - 1:
                                if g + 1 == len(tiles) or tiles[g + 1][0] != n:
                                    ins.then_inc(*S.weights_used.inc())
                                else:
                                    ins.then_inc(*S.pe.inc())

                    def score(i):
                        t, h = jobs[i]
                        if i >= 2:
                            pe.wait_ge(*S.exp_ready.reach(i - 1))
                        nc.tensor.matmul(bank[i % 2][:, 0:keys(t)], qT[0:QK, h, t * P:(t + 1) * P],
                                         kT[0:QK, h, 0:keys(t)], start=True, stop=True).then_inc(*S.scores_ready.inc())

                    def values(i):
                        t, h = jobs[i]
                        pe.wait_ge(*S.pT_ready.reach(i + 1))
                        if i >= 2:
                            pe.wait_ge(*S.num_read.reach(i - 1))
                        nk = keys(t) // P
                        for s in range(nk):
                            ins = nc.tensor.matmul(bank[4 + i % 2][:, 0:DH], pT[:, i % 2, s * P:(s + 1) * P],
                                                   v_mla[:, s, h, :], start=(s == 0), stop=(s == nk - 1))
                        ins.then_inc(*S.pv_done.inc())

                    score(0)
                    for i, (t, h) in enumerate(jobs):
                        if i + 1 < len(jobs):
                            score(i + 1)
                        middle = per_job * i + per_job // 2 + 1
                        project(per_job * i, middle)
                        pe.wait_ge(*S.exp_ready.reach(i + 1))
                        if i >= 2:
                            pe.wait_ge(*S.pT_ready.reach(i - 1))
                        for s in range(keys(t) // P):
                            ins = nc.tensor.transpose(bank[2 + i % 2][:, s * P:(s + 1) * P],
                                                      probs[:, i % 2, s * P:(s + 1) * P], ident)
                        ins.then_inc(*S.pT_done.inc())
                        if i:
                            values(i - 1)
                        project(middle, per_job * (i + 1))
                    values(len(jobs) - 1)
                    for t in range(NT):
                        if t >= 2:
                            pe.wait_ge(*S.p_ready.reach(t - 1))
                        if t == 2:
                            pe.wait_ge(*S.dve.reach(len(tiles)))
                        for f in range(4):
                            ins = nc.tensor.transpose(bank[(2, 3, 6, 7)[t]][:, f * P:(f + 1) * P],
                                                      rqk[:, t, f * P:(f + 1) * P], ident)
                        ins.then_inc(*S.gate_pe.inc())
                    pe.wait_ge(*S.num_read.reach(len(jobs)))
                    for j, t in enumerate(q_tiles):
                        for f in range(4):
                            ins = nc.tensor.transpose(bank[(0, 1, 4, 5)[j]][:, f * P:(f + 1) * P],
                                                      y[:, t, f * P:(f + 1) * P], ident)
                        ins.then_inc(*S.norm_pe.inc())

                @block.vector
                def _(dve):
                    def sums_out(i):
                        t, h = jobs[i]
                        dve.wait_ge(*S.pv_done.reach(i + 1))
                        link(dve, S.dve_step, nc.vector.reciprocal(st[:, i % 2, 3:4], st[:, i % 2, 2:3]))
                        nc.vector.tensor_scalar(y[:, t, h * DH:(h + 1) * DH], bank[4 + i % 2][:, 0:DH],
                                                st[:, i % 2, 3:4], None, ALU.mult).then_inc(*S.num_read.inc())

                    def pT_copy(i):
                        dve.wait_ge(*S.pT_done.reach(i + 1))
                        n = keys(jobs[i][0])
                        nc.vector.tensor_copy(pT[:, i % 2, 0:n], bank[2 + i % 2][:, 0:n]).then_inc(*S.pT_ready.inc())

                    def bias(g):
                        n, t, b0, dst = tiles[g]
                        if g + 1 == len(tiles) or tiles[g + 1][0] != n:
                            dve.wait_ge(S.weights_used.sem, n + 1)
                        else:
                            dve.wait_ge(*S.pe.reach(g + 1 - (n - n_qk)))
                        nc.vector.tensor_tensor(dst, bank[6 + g % 2][:, :], bias_c[:, b0:b0 + 512], ALU.add) \
                            .then_inc(*S.dve.inc())

                    def rotate(t):
                        x = rqk[:, t, :].rearrange("p (h d) -> p h d", d=RK)
                        swapped, turned = (v.rearrange("p (h d) -> p h d", d=RK) for v in (bias_c[:, 0:512], spare))
                        link(dve, S.dve_step, rope_halves(x, turned, swapped, rope[:, t - 2], 2 * H))
                        link(dve, S.p_ready, nc.vector.tensor_tensor(x, turned, swapped, ALU.add))

                    dve.wait_ge(*S.small_loaded.reach(16))
                    biased = 0
                    for i, (t, h) in enumerate(jobs):
                        dve.wait_ge(*S.scores_ready.reach(i + 1))
                        if i >= 2:
                            sums_out(i - 2)
                        link(dve, S.dve_step, nc.vector.reduce_max(st[:, i % 2, 0:1], bank[i % 2][:, 0:keys(t)],
                                                                   axis=AX.X))
                        nc.vector.tensor_scalar(st[:, i % 2, 1:2], st[:, i % 2, 0:1], -scale, None, ALU.mult) \
                            .then_inc(*S.max_ready.inc())
                        if i:
                            pT_copy(i - 1)
                        while (biased + 1) * KD <= per_job * i:
                            bias(biased)
                            biased += 1
                            if biased in (NT + 1, NT + 2):
                                rotate(biased - NT + 1)
                    i = len(jobs)
                    sums_out(i - 2)
                    pT_copy(i - 1)
                    for g in range(biased, len(tiles)):
                        bias(g)
                    sums_out(i - 1)
                    for j, t in enumerate(q_tiles):
                        dve.wait_ge(*S.norm_pe.reach(j + 1))
                        nc.vector.tensor_copy(yT[:, 4:8, t * P:(t + 1) * P],
                                              bank[(0, 1, 4, 5)[j]][:, :].rearrange("p (f t) -> p f t", f=4))

                @block.scalar
                def _(act):
                    for i, (t, h) in enumerate(jobs):
                        act.wait_ge(*S.max_ready.reach(i + 1))
                        if i >= 2:
                            act.wait_ge(*S.pT_done.reach(i - 1))
                        nc.scalar.activation(probs[:, i % 2, 0:keys(t)], bank[i % 2][:, 0:keys(t)], ACT.Exp,
                                             bias=st[:, i % 2, 1:2], scale=scale, accum_out=st[:, i % 2, 2:3]) \
                            .then_inc(*S.exp_ready.inc())
                    for t in range(NT):
                        act.wait_ge(*S.gate_pe.reach(t + 1))
                        nc.scalar.copy(rT[:, :, t * P:(t + 1) * P],
                                       bank[(2, 3, 6, 7)[t]][:, :].rearrange("p (f t) -> p f t", f=4))

        def retention_and_merge(l, last):
            t0 = 2 if last else 0
            lo = t0 * P
            table_loaded = (S.even_table, S.odd_table)
            merged, early_sig = region(4096, KD, T), region(YC, 2, T)
            sig, tmp = region(2048, 2, T), region(3072, 2, T)
            norm = HeadNorm(l, last, h_ret, s_gate, ret_ring, 8, "retn")
            rounds = [Modulation(1, r, r, 9216, bank[4 if r < 2 else 0], bank[5 if r < 2 else 2])
                      for r in range(3)] if l == 0 else []
            vectors = Vectors(1, 11776)
            jobs = [(n, c, d) for n in range(3) for c in range(2) for d in range(4)]
            STEPS = KD + 4
            m0 = first["out", l]

            def sig_at(i):
                return (early_sig if i < KD else sig)[:, i % 2, lo:]

            with stage() as block:
                @block.sync
                def _(sp):
                    run_ahead(sp, ("moe", l), range(C_SLOT))
                    sp.wait_ge(*S.norm_dve.reach(3))
                    run_ahead(sp, ("moe", l))

                @block.gpsimd
                def _(pool):
                    for h in range(H):
                        if h >= 2:
                            pool.wait_ge(*S.p_ready.reach(NT * (h - 1)))
                        pool.dma_start(decay[:, h % 2], a["decay"][h]).then_inc(*table_loaded[h % 2].inc(16))
                    if rounds:
                        vectors.load(pool)

                @block.tensor
                def _(pe):
                    def merge(first_step, last_step):
                        for step in range(first_step, last_step):
                            i, k = divmod(step, STEPS)
                            n, c, d = jobs[i]
                            at = first["merge", l, 2 * n + c]
                            cols = slice(d * P, (d + 1) * P)
                            if k == 0 and d == 0:
                                arrived(pe, at)
                                arrived(pe, at + 1)
                            if k < KD:
                                if k == 0 and i >= 2:
                                    pe.wait_ge(*S.act.reach(i - 1))
                                ins = nc.tensor.matmul(bank[i % 2][:, lo:], slot_view(at, KD, 512)[:, k, cols],
                                                       hT[:, k, lo:], start=(k == 0), stop=(k == KD - 1))
                                if k == KD - 1:
                                    ins.then_inc(*S.pe.inc())
                            else:
                                k -= KD
                                if k == 0 and i >= 2:
                                    pe.wait_ge(*S.dve.reach(i - 1))
                                ins = nc.tensor.matmul(bank[2 + i % 2][:, lo:], slot_view(at + 1, 4, 512)[:, k, cols],
                                                       yT[:, 4 * n + k, lo:], start=(k == 0), stop=(k == 3))
                                if k == 3 and d < 3:
                                    ins.then_inc(*S.branch_done.inc())
                                if k == 3 and d == 3:
                                    ins.then_inc(*S.weights_used.inc(2))

                    def score(h, s):
                        at = RK * (h % 4)
                        q, k = rT[at:at + RK, h // 4, :], rT[at:at + RK, 2 + h // 4, :]
                        o = bank[4 + s][:, lo:] if s < 2 else bank[6][:, (s - 2) * CT:(s - 1) * CT]
                        nc.tensor.matmul(o, k[:, s * P:(s + 1) * P], q[:, (lo if s < 2 else CT):],
                                         start=True, stop=True).then_inc(*S.scores_ready.inc())

                    for s in range(NT):
                        score(0, s)
                    per_item = KD * STEPS // (H * NT)
                    for h in range(H):
                        if h:
                            pe.wait_ge(*S.num_read.reach(h))
                        for s in range(NT):
                            item = NT * h + s
                            pe.wait_ge(*S.p_ready.reach(item + 1))
                            for t in range(t0 if s < 2 else 2, NT):
                                ins = nc.tensor.matmul(bank[7][:, t * DH:(t + 1) * DH],
                                                       ret_ring[:, s, t * P:(t + 1) * P], v_ret[:, s, h, :],
                                                       start=(s == 0 and t == t0), stop=(s == NT - 1 and t == NT - 1),
                                                       skip_group_check=True)
                            ins.then_inc(*S.pv_done.inc())
                            if h + 1 < H:
                                for s2 in {0: (0,), 1: (1,), 2: (), 3: (2, 3)}[s]:
                                    score(h + 1, s2)
                            merge(per_item * item, per_item * (item + 1))
                    for i in range(KD, len(jobs)):
                        merge(STEPS * i, STEPS * (i + 1))
                        if i == KD + 4:
                            norm.turn(pe)
                        if rounds and i in (15, 19):
                            if i == 15:
                                pe.wait_ge(*S.norm_dve.reach(3 + norm.nq))
                                pe.wait_ge(*S.small_loaded.reach(16 * 11))
                                vectors.turn(pe, bank[6])
                            rounds[i // 4 - 3].product(pe)
                        if rounds and i in (16, 20):
                            rounds[i // 4 - 4].turn(pe)
                    if rounds:
                        pe.wait_ge(*S.dve.reach(len(jobs) - 1))
                        rounds[2].product(pe)
                    pe.wait_ge(*S.dve.reach(len(jobs)))
                    for d in range(KD):
                        if d % 4 == 0:
                            arrived(pe, m0 + d // 4)
                        if d >= 4:
                            pe.wait_ge(*S.x_added.reach(d - 3))
                        for k in range(KD):
                            ins = nc.tensor.matmul(bank[4 + d % 4][:, lo:],
                                                   slot_view(m0 + d // 4, KD, 512)[:, k, (d % 4) * P:(d % 4 + 1) * P],
                                                   merged[:, k, lo:], start=(k == 0), stop=(k == KD - 1))
                        if d % 4 < 3:
                            ins.then_inc(*S.pT_done.inc())
                        else:
                            ins.then_inc(*S.weights_used.inc())
                        if rounds and d == 1:
                            rounds[2].turn(pe)

                @block.scalar
                def _(act):
                    def gate(i):
                        n, c, d = jobs[i]
                        f = VA["blog"] + n * KD + c * 4 + d
                        act.wait_ge(*S.pe.reach(i + 1))
                        if i >= 2:
                            act.wait_ge(*S.dve.reach(i - 1))
                        nc.scalar.activation(sig_at(i), bank[i % 2][:, lo:], ACT.Sigmoid,
                                             bias=vA[:, l, f:f + 1]).then_inc(*S.act.inc())

                    nc.scalar.activation(s_gate[:, t0:, :], s_gate[:, t0:, :], ACT.Silu)
                    for h in range(H):
                        gate(h)
                        act.wait_ge(*S.pv_done.reach(NT * (h + 1)))
                        nc.scalar.copy(h_ret[:, t0:, h, :],
                                       bank[7][:, t0 * DH:NT * DH].rearrange("p (t d) -> p t d", d=DH)) \
                            .then_inc(*S.num_read.inc())
                    norm.square(act)
                    for i in range(KD, len(jobs)):
                        if i == KD + 2:
                            norm.root(act)
                        if rounds and i in (16, 20):
                            rounds[i // 4 - 4].copy_rows(act)
                        gate(i)
                    if rounds:
                        rounds[2].copy_rows(act)

                @block.vector
                def _(dve):
                    def gated(i):
                        n, c, d = jobs[i]
                        m = merged[:, 4 * c + d, lo:]
                        dve.wait_ge(*S.act.reach(i + 1))
                        if d < 3:
                            dve.wait_ge(*S.branch_done.reach(i - i // 4 + 1))
                        else:
                            dve.wait_ge(S.weights_used.sem, first["merge", l, i // 4] + 2)
                        if n == 0:
                            nc.vector.tensor_tensor(m, sig_at(i), bank[2 + i % 2][:, lo:], ALU.mult) \
                                .then_inc(*S.dve.inc())
                        else:
                            link(dve, S.dve_step, nc.vector.tensor_tensor(tmp[:, i % 2, lo:], sig_at(i),
                                                                          bank[2 + i % 2][:, lo:], ALU.mult))
                            nc.vector.tensor_tensor(m, m, tmp[:, i % 2, lo:], ALU.add).then_inc(*S.dve.inc())

                    for h in range(H):
                        dve.wait_ge(*table_loaded[h % 2].reach(16 * (h // 2 + 1)))
                        for s in range(NT):
                            dve.wait_ge(*S.scores_ready.reach(NT * h + (s + 1 if s < 2 else NT)))
                            if h:
                                dve.wait_ge(*S.pv_done.reach(NT * (h - 1) + s + 1))
                            off = P if s % 2 == 0 else 0
                            if s < 2:
                                part = slice(1 if last else 0, 2)
                                o = ret_ring[:, s, lo:].rearrange("p (a t) -> p a t", t=CT)
                                x = bank[4 + s][:, lo:].rearrange("p (a t) -> p a t", t=CT)
                                tab = decay[:, h % 2, part, off:off + CT]
                            else:
                                o, x = ret_ring[:, s, CT:], bank[6][:, (s - 2) * CT:(s - 1) * CT]
                                tab = decay[:, h % 2, 0, off:off + CT]
                            nc.vector.tensor_tensor(o, x, tab, ALU.mult).then_inc(*S.p_ready.inc())
                        if h:
                            gated(h - 1)
                    gated(H - 1)
                    dve.wait_ge(*S.num_read.reach(H))
                    norm.centre(dve)
                    for i in range(KD, len(jobs)):
                        if i in (9, 11, 13):
                            (norm.variance, norm.scale_and_gate, norm.store)[i // 2 - 4](dve)
                        if rounds and i == 16:
                            vectors.store(dve, bank[6])
                        if rounds and i in (17, 21):
                            rounds[i // 4 - 4].add(dve)
                        gated(i)
                    for d in range(KD):
                        if rounds and d == 2:
                            rounds[2].add(dve)
                        if d % 4 < 3:
                            dve.wait_ge(*S.pT_done.reach(d - d // 4 + 1))
                        else:
                            dve.wait_ge(S.weights_used.sem, m0 + d // 4 + 1)
                        for s in range(lo // CT, 2):
                            sl = slice(s * CT, (s + 1) * CT)
                            ins = nc.vector.scalar_tensor_tensor(xT[:, d, sl], bank[4 + d % 4][:, sl],
                                                                 mod[:, l, 2 * KD + d, s:s + 1], xT[:, d, sl],
                                                                 ALU.mult, ALU.add)
                        ins.then_inc(*S.x_added.inc())

        SCATTER = (0, 4, 1, 5, 2, 6, 3, 7)
        OUT_BANKS = (0, 6, 7)
        h_tok = region(0, NT, D)
        select = region(4096, NT, E + 1, CAP)
        weight = region(6272, NT, E + 1)
        xs_all = region(10240, KD, E, 64)
        placed = region(0, 2, NT, P)
        selT = region(1024, 2, T)
        gate_s, hid = work[0:64, 2048:3072], work[0:64, 3072:4096]
        hidT = region(6400, 2, KD, 64)
        ys = region(7424, 2, 512)
        xs = region(8448, 2, KD, 64)

        def route(l, last):
            tiles = [2, 3] if last else [0, 1, 2, 3]
            t0, s0 = tiles[0], tiles[0] // 2
            nt = len(tiles)
            R = 32 * (1 - s0) + E
            rest, mask, pos = (work[0:R, x:x + CT] for x in (6400, 6656, 6912))
            one = ones[0:R, 0:1].broadcast_to([R, CT])
            posT = region(8960, NT, E)
            best = work[0:R, 9024:9032]
            router = region(9104, KD, 32)
            top, tot, ex = region(9360, NT), region(9364, NT), region(9368, NT, E)
            logitsT = work[0:32 * nt, 9432:9432 + P]
            gathers = [(d, s) for d in range(KD) for s in range(s0, 2)]
            norm = Normalise(l, 1, t0 * P, 0, bank[1])

            def gathered_out(i):
                d, s = gathers[i]
                return (bank[2 + i % 4][:, :].rearrange("p (e c) -> p e c", c=CAP),
                        xs_all[:, d, :, CAP * (s - s0):CAP * (s - s0) + CAP])
            with stage() as block:
                @block.gpsimd
                def _(pool):
                    pool.dma_start(router[:, :, 0:E], a["router_w"][l].rearrange("(k p) e -> p k e", p=P)) \
                        .then_inc(*S.small_loaded.inc(16))
                    nc.gpsimd.memset(router[:, :, E:], 0.0).then_inc(*S.pool.inc())
                    nc.gpsimd.memset(rest, 0.0).then_inc(*S.pool.inc())
                    nc.gpsimd.memset(select[:, :, :, :], 0.0).then_inc(*S.pool.inc())
                    nc.gpsimd.memset(weight[:, :, :], 0.0).then_inc(*S.pool.inc())

                @block.tensor
                def _(pe):
                    norm.total(pe)
                    pe.wait_ge(*S.small_loaded.reach(16))
                    pe.wait_ge(*S.pool.reach(1))
                    for k in range(KD):
                        pe.wait_ge(*S.h_ready.reach(k + 1))
                        for i, t in enumerate(tiles):
                            ins = nc.tensor.matmul(bank[0][32 * i:32 * i + 32, 0:P], router[:, k, :],
                                                   hT[:, k, t * P:(t + 1) * P], start=(k == 0), stop=(k == KD - 1))
                    ins.then_inc(*S.pe.inc())
                    for i, t in enumerate(tiles):
                        for c in range(2):
                            b = 2 + (2 * i + c) % 4
                            if 2 * i + c >= 4:
                                pe.wait_ge(*S.act.reach(2 * i + c - 3))
                            for j in range(4):
                                ins = nc.tensor.transpose(bank[b][:, j * P:(j + 1) * P],
                                                          hT[:, 4 * c + j, t * P:(t + 1) * P], ident)
                            ins.then_inc(*S.pv_done.inc())
                            if i == 0 and c == 0:
                                pe.wait_ge(*S.norm_act.reach(1))
                                nc.tensor.transpose(bank[1][:, 0:32 * nt], logitsT, ident[0:32 * nt, 0:32 * nt]) \
                                    .then_inc(*S.pe.inc())
                    pe.wait_ge(*S.dve.reach(2))
                    for t in tiles:
                        r = 32 * (t // 2 - s0)
                        ins = nc.tensor.matmul(bank[6][r:r + E, (t % 2) * P:(t % 2 + 1) * P], weight[:, t, 0:E],
                                               ident, start=True, stop=True)
                    ins.then_inc(*S.pe.inc())
                    pe.wait_ge(*S.dve.reach(3))
                    for j in range(2):
                        ins = nc.tensor.transpose(bank[7][:, 64 * j:64 * j + R], pos[:, j * P:(j + 1) * P],
                                                  ident[0:R, 0:R])
                    ins.then_inc(*S.pe.inc())
                    for i, (d, s) in enumerate(gathers):
                        if i < 2:
                            pe.wait_ge(*S.dve.reach(4))
                            pe.wait_ge(*S.act.reach(2 * nt))
                        if i >= 4:
                            pe.wait_ge(*(S.xs_ready if i % 2 else S.x_added).reach(i // 2 - 1))
                        for t in (0, 1):
                            ins = nc.tensor.matmul(bank[2 + i % 4][:, :], h_tok[:, 2 * s + t, d * P:(d + 1) * P],
                                                   select[:, 2 * s + t, 0:E, :].rearrange("p e c -> p (e c)"),
                                                   start=(t == 0), stop=(t == 1))
                        ins.then_inc(*S.gathered.inc())

                @block.scalar
                def _(act):
                    norm.squares(act)
                    norm.root(act)
                    norm.shift(act)
                    act.wait_ge(*S.pe.reach(1))
                    nc.scalar.copy(logitsT, bank[0][0:32 * nt, 0:P]).then_inc(*S.norm_act.inc())
                    for i in range(2 * nt):
                        if i == 2 * nt - 1:
                            act.wait_ge(*S.dve.reach(1))
                            nc.scalar.activation(ex[:, t0:, :], ex[:, t0:, :], ACT.Exp).then_inc(*S.exp_ready.inc())
                        t, c = tiles[i // 2], i % 2
                        act.wait_ge(*S.pv_done.reach(i + 1))
                        nc.scalar.copy(h_tok[:, t, c * 512:(c + 1) * 512], bank[2 + i % 4][:, :]).then_inc(*S.act.inc())
                    for i in range(1, len(gathers), 2):
                        src, dst = gathered_out(i)
                        act.wait_ge(*S.gathered.reach(i + 1))
                        nc.scalar.copy(dst, src).then_inc(*S.xs_ready.inc())

                @block.vector
                def _(dve):
                    norm.inverse(dve)
                    norm.scale(dve)
                    dve.wait_ge(*S.pe.reach(2))
                    lg = bank[1][:, 0:32 * nt].rearrange("p (t e) -> p t e", e=32)[:, :, 0:E]
                    link(dve, S.dve_step, nc.vector.reduce_max(top[:, t0:], lg, axis=AX.X))
                    nc.vector.tensor_tensor(ex[:, t0:, :], lg, top[:, t0:].unsqueeze(2).broadcast_to([P, nt, E]),
                                            ALU.subtract).then_inc(*S.dve.inc())
                    dve.wait_ge(*S.exp_ready.reach(1))
                    link(dve, S.dve_step, nc.vector.reduce_sum(tot[:, t0:], ex[:, t0:, :], axis=AX.X))
                    link(dve, S.dve_step, nc.vector.reciprocal(tot[:, t0:], tot[:, t0:]))
                    dve.wait_ge(*S.pool.reach(4))
                    nc.vector.tensor_tensor(weight[:, t0:, 0:E], ex[:, t0:, :],
                                            tot[:, t0:].unsqueeze(2).broadcast_to([P, nt, E]),
                                            ALU.mult).then_inc(*S.dve.inc())
                    dve.wait_ge(*S.pe.reach(3))
                    for s in range(s0, 2):
                        r = 32 * (s - s0)
                        ins = nc.vector.tensor_copy(rest[r:r + E, :], bank[6][r:r + E, 0:CT])
                    link(dve, S.dve_step, ins)
                    for _ in range(CAP // 8):
                        link(dve, S.dve_step, nc.vector.max(best, rest))
                        link(dve, S.dve_step, nc.vector.match_replace(rest, best, rest, -1.0))
                    link(dve, S.dve_step, nc.vector.tensor_scalar(mask, rest, 0.0, None, ALU.is_lt))
                    link(dve, S.dve_step, nc.vector.tensor_tensor_scan(pos, one, mask, 0.0, ALU.mult, ALU.add))
                    nc.vector.tensor_tensor(pos, pos, mask, ALU.mult).then_inc(*S.dve.inc())
                    dve.wait_ge(*S.pe.reach(4))
                    for s in range(s0, 2):
                        ins = nc.vector.tensor_copy(posT[:, 2 * s:2 * s + 2, :],
                                                    bank[7][:, 0:128].rearrange("p (t r) -> p t r", t=2)
                                                    [:, :, 32 * (s - s0):32 * (s - s0) + E])
                    link(dve, S.dve_step, ins)
                    for t in tiles:
                        ins = nc.vector.tensor_tensor(select[:, t, 0:E, :],
                                                      posT[:, t, :].unsqueeze(2).broadcast_to([P, E, CAP]),
                                                      slot_no[:, :].unsqueeze(1).broadcast_to([P, E, CAP]),
                                                      ALU.is_equal)
                    ins.then_inc(*S.dve.inc())
                    for i in range(0, len(gathers), 2):
                        src, dst = gathered_out(i)
                        dve.wait_ge(*S.gathered.reach(i + 1))
                        nc.vector.tensor_copy(dst, src).then_inc(*S.x_added.inc())

        def experts(l, last):
            tiles = [2, 3] if last else [0, 1, 2, 3]
            t0, s0 = tiles[0], tiles[0] // 2
            ns, nt, lo = 2 - s0, len(tiles), t0 * P
            M = CAP * ns
            n0 = first["moe", l]

            def weights_at(j, k4, cols):
                return slot_view(n0 + j, k4, cols)

            with stage() as block:
                @block.sync
                def _(sp):
                    assert issued[0] == n0 + 6
                    with sp.Fori(0, E - 1) as e:
                        for j in range(6):
                            sp.wait_ge(S.weights_used.sem, n0 + 6 * e + j + 1)
                            src = a[("exp_w1", "exp_w3", "exp_w1", "exp_w3", "exp_w2", "exp_w2")[j]][l]
                            k4 = (0, 0, 1, 1, 0, 1)[j]
                            sp.dma_start(weights_at(j, 4, 1024),
                                         src[bass.ds(e + 1, 1), k4 * 512:(k4 + 1) * 512, :]
                                         .rearrange("e (k p) n -> p (e k) n", p=P)) \
                                .then_inc(slot_loaded[slot_of[n0 + j]], 16)
                    issued[0] += 6 * (E - 1)
                    run_ahead(sp, ("g", l + 1))

                @block.gpsimd
                def _(pool):
                    def stage_in(e, b):
                        for half in range(2):
                            for s in range(s0, 2):
                                at = 64 * half + CAP * (s - s0)
                                ins = nc.gpsimd.tensor_tensor(
                                    placed[:, b, 2 * s:2 * s + 2, at:at + CAP],
                                    select[:, 2 * s:2 * s + 2, bass.ds(e, 1), :].rearrange("p t e c -> p t (e c)"),
                                    weight[:, 2 * s:2 * s + 2, bass.ds(e, 1)].broadcast_to([P, 2, CAP]), ALU.mult)
                        return ins

                    def tokens_in(e, b):
                        nc.gpsimd.tensor_copy(xs[:, b, :, 0:M],
                                              xs_all[:, :, bass.ds(e, 1), 0:M].rearrange("p k e c -> p k (e c)"))

                    nc.gpsimd.memset(placed[:, :, :, :], 0.0).then_inc(*S.pool.inc())
                    pool.wait_ge(*S.pool.latest())
                    for e in range(2):
                        tokens_in(e, e)
                        stage_in(e, e).then_inc(S.sel_ready.sem, 1)
                    with pool.Fori(0, E // 2 - 1) as i:
                        for j in range(2):
                            pool.wait_ge(S.selT_done.sem, S.selT_done.base + 2 * i + j + 2)
                            tokens_in(2 * i + 2 + j, j)
                            stage_in(2 * i + 2 + j, j).then_inc(S.sel_ready.sem, 1)
                    pool.wait_ge(*S.selT_done.reach(E))
                    stage_in(E, 0).then_inc(S.sel_ready.sem, 1)

                @block.tensor
                def _(pe):
                    def turn_selection(b):
                        for t in tiles:
                            ins = nc.tensor.transpose(bank[1][:, t * P:(t + 1) * P], placed[:, b, t, :], ident)
                        ins.then_inc(S.selT_done.sem, 1)

                    def scatter(e, b):
                        pe.wait_ge(S.ys_ready.sem, S.ys_ready.base + e + 2)
                        for i, d in enumerate(SCATTER):
                            half = 64 * (d // 4)
                            pe.wait_ge(S.x_added.sem, S.x_added.base + 8 * e + 9 + max(i - 2, 0))
                            nc.tensor.matmul(bank[OUT_BANKS[i % 3]][:, lo:], ys[half:half + M, b, (d % 4) * P:(d % 4 + 1) * P],
                                             selT[half:half + M, b, lo:], start=True, stop=True) \
                                .then_inc(S.scattered.sem, 1)

                    pe.wait_ge(*S.sel_ready.reach(1))
                    turn_selection(0)
                    with pe.Fori(0, E // 2) as i:
                        for b in range(2):
                            e = 2 * i + b
                            pe.wait_ge(S.sel_ready.sem, S.sel_ready.base + e + 1)
                            pe.wait_ge(S.hid_ready.sem, S.hid_ready.base + 2 * e + 2)
                            for kh in range(2):
                                for j in (2 * kh, 2 * kh + 1):
                                    pe.wait_ge(slot_loaded[slot_of[n0 + j]], loaded_count(n0 + j)[1] + 16 * e)
                                w1, w3 = weights_at(2 * kh, 4, 1024), weights_at(2 * kh + 1, 4, 1024)
                                for c in range(2):
                                    for k in range(4):
                                        st, en = kh == 0 and k == 0, kh == 1 and k == 3
                                        x = xs[:, b, 4 * kh + k, 0:M]
                                        nc.tensor.matmul(bank[2 + c][0:M, :], x, w1[:, k, c * 512:(c + 1) * 512],
                                                         start=st, stop=en)
                                        ins = nc.tensor.matmul(bank[2 + c][64:64 + M, :], x,
                                                               w3[:, k, c * 512:(c + 1) * 512], start=st, stop=en)
                                    if kh == 1 and c == 0:
                                        ins.then_inc(S.w13_done.sem, 1)
                                ins.then_inc(S.weights_used.sem, 2)
                            scatter(e - 1, 1 - b)
                            pe.wait_ge(S.sel_ready.sem, S.sel_ready.base + e + 2)
                            pe.wait_ge(S.hid_ready.sem, S.hid_ready.base + 2 * e + 4)
                            pe.wait_ge(S.hidT_ready.sem, S.hidT_ready.base + e + 1)
                            turn_selection(1 - b)
                            for k in range(KD):
                                ins = nc.tensor.transpose(bank[4][:, k * 64:k * 64 + M], hid[0:M, k * P:(k + 1) * P],
                                                          ident[0:M, 0:M])
                            ins.then_inc(S.hidT_done.sem, 1)
                            pe.wait_ge(S.hidT_ready.sem, S.hidT_ready.base + e + 2)
                            for kh in range(2):
                                j = 4 + kh
                                pe.wait_ge(slot_loaded[slot_of[n0 + j]], loaded_count(n0 + j)[1] + 16 * e)
                                w2 = weights_at(j, 4, 1024)
                                for k in range(4):
                                    for c in range(2):
                                        ins = nc.tensor.matmul(bank[5][64 * c:64 * c + M, :], hidT[:, b, 4 * kh + k, 0:M],
                                                               w2[:, k, c * 512:(c + 1) * 512],
                                                               start=(kh == 0 and k == 0), stop=(kh == 1 and k == 3))
                                ins.then_inc(S.weights_used.sem, 1)
                    scatter(E - 1, 1)

                @block.scalar
                def _(act):
                    with act.Fori(0, E // 2) as i:
                        for b in range(2):
                            e = 2 * i + b
                            for c in range(2):
                                if c == 0:
                                    act.wait_ge(S.w13_done.sem, S.w13_done.base + e + 1)
                                else:
                                    act.wait_ge(S.weights_used.sem, n0 + 6 * e + 4)
                                nc.scalar.activation(gate_s[0:M, c * 512:(c + 1) * 512], bank[2 + c][0:M, :], ACT.Silu) \
                                    .then_inc(S.silu_done.sem, 1)
                            act.wait_ge(S.hidT_done.sem, S.hidT_done.base + e + 2)
                            nc.scalar.copy(hidT[:, b, :, 0:M], bank[4][:, :].rearrange("p (k c) -> p k c", c=64)[:, :, 0:M]) \
                                .then_inc(S.hidT_ready.sem, 1)
                            act.wait_ge(S.weights_used.sem, n0 + 6 * e + 6)
                            for half in (0, 64):
                                ins = nc.scalar.copy(ys[half:half + M, b, :], bank[5][half:half + M, :])
                            ins.then_inc(S.ys_ready.sem, 1)

                @block.vector
                def _(dve):
                    def add_to_x(e):
                        for i, d in enumerate(SCATTER):
                            dve.wait_ge(S.scattered.sem, S.scattered.base + 8 * e + 9 + i)
                            for s in range(s0, 2):
                                sl = slice(s * CT, (s + 1) * CT)
                                ins = nc.vector.scalar_tensor_tensor(xT[:, d, sl], bank[OUT_BANKS[i % 3]][:, sl],
                                                                     mod[:, l, 5 * KD + d, s:s + 1], xT[:, d, sl],
                                                                     ALU.mult, ALU.add)
                            ins.then_inc(S.x_added.sem, 1)

                    def selT_copy(e, b):
                        dve.wait_ge(S.selT_done.sem, S.selT_done.base + e + 1)
                        nc.vector.tensor_copy(selT[:, b, lo:], bank[1][:, lo:])

                    nc.vector.memset(ys[:, 1, :], 0.0)
                    nc.vector.memset(selT[:, 1, :], 0.0).then_inc(S.ys_ready.sem, 1)
                    nc.vector.engine_nop().then_inc(S.x_added.sem, 1)
                    nc.vector.engine_nop().then_inc(S.hid_ready.sem, 2)
                    nc.vector.engine_nop().then_inc(S.hidT_ready.sem, 1)
                    nc.vector.engine_nop().then_inc(S.hidT_done.sem, 1)
                    selT_copy(0, 0)
                    with dve.Fori(0, E // 2) as i:
                        for b in range(2):
                            e = 2 * i + b
                            dve.wait_ge(S.hidT_done.sem, S.hidT_done.base + e + 1)
                            for c in range(2):
                                cols = slice(c * 512, (c + 1) * 512)
                                dve.wait_ge(S.silu_done.sem, S.silu_done.base + 2 * e + c + 1)
                                nc.vector.tensor_tensor(hid[0:M, cols], bank[2 + c][64:64 + M, :], gate_s[0:M, cols],
                                                        ALU.mult).then_inc(S.hid_ready.sem, 1)
                            add_to_x(e - 1)
                            selT_copy(e + 1, 1 - b)
                    add_to_x(E - 1)
            S.sel_ready.total += E + 1
            S.selT_done.total += E + 1
            S.hid_ready.total += 2 * E + 2
            S.w13_done.total += E
            S.silu_done.total += 2 * E
            S.weights_used.total += 6 * E
            S.hidT_done.total += E + 1
            S.hidT_ready.total += E + 1
            S.ys_ready.total += E + 1
            S.scattered.total += 8 * (E + 1)
            S.x_added.total += 8 * (E + 1) + 1

        def store_latents():
            rows = region(0, 2, D)
            with stage() as block:
                @block.tensor
                def _(pe):
                    for i in range(4):
                        for j in range(4):
                            ins = nc.tensor.transpose(bank[i][:, j * P:(j + 1) * P],
                                                      xT[:, 4 * (i % 2) + j, CT + (i // 2) * P:CT + (i // 2 + 1) * P], ident)
                        ins.then_inc(*S.pe.inc())

                @block.vector
                def _(dve):
                    for i in range(4):
                        dve.wait_ge(*S.pe.reach(i + 1))
                        nc.vector.tensor_copy(rows[:, i // 2, (i % 2) * 512:(i % 2 + 1) * 512], bank[i][:, :]) \
                            .then_inc(*S.dve.inc())

                @block.sync
                def _(sp):
                    dst = out.rearrange("b (t p) d -> p (b t) d", p=P)
                    for t in range(2):
                        sp.wait_ge(*S.dve.reach(2 * t + 2))
                        sp.dma_start(dst[:, t, :], rows[:, t, :]).then_inc(*S.stored.inc(16))
                    sp.wait_ge(*S.stored.reach(32))

        for l in range(DEPTH):
            last = l == DEPTH - 1
            project_a(l, last)
            mlstm(l, last)
            project_b(l, last)
            mla_heads(l, last)
            attention_and_project_c(l, last)
            retention_and_merge(l, last)
            route(l, last)
            experts(l, last)
        store_latents()


_INS = ["x", "c", "ctx", "c_ctx", "ada_w", "ada_b", "norm1_w", "norm2_w", "w_in", "b_in", "conv_w", "conv_b",
        "ml_norm_w", "mla_qa_norm", "mla_wq_b", "mla_kva_norm", "mla_wkv_b", "q_norm_w", "k_norm_w", "ret_norm_w",
        "w_branch", "w_out", "router_w", "exp_w1", "exp_w3", "exp_w2"]


def shape_constants(np):
    i = np.arange(P)
    f32 = np.float32
    before = (i[:, None] <= i[None, :]).astype(f32)
    after = (i[:, None] >= i[None, :]).astype(f32)
    eye = np.eye(P, dtype=f32)
    big = f32(-1e30)
    half = ROPE // 4
    inv = (f32(10000.0) ** (-np.arange(half, dtype=f32) / f32(half))).astype(f32)
    tok = np.arange(LT)
    angle = [(v.astype(f32)[:, None] * inv).astype(f32) for v in (tok // 64, tok % 64)]
    cos, sin = [np.cos(v).astype(f32) for v in angle], [np.sin(v).astype(f32) for v in angle]
    rope = np.stack([np.concatenate([cos[0], cos[0], cos[1], cos[1]], 1),
                     np.concatenate([-sin[0], sin[0], -sin[1], sin[1]], 1)], 1)
    rope = rope.reshape(2, P, 2, ROPE).transpose(1, 0, 2, 3)
    g = np.log1p(-np.exp2(-5.0 - np.arange(H)))
    dt = (np.arange(3 * P)[None, :] - P - i[:, None]).astype(np.float64)
    decay = np.zeros((H, P, 2, 3 * P))
    for h in range(H):
        gf, gb = g[h], g[H - 1 - h]
        decay[h, :, 0] = np.where(dt >= 0, np.exp(np.maximum(dt, 0) * gf), 0) + \
            np.where(dt <= 0, np.exp(np.maximum(-dt, 0) * gb), 0)
        decay[h, :, 1] = np.exp((CT + dt) * gf) + np.exp((CT - dt) * gb)
    return {
        "consts": np.concatenate([eye, np.ones((P, P), f32)], 1),
        "masks": np.concatenate([eye, big * (1 - before), big * (1 - after)], 1),
        "rope": rope.astype(f32),
        "slot_no": np.tile(np.arange(1, CAP + 1, dtype=f32), (P, 1)),
        "decay": (decay * RK ** -0.5).astype(f32),
    }


def kernel(**inputs):
    import numpy as np
    import concourse.bacc as bacc
    from concourse.bass_utils import run_bass_kernel_spmd

    nc = bacc.Bacc("TRN2", target_bir_lowering=False, num_devices=1)
    arrays = {name: np.ascontiguousarray(inputs[name]) for name in _INS}
    arrays.update({k: np.ascontiguousarray(v) for k, v in shape_constants(np).items()})
    aps = {name: nc.dram_tensor(f"in_{name}", v.shape, mybir.dt.from_np(v.dtype), kind="ExternalInput").ap()
           for name, v in arrays.items()}
    out = nc.dram_tensor("out_latents", (1, LT, D), F32, kind="ExternalOutput").ap()
    build_program(nc, aps, out)
    r = run_bass_kernel_spmd(nc, [{f"in_{name}": v for name, v in arrays.items()}], core_ids=[0])
    return r.results[0]["out_latents"]
```
